# Optimizing a Trainium2 kernel written in Bass

```python
import jax, jax.numpy as jnp
from jax import lax
import numpy as np

D_MODEL = 1024
BATCH = 1
SEQ = 1024
DEPTH = 1

CHUNK = 64
PLE_DIM = 256
HEAD_DIM = 64
SWA_HEADS = 8
SWA_KV_HEADS = 2
SWA_GROUP = SWA_HEADS // SWA_KV_HEADS
WINDOW = 128
SWA_BLOCK = WINDOW
FOX_HEADS = 8
FOX_BLOCK = 128
D_FF = 4 * D_MODEL
N_BRANCH = 2
RMS_EPS = 1e-6

SWA_Q = SWA_HEADS * HEAD_DIM
SWA_KV = SWA_KV_HEADS * HEAD_DIM
FOX_W = FOX_HEADS * HEAD_DIM
GATE_W = N_BRANCH * D_MODEL
SPLIT_POINTS = tuple(np.cumsum([SWA_Q, SWA_KV, SWA_KV, FOX_W, FOX_W, FOX_W, FOX_HEADS]).tolist())
D_IN = SPLIT_POINTS[-1] + GATE_W


def alibi_slopes(n_heads):
    return jnp.asarray(np.array([2.0 ** (-8.0 * (h + 1) / n_heads) for h in range(n_heads)], dtype=np.float32))

def rms_norm(x, g):
    x32 = x.astype(jnp.float32)
    y = x32 * lax.rsqrt(jnp.mean(jnp.square(x32), axis=-1, keepdims=True) + RMS_EPS)
    return (y * g.astype(jnp.float32)).astype(x.dtype)

def sliding_window_attention(q, k, v, sinks):
    B, S = q.shape[0], q.shape[1]
    nb = S // SWA_BLOCK
    SB = SWA_BLOCK
    qb = q.reshape(B, nb, SB, SWA_KV_HEADS, SWA_GROUP, HEAD_DIM)
    kb = k.reshape(B, nb, SB, SWA_KV_HEADS, HEAD_DIM)
    vb = v.reshape(B, nb, SB, SWA_KV_HEADS, HEAD_DIM)

    def band(t):
        prev = jnp.pad(t[:, :-1], ((0, 0), (1, 0), (0, 0), (0, 0), (0, 0)))
        return jnp.concatenate([prev, t], axis=2)

    k_band, v_band = band(kb), band(vb)
    s = jnp.einsum('bnqkgd,bnskd->bnkgqs', qb, k_band).astype(jnp.float32) * (HEAD_DIM ** -0.5)

    qi = jnp.arange(SB)[:, None] + SB
    si = jnp.arange(2 * SB)[None, :]
    chunk_diff = qi // CHUNK - si // CHUNK
    band_ok = (chunk_diff >= 0) & (chunk_diff <= WINDOW // CHUNK)
    real_key = (jnp.arange(nb)[:, None, None] > 0) | (si >= SB)[None]
    mask = band_ok[None] & real_key

    slopes = alibi_slopes(SWA_HEADS).reshape(SWA_KV_HEADS, SWA_GROUP)
    alibi = -slopes[:, :, None, None] * jnp.abs(qi - si).astype(jnp.float32)
    s = jnp.where(mask[None, :, None, None], s + alibi[None, None], -jnp.inf)

    sink = jnp.broadcast_to(sinks.astype(jnp.float32).reshape(SWA_KV_HEADS, SWA_GROUP)[None, None, :, :, None, None],
                            s.shape[:-1] + (1,))
    probs = jax.nn.softmax(jnp.concatenate([s, sink], axis=-1), axis=-1)[..., :-1]
    out = jnp.einsum('bnkgqs,bnskd->bnqkgd', probs.astype(v.dtype), v_band)
    return out.reshape(B, S, SWA_Q)

def forgetting_attention(q, k, v, f_logit):
    B, S = q.shape[0], q.shape[1]
    nb = S // FOX_BLOCK
    log_f = jax.nn.log_sigmoid(f_logit.astype(jnp.float32))
    c = jnp.cumsum(log_f, axis=1)
    c_k = c.transpose(0, 2, 1)
    kh = k.transpose(0, 2, 1, 3)
    vh = v.transpose(0, 2, 1, 3)
    q_blocks = q.reshape(B, nb, FOX_BLOCK, FOX_HEADS, HEAD_DIM).transpose(1, 0, 3, 2, 4)
    c_blocks = c.reshape(B, nb, FOX_BLOCK, FOX_HEADS).transpose(1, 0, 3, 2)
    k_pos = jnp.arange(S)
    scale = HEAD_DIM ** -0.5

    def one_block(args):
        qb, cq, n = args
        s = jnp.einsum('bhqd,bhsd->bhqs', qb, kh).astype(jnp.float32) * scale
        s = s + cq[..., None] - c_k[:, :, None, :]
        q_pos = n * FOX_BLOCK + jnp.arange(FOX_BLOCK)
        s = jnp.where((k_pos[None, :] <= q_pos[:, None])[None, None], s, -jnp.inf)
        probs = jax.nn.softmax(s, axis=-1)
        return jnp.einsum('bhqs,bhsd->bhqd', probs.astype(vh.dtype), vh)

    out = lax.map(one_block, (q_blocks, c_blocks, jnp.arange(nb, dtype=jnp.int32)))
    return out.transpose(1, 0, 3, 2, 4).reshape(B, S, FOX_W)

def first_inputs(seed: int = 0) -> dict:
    key = jax.random.key(seed)
    ks = jax.random.split(key, 18)

    def dense(k, fan_in, fan_out):
        return jax.random.normal(k, (DEPTH, fan_in, fan_out), jnp.float32) * fan_in ** -0.5

    def gain(k, shape):
        return 1.0 + 0.02 * jax.random.normal(k, shape, jnp.float32)

    return {
        "x": jax.random.normal(ks[0], (BATCH, SEQ, D_MODEL), jnp.float32),
        "p": jax.random.normal(ks[1], (DEPTH, BATCH, SEQ, PLE_DIM), jnp.float32),
        "g_mix": gain(ks[2], (DEPTH, D_MODEL)),
        "w_in": dense(ks[3], D_MODEL, D_IN),
        "b_forget": 3.0 + 0.5 * jax.random.normal(ks[4], (DEPTH, FOX_HEADS), jnp.float32),
        "swa_sinks": 0.5 * jax.random.normal(ks[5], (DEPTH, SWA_HEADS), jnp.float32),
        "w_br_swa": dense(ks[6], SWA_Q, D_MODEL),
        "w_br_fox": dense(ks[7], FOX_W, D_MODEL),
        "w_mix_out": dense(ks[8], D_MODEL, D_MODEL),
        "g_mlp": gain(ks[9], (DEPTH, D_MODEL)),
        "w_ff1": dense(ks[10], D_MODEL, D_FF),
        "w_ff2": dense(ks[11], D_FF, D_MODEL),
        "g_ple": gain(ks[12], (DEPTH, D_MODEL)),
        "w_ple_gate": dense(ks[13], D_MODEL, D_MODEL),
        "w_ple_proj": dense(ks[14], PLE_DIM, D_MODEL),
        "g_final": gain(ks[15], (D_MODEL,)),
    }

def first_block(x, p, g_mix, w_in, b_forget, swa_sinks, w_br_swa, w_br_fox, w_mix_out,
              g_mlp, w_ff1, w_ff2, g_ple, w_ple_gate, w_ple_proj, g_final):
    B, S = x.shape[0], x.shape[1]
    h = x
    for i in range(DEPTH):
        u = rms_norm(h, g_mix[i])
        z = u @ w_in[i]
        q_a, k_a, v_a, q_b, k_b, v_b, f_b, gate_logits = jnp.split(z, SPLIT_POINTS, axis=-1)
        y_a = sliding_window_attention(
            q_a.reshape(B, S, SWA_HEADS, HEAD_DIM),
            k_a.reshape(B, S, SWA_KV_HEADS, HEAD_DIM),
            v_a.reshape(B, S, SWA_KV_HEADS, HEAD_DIM),
            swa_sinks[i]) @ w_br_swa[i]
        y_b = forgetting_attention(
            q_b.reshape(B, S, FOX_HEADS, HEAD_DIM),
            k_b.reshape(B, S, FOX_HEADS, HEAD_DIM),
            v_b.reshape(B, S, FOX_HEADS, HEAD_DIM),
            f_b + b_forget[i]) @ w_br_fox[i]
        gates = jax.nn.sigmoid(gate_logits).reshape(B, S, N_BRANCH, D_MODEL)
        mixed = gates[:, :, 0] * y_a + gates[:, :, 1] * y_b
        h = h + mixed @ w_mix_out[i]
        u = rms_norm(h, g_mlp[i])
        h = h + jnp.square(jax.nn.relu(u @ w_ff1[i])) @ w_ff2[i]
        ple_gate = jax.nn.sigmoid(rms_norm(h, g_ple[i]) @ w_ple_gate[i])
        h = h + ple_gate * (p[i] @ w_ple_proj[i])
    return rms_norm(h, g_final)


N_MIXERS = 2
N_POOL_LAYERS = (DEPTH + N_MIXERS - 1) // N_MIXERS
N_GLA_LAYERS = DEPTH // N_MIXERS

POOL_WIDTH = D_MODEL
POOL_WINDOWS = (2, 4, 8, 16)
POOL_GROUPS = len(POOL_WINDOWS)
POOL_GROUP_DIM = POOL_WIDTH // POOL_GROUPS

GLA_HEADS = 4
GLA_KEY_WIDTH = D_MODEL // 2
GLA_VALUE_WIDTH = D_MODEL
GLA_HEAD_K = GLA_KEY_WIDTH // GLA_HEADS
GLA_HEAD_V = GLA_VALUE_WIDTH // GLA_HEADS
GLA_GATE_RANK = 16
GLA_GATE_NORMALIZER = 16.0
GLA_IN_WIDTH = 2 * GLA_KEY_WIDTH + 2 * GLA_VALUE_WIDTH + GLA_GATE_RANK


def rms_norm_2(x, w):
    xf = x.astype(jnp.float32)
    y = xf * lax.rsqrt(jnp.mean(xf * xf, axis=-1, keepdims=True) + RMS_EPS)
    return (y * w.astype(jnp.float32)).astype(x.dtype)

def trailing_mean(u, window):
    seq = u.shape[1]
    cs = jnp.cumsum(u.astype(jnp.float32), axis=1)
    lagged = jnp.pad(cs, ((0, 0), (window, 0), (0, 0)))[:, :seq]
    count = jnp.minimum(jnp.arange(1, seq + 1), window).astype(jnp.float32)
    return ((cs - lagged) / count[None, :, None]).astype(u.dtype)

def pool_mixer(h, in_w, group_w, group_b, scale, out_w):
    b, s, _ = h.shape
    u, gate = jnp.split(h @ in_w, 2, axis=-1)
    ug = u.reshape(b, s, POOL_GROUPS, POOL_GROUP_DIM)
    pooled = jnp.stack([trailing_mean(ug[:, :, g], w) for g, w in enumerate(POOL_WINDOWS)],
                       axis=2) - ug
    mixed = jnp.einsum('bsgc,gcd->bsgd', pooled, group_w) + group_b
    y = mixed.reshape(b, s, POOL_WIDTH) * scale * jax.nn.silu(gate)
    return y @ out_w

def gla_mixer(h, in_w, gk_w, gk_b, head_norm_w, out_w):
    b, s, _ = h.shape
    n_chunks = s // CHUNK
    f32 = jnp.float32
    proj = h @ in_w
    q, k, v, gate, gk_low = jnp.split(
        proj, [GLA_KEY_WIDTH, 2 * GLA_KEY_WIDTH, 2 * GLA_KEY_WIDTH + GLA_VALUE_WIDTH,
               2 * GLA_KEY_WIDTH + 2 * GLA_VALUE_WIDTH], axis=-1)
    log_g = jax.nn.log_sigmoid((gk_low @ gk_w + gk_b).astype(f32)) / GLA_GATE_NORMALIZER

    def to_chunks(t, d):
        return t.astype(f32).reshape(b, n_chunks, CHUNK, GLA_HEADS, d)

    qc = to_chunks(q, GLA_HEAD_K) * (GLA_HEAD_K ** -0.5)
    kc = to_chunks(k, GLA_HEAD_K)
    vc = to_chunks(v, GLA_HEAD_V)
    cum = jnp.cumsum(to_chunks(log_g, GLA_HEAD_K), axis=2)
    cum_last = cum[:, :, -1:]
    e_pos, e_neg = jnp.exp(cum), jnp.exp(-cum)

    fwd = jnp.einsum('bnthk,bnshk->bnhts', qc * e_pos, kc * e_neg)
    bwd = jnp.einsum('bnthk,bnshk->bnhts', qc * e_neg, kc * e_pos)
    idx = jnp.arange(CHUNK)
    lower = idx[:, None] >= idx[None, :]
    scores = jnp.where(lower, fwd, bwd)
    o_intra = jnp.einsum('bnhts,bnshv->bnthv', scores, vc)

    q_dec = qc * e_pos
    k_dec = kc * jnp.exp(cum_last - cum)
    chunk_decay = jnp.exp(cum_last[:, :, 0])

    def step(state, inp):
        q_n, k_n, v_n, d_n = inp
        o_n = jnp.einsum('bthk,bhkv->bthv', q_n, state)
        state = state * d_n[..., None] + jnp.einsum('bthk,bthv->bhkv', k_n, v_n)
        return state, o_n

    xs = (jnp.moveaxis(q_dec, 1, 0), jnp.moveaxis(k_dec, 1, 0),
          jnp.moveaxis(vc, 1, 0), jnp.moveaxis(chunk_decay, 1, 0))
    state0 = jnp.zeros((b, GLA_HEADS, GLA_HEAD_K, GLA_HEAD_V), f32)
    _, o_inter = lax.scan(step, state0, xs)
    o = (o_intra + jnp.moveaxis(o_inter, 0, 1)).reshape(b, s, GLA_HEADS, GLA_HEAD_V)

    o = o * lax.rsqrt(jnp.mean(o * o, axis=-1, keepdims=True) + RMS_EPS) * head_norm_w.astype(f32)
    y = o.reshape(b, s, GLA_VALUE_WIDTH).astype(h.dtype) * jax.nn.silu(gate)
    return y @ out_w

def second_inputs(seed: int = 0) -> dict:
    key = jax.random.key(seed)
    ks = jax.random.split(key, 16)
    nrm = jax.random.normal
    f32 = jnp.float32
    NP, NG = N_POOL_LAYERS, N_GLA_LAYERS
    return {
        "x": nrm(ks[0], (BATCH, SEQ, D_MODEL), f32),
        "norm_w": 1.0 + 0.02 * nrm(ks[1], (DEPTH, D_MODEL), f32),
        "pool_in_w": nrm(ks[2], (NP, D_MODEL, 2 * POOL_WIDTH), f32) * D_MODEL ** -0.5,
        "pool_group_w": nrm(ks[3], (NP, POOL_GROUPS, POOL_GROUP_DIM, POOL_GROUP_DIM), f32) * POOL_GROUP_DIM ** -0.5,
        "pool_group_b": 0.02 * nrm(ks[4], (NP, POOL_GROUPS, POOL_GROUP_DIM), f32),
        "pool_scale": 1.0 + 0.1 * nrm(ks[5], (NP, POOL_WIDTH), f32),
        "pool_out_w": nrm(ks[6], (NP, POOL_WIDTH, D_MODEL), f32) * POOL_WIDTH ** -0.5,
        "gla_in_w": nrm(ks[7], (NG, D_MODEL, GLA_IN_WIDTH), f32) * D_MODEL ** -0.5,
        "gla_gk_w": nrm(ks[8], (NG, GLA_GATE_RANK, GLA_KEY_WIDTH), f32) * GLA_GATE_RANK ** -0.5,
        "gla_gk_b": 0.02 * nrm(ks[9], (NG, GLA_KEY_WIDTH), f32),
        "gla_head_norm_w": 1.0 + 0.02 * nrm(ks[10], (NG, GLA_HEAD_V), f32),
        "gla_out_w": nrm(ks[11], (NG, GLA_VALUE_WIDTH, D_MODEL), f32) * GLA_VALUE_WIDTH ** -0.5,
        "final_norm_w": 1.0 + 0.02 * nrm(ks[12], (D_MODEL,), f32),
    }

def second_block(x, norm_w, pool_in_w, pool_group_w, pool_group_b, pool_scale, pool_out_w,
              gla_in_w, gla_gk_w, gla_gk_b, gla_head_norm_w, gla_out_w, final_norm_w):
    h = x
    for i in range(DEPTH):
        normed = rms_norm_2(h, norm_w[i])
        j = i // N_MIXERS
        if i % N_MIXERS == 0:
            h = h + pool_mixer(normed, pool_in_w[j], pool_group_w[j], pool_group_b[j],
                               pool_scale[j], pool_out_w[j])
        else:
            h = h + gla_mixer(normed, gla_in_w[j], gla_gk_w[j], gla_gk_b[j],
                              gla_head_norm_w[j], gla_out_w[j])
    return rms_norm_2(h, final_norm_w)


def setup_inputs(seed=0):
    out = dict(first_inputs(seed))
    for name, value in second_inputs(seed + 1).items():
        if name != "x":
            out[name + "_2"] = value
    return out


def reference(
    x, p, g_mix, w_in, b_forget, swa_sinks, w_br_swa, w_br_fox, w_mix_out, g_mlp, w_ff1, w_ff2,
    g_ple, w_ple_gate, w_ple_proj, g_final, norm_w_2, pool_in_w_2, pool_group_w_2,
    pool_group_b_2, pool_scale_2, pool_out_w_2, gla_in_w_2, gla_gk_w_2, gla_gk_b_2,
    gla_head_norm_w_2, gla_out_w_2, final_norm_w_2,
):
    x = first_block(
        x, p, g_mix, w_in, b_forget, swa_sinks, w_br_swa, w_br_fox, w_mix_out, g_mlp, w_ff1,
        w_ff2, g_ple, w_ple_gate, w_ple_proj, g_final,
    )
    return second_block(
        x, norm_w_2, pool_in_w_2, pool_group_w_2, pool_group_b_2, pool_scale_2, pool_out_w_2,
        gla_in_w_2, gla_gk_w_2, gla_gk_b_2, gla_head_norm_w_2, gla_out_w_2, final_norm_w_2,
    )


_drawn_inputs = setup_inputs


def setup_inputs(seed=0):
    import zlib

    import numpy as np

    out = dict(_drawn_inputs(seed))
    spreads = {}
    factors = {'g_mix': 7.282,
     'swa_sinks': 8.0,
     'g_mlp': 3.03,
     'g_ple': 8.0,
     'norm_w_2': 4.33,
     'pool_group_b_2': 5.348,
     'final_norm_w_2': 2.831}
    for name, (base, spread) in spreads.items():
        noise = np.random.default_rng([zlib.crc32(name.encode()), seed]).standard_normal(out[name].shape)
        drawn = base * np.exp(spread * noise) if base else spread * noise
        out[name] = __import__('jax').numpy.asarray(drawn.astype(out[name].dtype))
    for name, factor in factors.items():
        out[name] = (out[name] * factor).astype(out[name].dtype)
    return out
```

```python
from contextlib import ExitStack

import numpy as np

import concourse.bass as bass
from concourse import mybir

F32 = mybir.dt.float32
F32R = mybir.dt.float32r
ALU = mybir.AluOpType
ACT = mybir.ActivationFunctionType
AX_X = mybir.AxisListType.X

P = 128
D = 1024
NT = 8
EPS = 1e-6
FAR = 3e38


class Queue:

    def __init__(self, sem):
        self.sem, self.count, self.ops, self.met = sem, 0, [], {}

    def wait(self, *marks):
        for m in marks:
            if m is None:
                continue
            if isinstance(m, list):
                self.wait(*m)
            elif self.met.get(id(m[0]), 0) < m[1]:
                self.met[id(m[0])] = m[1]
                self.ops.append((None, m[0], m[1]))

    def do(self, fn, *marks, signal=True):
        self.wait(*marks)
        if not signal:
            self.ops.append((fn, None, 0))
            return None
        self.count += 1
        self.ops.append((fn, self.sem, 1))
        return (self.sem, self.count)

    def run(self, eng):
        for fn, sem, n in self.ops:
            if fn is None:
                eng.wait_ge(sem, n)
            elif sem is None:
                fn(eng)
            else:
                fn(eng).then_inc(sem, n)


class DmaSem:
    def __init__(self, sem):
        self.sem, self.count = sem, 0


def build(nc, A, out):
    ctx = ExitStack()
    with ctx:
        def new_sem(name):
            return ctx.enter_context(nc.semaphore(name))

        SIZE = 212832
        arena = ctx.enter_context(nc.sbuf_tensor("arena", [P, SIZE // 4], F32))
        ARENA0 = (16481 + 31) // 32 * 32

        def at(name, off, shape, dt=F32):
            n = int(np.prod(shape[1:])) * 4
            assert off + n <= SIZE, (name, off, n)
            return nc.alloc_sbuf_tensor_at(name, list(shape), dt, offset=ARENA0 + off)

        K = 1024
        RAW = at("RAW", 0, [P, 4, 1024])
        RH = at("RH", 16 * K, [P, 4, 1024], F32R)
        RL = at("RL", 32 * K, [P, 4, 1024], F32R)
        o = 48 * K
        CST = at("CST", o, [P, 4, 128])
        o += 2048
        INV = at("INV", o, [P, 4, 16])
        o += 256
        SM = at("SM", o, [P, 256])
        o += 1024
        GB = at("GB", o, [P, D])
        o += 4096
        OH = o
        H = at("H", OH, [P, NT, D])
        OU = OH + 32 * K
        UH = at("UH", OU, [P, NT, D], F32R)
        UL = at("UL", OU + 32 * K, [P, NT, D], F32R)
        OX = OU + 64 * K
        ident, causal, tri, ones = (CST[:, i, :] for i in range(4))

        PS = ctx.enter_context(nc.psum_tensor("PS", [P, 8, 512], F32))

        pe, act, dve, pool, sp = (Queue(new_sem(f"done_{n}")) for n in ("pe", "act", "dve", "pool", "sp"))

        def dma(dst, src, ds, *marks):
            sp.wait(*marks)
            ds.count += 16
            sp.ops.append((lambda e: e.dma_start(dst, src), ds.sem, 16))
            return (ds.sem, ds.count)

        def dsem(name):
            return DmaSem(new_sem(name))

        small_at = [0]

        def small(n):
            a = small_at[0]
            small_at[0] += n
            assert small_at[0] <= 256
            return SM[:, a:a + n]

        x_v = A["x"].rearrange("b (t p) d -> p (b t) d", p=P)
        p_v = A["p"].rearrange("l b (t p) d -> p (l b t) d", p=P)
        out_v = out.rearrange("b (t p) d -> p (b t) d", p=P)

        def mat(name):
            v = A[name]
            while len(v.shape) > 2:
                v = v.rearrange("a b c -> (a b) c") if len(v.shape) == 3 else v.rearrange("a b c d -> (a b) c d")
            return v

        w_in, w_sa, w_fx, w_mix = mat("w_in"), mat("w_br_swa"), mat("w_br_fox"), mat("w_mix_out")
        w_f1, w_f2, w_pg, w_pp = mat("w_ff1"), mat("w_ff2"), mat("w_ple_gate"), mat("w_ple_proj")
        w_pi, w_gr, w_po = mat("pool_in_w_2"), mat("pool_group_w_2"), mat("pool_out_w_2")

        def row(name):
            v = A[name]
            if len(v.shape) == 2:
                v = v.rearrange("a b -> (a b)")
            return v.partition_broadcast(P)

        gates_d = nc.dram_tensor("gates_scratch", [16, P, D], F32, kind="Internal").ap()
        h2_d = nc.dram_tensor("h2_scratch", [P, NT, D], F32, kind="Internal").ap()

        loads = []

        def load(parts, n):
            loads.append((parts, n))
            return len(loads) - 1

        def load_k2(w, r0, c0):
            src = w[r0:r0 + 256, c0:c0 + 512].rearrange("(k p) c -> p k c", p=P)
            return load([(lambda s: s.rearrange("p (k c) -> p k c", k=2), src)], 1024)

        def load_k4(w, r0, nk, c0):
            src = w[r0:r0 + nk * P, c0:c0 + 256].rearrange("(k p) c -> p k c", p=P)
            return load([(lambda s: s[:, 0:nk * 256].rearrange("p (k c) -> p k c", k=nk), src)], nk * 256)

        class Slab:

            def __init__(self, idx, per, width):
                self.idx, self.per, self.width = idx, per, width

            def load_of(self, k):
                return self.idx[k // self.per]

            def at(self, k, c0, c1):
                s = self.load_of(k) % 4
                a = (k % self.per) * self.width
                return RH[:, s, a + c0:a + c1], RL[:, s, a + c0:a + c1]

        def slab512(w, r0, c0, nk=8):
            return Slab([load_k2(w, r0 + 256 * j, c0) for j in range(nk // 2)], 2, 512)

        def slab256(w, r0, c0, nk=8):
            step = min(nk, 4)
            return Slab([load_k4(w, r0 + P * step * j, step, c0) for j in range(nk // step)], step, 256)

        def slab_misc():
            idx = []
            for k0 in (0, 3, 6):
                nk = min(3, 8 - k0)
                rows = slice(k0 * P, (k0 + nk) * P)
                idx.append(load([
                    (lambda s, nk=nk: s[:, 0:nk * 264].rearrange("p (k c) -> p k c", k=nk)[:, :, 0:256],
                     w_in[rows, 512:768].rearrange("(k p) c -> p k c", p=P)),
                    (lambda s, nk=nk: s[:, 0:nk * 264].rearrange("p (k c) -> p k c", k=nk)[:, :, 256:264],
                     w_in[rows, 2304:2312].rearrange("(k p) c -> p k c", p=P))], nk * 264))
            return Slab(idx, 3, 264)

        S_qa = slab512(w_in, 0, 0)
        S_ms = slab_misc()
        S_qb = slab512(w_in, 0, 768)
        S_kb = slab512(w_in, 0, 1280)
        S_vb = slab512(w_in, 0, 1792)
        S_gt = [slab512(w_in, 0, 2312 + 512 * j) for j in range(4)]
        S_y = [(slab512(w_sa, 0, 512 * j, 4), slab512(w_fx, 0, 512 * j, 4)) for j in range(2)]
        S_mx = [slab512(w_mix, 0, 512 * j) for j in range(2)]
        S_ff = []
        for c in range(8):
            S_ff.append((slab512(w_f1, 0, 512 * c), slab512(w_f2, 512 * c, 0, 4), slab512(w_f2, 512 * c, 512, 4)))
        S_pp = [slab512(w_pp, 0, 512 * j, 2) for j in range(2)]
        S_pg = [slab512(w_pg, 0, 512 * j) for j in range(2)]
        S_pi = []
        for g in range(4):
            S_pi.append((slab256(w_pi, 0, 256 * g), slab256(w_pi, 0, D + 256 * g), slab256(w_gr, 256 * g, 0, 2)))
        S_po = [slab512(w_po, 0, 512 * j) for j in range(2)]

        raw_ds = [dsem(f"raw{i}") for i in range(4)]
        landed, split_done = {}, {}

        def fetch(i):
            if i >= len(loads):
                return
            for view, src in loads[i][0]:
                landed[i] = dma(view(RAW[:, i % 4, :]), src, raw_ds[i % 4], split_done.get(i - 4))

        def split(i, released=None):
            if i >= len(loads):
                return
            n, s = loads[i][1], i % 4
            m = act.do(lambda e: e.activation(RH[:, s, 0:n], RAW[:, s, 0:n], ACT.Copy), landed[i], released)
            split_done[i] = dve.do(lambda e: e.tensor_tensor(RL[:, s, 0:n], RAW[:, s, 0:n], RH[:, s, 0:n].bitcast(F32),
                                                             ALU.subtract), m, released)
            fetch(i + 4)

        freed = [None] * 8
        turn = [0]

        def banks(n):
            got = [(turn[0] + j) % 8 for j in range(n)]
            turn[0] = (turn[0] + n) % 8
            return got

        def products(groups, ks, order="kout", release=()):
            last_use = {}
            steps = [(k, g) for k in ks for g in range(len(groups))] if order == "kout" else \
                [(k, g) for g in range(len(groups)) for k in ks]
            for n, (k, g) in enumerate(steps):
                last_use[k] = n
            ends = [None] * len(groups)
            of_load = {}
            for slab in release:
                for k in ks:
                    ld = slab.load_of(k)
                    of_load[ld] = max(of_load.get(ld, 0), last_use[k])
            for n, (k, g) in enumerate(steps):
                o_ap, b, operands = groups[g]
                (sh, sl), (mh, ml), marks = operands(k)
                first, last = k == ks[0], k == ks[-1]
                if first:
                    pe.wait(freed[b])
                pe.wait(marks)
                pe.do(lambda e, o_ap=o_ap, sh=sh, mh=mh, first=first: e.matmul(o_ap, sh, mh, start=first, stop=False),
                      signal=False)
                pe.do(lambda e, o_ap=o_ap, sh=sh, ml=ml: e.matmul(o_ap, sh, ml, start=False, stop=False), signal=False)
                out_of = [ld for ld, m in of_load.items() if m == n]
                mark = pe.do(lambda e, o_ap=o_ap, sl=sl, mh=mh, last=last:
                             e.matmul(o_ap, sl, mh, start=False, stop=last), signal=last or bool(out_of))
                if last:
                    ends[g] = mark
                for ld in sorted(out_of):
                    split(ld + 4, mark)
            return ends

        def bank(b, n=512):
            return PS[:, b, 0:n]

        u_ready = [None] * NT

        def by_columns(slab, j, half, b, hi=None, lo=None, ready=None, kin=None):
            hi, lo, ready = hi or UH, lo or UL, ready or u_ready
            t0, t1 = 512 * half, 512 * half + 512

            def operands(k):
                r = ready(k, half) if callable(ready) else ready[4 * half:4 * half + 4]
                return slab.at(k, 128 * j, 128 * j + 128), (hi[:, k, t0:t1], lo[:, k, t0:t1]), \
                    [split_done[slab.load_of(k)], r]
            return (bank(b), b, operands)

        def by_tokens(slab, t, b, c0=0, c1=512, hi=None, lo=None, ready=None, o_ap=None):
            hi, lo = hi or UH, lo or UL

            def operands(k):
                r = ready(k, t) if callable(ready) else (ready or u_ready)[t]
                return (hi[:, k, P * t:P * t + P], lo[:, k, P * t:P * t + P]), slab.at(k, c0, c1), \
                    [split_done[slab.load_of(k)], r]
            return (bank(b, c1 - c0) if o_ap is None else o_ap, b, operands)

        ssq, rms, rst = small(NT), small(NT), small(NT)
        XS = [at(f"XS{i}", OX + 48 * K + 4096 * i, [P, D]) for i in range(2)]
        xs_read = [None, None]

        def rstd(t, src, scratch, *marks):
            a = act.do(lambda e: e.activation(scratch, src, ACT.Square, accum_out=ssq[:, t:t + 1]), *marks)
            b = dve.do(lambda e: e.tensor_scalar(rms[:, t:t + 1], ssq[:, t:t + 1], 1.0 / D, EPS, ALU.mult, ALU.add), a)
            c = act.do(lambda e: e.activation(rms[:, t:t + 1], rms[:, t:t + 1], ACT.Sqrt), b)
            return a, dve.do(lambda e: e.reciprocal(rst[:, t:t + 1], rms[:, t:t + 1]), c)

        def norm(t, src, gain, gain_ready, *marks):
            i = t % 2
            a, r = rstd(t, src, XS[i][:, :], xs_read[i], *marks)
            return dve.do(lambda e: e.scalar_tensor_tensor(out=XS[i][:, :], in0=src, scalar=rst[:, t:t + 1], in1=gain,
                                                           op0=ALU.mult, op1=ALU.mult), r, a, gain_ready)

        def to_u(t, xs_mark, *marks):
            i = t % 2
            for q in range(2):
                b, = banks(1)
                pe.wait(freed[b], xs_mark, c_ready)
                for k in range(4):
                    m = pe.do(lambda e, k=k, q=q, b=b: e.transpose(
                        PS[:, b, P * k:P * k + P], XS[i][:, P * (4 * q + k):P * (4 * q + k) + P], ident),
                              signal=(k == 3))
                xs_read[i] = m
                src = PS[:, b, :].rearrange("p (k c) -> p k c", k=4)
                hi, lo = (v[:, 4 * q:4 * q + 4, P * t:P * t + P] for v in (UH, UL))
                a = act.do(lambda e, src=src, hi=hi: e.activation(hi, src, ACT.Copy), m, *marks)
                freed[b] = u_ready[t] = dve.do(lambda e, src=src, hi=hi, lo=lo: e.tensor_tensor(
                    lo, src, hi.bitcast(F32), ALU.subtract), a, *marks)

        x_ds = [dsem(f"x{t}") for t in range(NT)]
        c_ds = dsem("consts")
        g_ds, sc_ds = dsem("gain"), dsem("small_consts")
        x_in = [dma(H[:, 0, :], x_v[:, 0, :], x_ds[0])]
        gb_ready = dma(GB[:, :], row("g_mix"), g_ds)
        c_ready = dma(CST[:, :, :], A["c_mats"].rearrange("i p c -> p i c"), c_ds)
        for t in range(1, NT):
            x_in.append(dma(H[:, t, :], x_v[:, t, :], x_ds[t]))
            if t % 2:
                fetch(t // 2)
        bf, snk = small(8), small(8)
        pgb, psc = small(8), small(8)
        dma(INV[:, :, :], A["c_inv"], sc_ds)
        dma(bf, row("b_forget"), sc_ds)
        dma(snk, row("swa_sinks"), sc_ds)
        dma(pgb, A["pool_group_b_2"], sc_ds)
        sc_ready = dma(psc, A["pool_scale_2"], sc_ds)

        xs_m = {}
        for t in range(NT):
            xs_m[t] = norm(t, H[:, t, :], GB[:, :], gb_ready, x_in[t])
            to_u(t, xs_m[t])
            if t % 2:
                split(t // 2)
        x_read = xs_m[NT - 1]

        QB = at("QB", OH, [P, 4, D])
        KB = at("KB", OH + 16 * K, [P, 4, D])
        QA = at("QA", OX, [P, 4, D])
        KD = at("KD", OX + 16 * K, [P, 2, D])
        VB = at("VB", OX + 24 * K, [P, NT, 512])
        VA = at("VA", OX + 40 * K, [P, NT, P])
        GST = [at(f"GST{i}", OX + 44 * K + 2048 * i, [P, 512]) for i in range(2)]

        def heads(slab, dst, scale, *marks):
            done = {}
            for j0 in (0, 2):
                bs = banks(4)
                gr = [(j, h) for h in range(2) for j in (j0, j0 + 1)]
                ends = products([by_columns(slab, j, h, bs[n]) for n, (j, h) in enumerate(gr)], range(8), "seq",
                                release=[slab] if j0 else ())
                for n, (j, h) in enumerate(gr):
                    freed[bs[n]] = done[j, h] = act.do(
                        lambda e, b=bs[n], j=j, h=h: e.activation(dst[:, j, 512 * h:512 * h + 512], bank(b), ACT.Copy,
                                                                  scale=scale), ends[n], *marks)
            return done

        qa_done = heads(S_qa, QA, 0.125)

        F = small(64)
        F3 = F.rearrange("p (t h) -> p t h", t=NT)
        bs = banks(2)
        ends = products([by_columns(S_ms, 0, h, bs[h]) for h in range(2)], range(8))
        kd_done = []
        for h in range(2):
            sl = slice(512 * h, 512 * h + 512)
            b = bs[h]
            for g in range(2):
                for r in range(2):
                    m = act.do(lambda e, g=g, r=r, b=b, sl=sl: e.activation(
                        KD[64 * r:64 * r + 64, g, sl], PS[64 * g:64 * g + 64, b, :], ACT.Copy), ends[h])
            freed[b] = m
            kd_done.append(m)
        bs = banks(4)
        va_done, f_done = {}, {}
        vf_end = {}
        for t in range(NT):
            b, c = bs[t // 2], 136 * (t % 2)
            vf_end[t], = products([by_tokens(S_ms, t, b, 128, 264, o_ap=PS[:, b, c:c + 136])], range(8),
                                  release=[S_ms] if t == NT - 1 else ())
            if t % 2:
                for tt in (t - 1, t):
                    c = 136 * (tt % 2)
                    va_done[tt] = dve.do(lambda e, tt=tt, b=b, c=c: e.tensor_copy(VA[:, tt, :], PS[:, b, c:c + P]),
                                         vf_end[t])
                    freed[b] = f_done[tt] = dve.do(lambda e, tt=tt, b=b, c=c: e.tensor_tensor(
                        F3[:, tt, :], PS[:, b, c + P:c + P + 8], bf, ALU.add), vf_end[t], sc_ready)

        qb_done = heads(S_qb, QB, 0.125, x_read)
        kb_done = heads(S_kb, KB, 1.0, x_read)
        vb_done = {}
        for t0 in (0, 4):
            bs = banks(4)
            ends = products([by_tokens(S_vb, t0 + n, bs[n]) for n in range(4)], range(8), "kout",
                            release=[S_vb] if t0 else ())
            for n in range(4):
                freed[bs[n]] = vb_done[t0 + n] = act.do(lambda e, t=t0 + n, b=bs[n]: e.activation(
                    VB[:, t, :], bank(b), ACT.Copy), ends[n])

        gst_ds = [dsem("gst0"), dsem("gst1")]
        gate_stored = {}
        stored = [None, None]
        n_st = 0
        last_gate = None
        for s in range(4):
            for j0 in (0, 2):
                bs = banks(4)
                gr = [(j, h) for j in (j0, j0 + 1) for h in range(2)]
                ends = products([by_columns(S_gt[s], j, h, bs[n]) for n, (j, h) in enumerate(gr)], range(8), "kout",
                                release=[S_gt[s]] if j0 else ())
                last_gate = ends[-1]
                for n, (j, h) in enumerate(gr):
                    i = n_st % 2
                    n_st += 1
                    g = GST[i][:, :]
                    freed[bs[n]] = m = act.do(lambda e, g=g, b=bs[n]: e.activation(g, bank(b), ACT.Exp, scale=-1.0),
                                              ends[n], stored[i])
                    m = dve.do(lambda e, g=g: e.tensor_scalar(g, g, 1.0, None, ALU.add), m)
                    m = dve.do(lambda e, g=g: e.reciprocal(g, g), m)
                    gate_stored[4 * s + j, h] = stored[i] = dma(gates_d[4 * s + j, :, 512 * h:512 * h + 512], g,
                                                                gst_ds[i], m)

        OA = at("OA", OU, [P, NT, 512])
        OB = at("OB", OU + 16 * K, [P, NT, 512])
        T = [at(f"T{i}", OU + 32 * K + 4096 * i, [P, D]) for i in range(2)]
        E = [at(f"E{i}", OU + 40 * K + 4096 * i, [P, D]) for i in range(2)]
        BIAS = at("BIAS", OU + 48 * K, [P, 8, 256])
        NC = [at(f"NC{i}", OU + 48 * K + 8192 * i, [P, 2, D]) for i in range(2)]
        PT = [at(f"PT{i}", OX + 48 * K + 2048 * i, [P, 4, P]) for i in range(4)]
        pt_read = [None] * 4
        n_pt = [0]
        free_u = last_gate
        bias_ready = dma(BIAS[:, :, :], A["c_bias"], dsem("bias"), free_u)

        def turn_probs(src_blocks, src_mark, b_of):
            got = []
            for q0 in range(0, len(src_blocks), 4):
                blk = src_blocks[q0:q0 + 4]
                b = b_of(q0 // 4)
                pe.wait(freed[b], src_mark)
                for n, s in enumerate(blk):
                    m = pe.do(lambda e, n=n, s=s, b=b: e.transpose(PS[:, b, P * n:P * n + P], s, ident),
                              signal=(n == len(blk) - 1))
                i = n_pt[0] % 4
                n_pt[0] += 1
                w = P * len(blk)
                q = act if (q0 // 4 + n_pt[0]) % 2 else dve
                dst = PT[i][:, 0:len(blk), :].rearrange("p k c -> p (k c)")
                if q is act:
                    freed[b] = q.do(lambda e, dst=dst, b=b, w=w: e.activation(dst, PS[:, b, 0:w], ACT.Copy), m, pt_read[i], xs_read)
                else:
                    freed[b] = q.do(lambda e, dst=dst, b=b, w=w: e.tensor_copy(dst, PS[:, b, 0:w]), m, pt_read[i], xs_read)
                got.append((i, freed[b]))
            return got

        FT = at("FT", OU + 56 * K, [P, 6, 64])
        fa, fe, fw, fl, fm, LF = (FT[:, i, :] for i in range(6))
        C = small(64)
        fd = [f_done[t] for t in range(NT)]
        m1 = dve.do(lambda e: e.tensor_scalar(fm, F, 0.0, None, ALU.min), fd, free_u)
        m2 = dve.do(lambda e: e.tensor_scalar(fa, F, -1.0, None, ALU.mult), fd)
        m2 = dve.do(lambda e: e.tensor_tensor(fa, F, fa, ALU.min), m2)
        m3 = act.do(lambda e: e.activation(fe, fa, ACT.Exp), m2)
        m4 = dve.do(lambda e: e.tensor_scalar(fw, fe, 1.0, None, ALU.add), m3)
        m5 = act.do(lambda e: e.activation(fl, fw, ACT.Ln), m4)
        m6 = dve.do(lambda e: e.tensor_scalar(fa, fw, -1.0, None, ALU.add), m4, m3)
        m6 = dve.do(lambda e: e.tensor_tensor(fa, fe, fa, ALU.subtract), m6)
        m7 = dve.do(lambda e: e.reciprocal(fw, fw), m5, m6)
        m7 = dve.do(lambda e: e.tensor_tensor(fa, fa, fw, ALU.mult), m7)
        m7 = dve.do(lambda e: e.tensor_tensor(fl, fl, fa, ALU.add), m7)
        lf_done = dve.do(lambda e: e.tensor_tensor(LF, fm, fl, ALU.subtract), m7, m1)
        LF3 = LF.rearrange("p (t h) -> p t h", t=NT)
        b, = banks(1)
        pe.wait(freed[b], lf_done, c_ready)
        for t in range(NT):
            for j in range(t + 1):
                m = pe.do(lambda e, t=t, j=j, b=b: e.matmul(PS[:, b, 8 * t:8 * t + 8], tri if j == t else ones,
                                                            LF3[:, j, :], start=(j == 0), stop=(j == t)),
                          signal=(t == NT - 1 and j == t))
        freed[b] = c_done = dve.do(lambda e, b=b: e.tensor_copy(C, PS[:, b, 0:64]), m)

        mx, nm, es, den, rd = (small(8) for _ in range(5))
        units = [(g, n) for n in range(NT) for g in range(2)]
        stage = {}
        t_read, e_read, rd_read, rs_read = [None] * 2, [None] * 2, [None] * 2, [None] * 2

        def swa_scores(i):
            g, n = units[i]
            w = 256 if n else P
            s0 = P * (n - 1) if n else 0
            sb = 2 * (i % 2)
            pe.wait(freed[sb], freed[sb + 1], kd_done, [qa_done[j, n // 4] for j in range(4)])
            for a in range(4):
                h = 4 * g + a
                r = slice(64 * (h % 2), 64 * (h % 2) + 64)
                m = pe.do(lambda e, a=a, h=h, r=r: e.matmul(PS[:, sb + a % 2, 256 * (a // 2):256 * (a // 2) + w],
                                                            QA[r, h // 2, P * n:P * n + P], KD[r, g, s0:s0 + w],
                                                            start=True, stop=True), signal=(a == 3))
            s = PS[:, sb:sb + 2, :].rearrange("p b (a c) -> p a b c", a=2)[:, :, :, 0:w]
            tv = T[i % 2][:, :].rearrange("p (a c) -> p a c", a=4)[:, :, 0:w]
            tv4 = T[i % 2][:, :].rearrange("p (a b c) -> p a b c", a=2, b=2)[:, :, :, 0:w]
            bv = BIAS[:, 4 * g:4 * g + 4, 256 - w:256].rearrange("p (a b) c -> p a b c", a=2)
            t1 = dve.do(lambda e: e.tensor_tensor(tv4, s, bv, ALU.add), m, bias_ready, t_read[i % 2], free_u)
            freed[sb] = freed[sb + 1] = t1
            q = slice(4 * (i % 2), 4 * (i % 2) + 4)
            t2 = dve.do(lambda e: e.tensor_reduce(mx[:, q], tv, AX_X, ALU.max), t1)
            t2 = dve.do(lambda e: e.tensor_tensor(mx[:, q], mx[:, q], snk[:, 4 * g:4 * g + 4], ALU.max), t2, sc_ready)
            t3 = dve.do(lambda e: e.tensor_scalar(nm[:, q], mx[:, q], -1.0, None, ALU.mult), t2, rs_read[i % 2])
            ev = E[i % 2][:, :].rearrange("p (a c) -> p a c", a=4)[:, :, 0:w]
            ms = []
            for a in range(4):
                c = 4 * (i % 2) + a
                ms.append(act.do(lambda e, a=a, c=c: e.activation(ev[:, a, :], tv[:, a, :], ACT.Exp, bias=nm[:, c:c + 1],
                                                                  accum_out=den[:, c:c + 1]), t3, e_read[i % 2], rd_read[i % 2]))
            t_read[i % 2] = ms[-1]
            t4 = dve.do(lambda e: e.tensor_tensor(es[:, q], snk[:, 4 * g:4 * g + 4], mx[:, q], ALU.subtract), t2, rd_read[i % 2])
            t5 = act.do(lambda e: e.activation(es[:, q], es[:, q], ACT.Exp), t4)
            t6 = dve.do(lambda e: e.tensor_tensor(den[:, q], den[:, q], es[:, q], ALU.add), t5, ms[-1])
            t7 = dve.do(lambda e: e.reciprocal(rd[:, q], den[:, q]), t6)
            rs_read[i % 2] = t5
            stage[i] = (ms[-1], t7)

        def swa_turn(i):
            g, n = units[i]
            nk = 2 if n else 1
            ev = E[i % 2][:, :].rearrange("p (a k c) -> p a k c", a=4, k=2)
            blocks = [ev[:, a, k, :] for a in range(4) for k in range(nk)]
            got = turn_probs(blocks, stage[i][0], lambda q: 4 + q)
            e_read[i % 2] = (pe.sem, pe.count)
            stage[i] += (got,)

        def swa_values(i):
            g, n = units[i]
            nk = 2 if n else 1
            _, rden, got = stage[i]
            b = 6 + i % 2
            pe.wait(freed[b], [m for _, m in got], [va_done[t] for t in range(max(n - 1, 0), n + 1)])
            for a in range(4):
                for k in range(nk):
                    blk = a * nk + k
                    pi = got[blk // 4][0]
                    tile = n - nk + 1 + k
                    m = pe.do(lambda e, a=a, k=k, pi=pi, blk=blk, tile=tile: e.matmul(
                        PS[:, b, 64 * a:64 * a + 64], PT[pi][:, blk % 4, :], VA[:, tile, 64 * g:64 * g + 64],
                        start=(k == 0), stop=(k == nk - 1)), signal=(k == nk - 1))
            for pi, _ in got:
                pt_read[pi] = m
            q = slice(4 * (i % 2), 4 * (i % 2) + 4)
            freed[b] = dve.do(lambda e: e.tensor_tensor(
                OA[:, n, 256 * g:256 * g + 256].rearrange("p (a c) -> p a c", a=4),
                PS[:, b, 0:256].rearrange("p (a c) -> p a c", a=4),
                rd[:, q].unsqueeze(2).to_broadcast([P, 4, 64]), ALU.mult), m, rden, free_u)
            rd_read[i % 2] = freed[b]
            oa_done[i] = freed[b]

        oa_done = {}
        LAGT, LAGV = 1, 2
        for i in range(len(units) + LAGV):
            if i >= LAGV:
                swa_values(i - LAGV)
            if LAGT <= i < len(units) + LAGT:
                swa_turn(i - LAGT)
            if i < len(units):
                swa_scores(i)

        nc_done, nc_read = {}, [None, None]
        C3 = C.rearrange("p (t h) -> p t h", t=NT)

        def fox_keys(h):
            i = h % 2
            bb = (6, 7)
            for q in range(2):
                b = bb[q]
                pe.wait(freed[b], c_done, c_ready)
                for k in range(4):
                    col = C3[:, 4 * q + k, h:h + 1]
                    m = pe.do(lambda e, k=k, b=b, col=col: e.matmul(PS[:, b, P * k:P * k + P],
                                                                    col.to_broadcast([P, P]), ident, start=True,
                                                                    stop=True), signal=(k == 3))
                freed[b] = a = act.do(lambda e, q=q, b=b: e.activation(NC[i][:, 0, 512 * q:512 * q + 512], bank(b), ACT.Copy,
                                                                       scale=-1.0), m, nc_read[i], oa_done[15], free_u)
            nc_done[h] = [a, pool.do(lambda e: e.tensor_tensor(
                NC[i][:, 1, :].rearrange("p (k c) -> p k c", k=NT), NC[i][:, 0, :].rearrange("p (k c) -> p k c", k=NT),
                causal.unsqueeze(1).to_broadcast([P, NT, P]), ALU.add), a, nc_read[i], c_ready)]

        fmx, fnm, fden, frd = (small(2) for _ in range(4))
        funits = [(h, t) for h in range(8) for t in range(NT)]
        fst = {}
        fnm_read, frd_read = [None] * 2, [None] * 2
        ob_done = {}

        def fox_scores(i):
            h, t = funits[i]
            n = P * (t + 1)
            r = slice(64 * (h % 2), 64 * (h % 2) + 64)
            sb = 2 * (i % 2)
            pe.wait(freed[sb], freed[sb + 1], [qb_done[h // 2, x] for x in range(2)], [kb_done[h // 2, x] for x in range(2)])
            for c0 in range(0, n, 512):
                c1 = min(n, c0 + 512)
                m = pe.do(lambda e, c0=c0, c1=c1: e.matmul(PS[:, sb + c0 // 512, 0:c1 - c0], QB[r, h // 2, P * t:P * t + P],
                                                           KB[r, h // 2, c0:c1], start=True, stop=True),
                          signal=(c1 == n))
            s = PS[:, sb:sb + 2, :].rearrange("p b c -> p (b c)")
            tv, ev = T[i % 2], E[i % 2]
            cq = C3[:, t, h:h + 1]
            j = i % 2
            if t:
                m = dve.do(lambda e: e.scalar_tensor_tensor(out=tv[:, 0:n - P], in0=s[:, 0:n - P], scalar=cq,
                                                            in1=NC[h % 2][:, 0, 0:n - P], op0=ALU.add, op1=ALU.add),
                           m, nc_done[h], c_done, t_read[j])
            t1 = dve.do(lambda e: e.scalar_tensor_tensor(out=tv[:, n - P:n], in0=s[:, n - P:n], scalar=cq,
                                                         in1=NC[h % 2][:, 1, n - P:n], op0=ALU.add, op1=ALU.add),
                        m, nc_done[h], c_done, t_read[j])
            freed[sb] = freed[sb + 1] = t1
            nc_read[h % 2] = t1
            t2 = dve.do(lambda e: e.tensor_reduce(fmx[:, j:j + 1], tv[:, 0:n], AX_X, ALU.max), t1, m)
            t3 = dve.do(lambda e: e.tensor_scalar(fnm[:, j:j + 1], fmx[:, j:j + 1], -1.0, None, ALU.mult), t2, fnm_read[j])
            t4 = act.do(lambda e: e.activation(ev[:, 0:n], tv[:, 0:n], ACT.Exp, bias=fnm[:, j:j + 1],
                                               accum_out=fden[:, j:j + 1]), t3, e_read[j], frd_read[j])
            t_read[j] = fnm_read[j] = t4
            fst[i] = (t4,)

        def fox_turn(i):
            h, t = funits[i]
            blocks = [E[i % 2][:, P * k:P * k + P] for k in range(t + 1)]
            got = turn_probs(blocks, fst[i][0], lambda q: 4 + q)
            e_read[i % 2] = (pe.sem, pe.count)
            j = i % 2
            rden = dve.do(lambda e: e.reciprocal(frd[:, j:j + 1], fden[:, j:j + 1]), fst[i][0], frd_read[j])
            fst[i] = (got, rden)

        def fox_values(i):
            h, t = funits[i]
            got, rden = fst[i]
            b = 6 + i % 2
            pe.wait(freed[b], [m for _, m in got], [vb_done[k] for k in range(t + 1)])
            for k in range(t + 1):
                pi = got[k // 4][0]
                m = pe.do(lambda e, k=k, pi=pi: e.matmul(PS[:, b, 0:64], PT[pi][:, k % 4, :], VB[:, k, 64 * h:64 * h + 64],
                                                         start=(k == 0), stop=(k == t)), signal=(k == t))
            for pi, _ in got:
                pt_read[pi] = m
            j = i % 2
            freed[b] = frd_read[j] = ob_done[i] = act.do(lambda e: e.activation(
                OB[:, t, 64 * h:64 * h + 64], PS[:, b, 0:64], ACT.Copy, scale=frd[:, j:j + 1]), m, rden, free_u)

        for i in range(len(funits) + LAGV):
            if i >= LAGV:
                fox_values(i - LAGV)
            if LAGT <= i < len(funits) + LAGT:
                fox_turn(i - LAGT)
            if i < len(funits):
                if funits[i][1] == 0:
                    fox_keys(funits[i][0])
                fox_scores(i)
        attn_end = ob_done[63]

        OAH, OAL = (at(f"OA{n}", OH + 16 * K * i, [P, 4, D], F32R) for i, n in enumerate("HL"))
        OBH, OBL = (at(f"OB{n}", OX + 16 * K * i, [P, 4, D], F32R) for i, n in enumerate("HL"))
        turn[0] = 0
        pe_mark = (pe.sem, pe.count)
        ot_ready = {}
        ot_end = None
        for src, hi, lo, done, br in ((OA, OAH, OAL, [oa_done[14], oa_done[15]], 0), (OB, OBH, OBL, [attn_end], 1)):
            for j in range(4):
                for hf in range(2):
                    b, = banks(1)
                    pe.wait(freed[b], done)
                    for n in range(4):
                        ot_end = m = pe.do(lambda e, n=n, b=b, src=src, j=j, hf=hf: e.transpose(
                            PS[:, b, P * n:P * n + P], src[:, 4 * hf + n, P * j:P * j + P], ident), signal=(n == 3))
                    d = slice(512 * hf, 512 * hf + 512)
                    a = act.do(lambda e, b=b, hi=hi, j=j, d=d: e.activation(hi[:, j, d], bank(b), ACT.Copy), m, pe_mark)
                    freed[b] = ot_ready[br, j, hf] = dve.do(lambda e, b=b, hi=hi, lo=lo, j=j, d=d: e.tensor_tensor(
                        lo[:, j, d], bank(b), hi[:, j, d].bitcast(F32), ALU.subtract), a, pe_mark)

        G = [at(f"G{i}", OX + 32 * K + 4096 * i, [P, 2, 512]) for i in range(2)]
        Y = [at(f"Y{i}", OX + 40 * K + 4096 * i, [P, 2, 512]) for i in range(2)]
        g_in_ds = [dsem("g_in0"), dsem("g_in1")]
        g_read, y_read = [pe_mark] * 2, [pe_mark] * 2
        mix_ready = {}

        def fetch_gates(i):
            if i >= 16:
                return None
            j, hf = i // 2, i % 2
            dma(G[i % 2][:, 0, :], gates_d[j, :, 512 * hf:512 * hf + 512], g_in_ds[i % 2], gate_stored[j, hf], g_read[i % 2])
            return dma(G[i % 2][:, 1, :], gates_d[8 + j, :, 512 * hf:512 * hf + 512], g_in_ds[i % 2],
                       gate_stored[8 + j, hf], g_read[i % 2])

        g_in = {0: fetch_gates(0), 1: fetch_gates(1)}
        y_end = None
        for j in range(8):
            bs = banks(4)
            sa, sf = S_y[j // 4]
            jj = j % 4
            gr = [(br, hf) for br in range(2) for hf in range(2)]
            ends = []
            for br, slab in ((0, sa), (1, sf)):
                hi, lo = ((OAH, OAL), (OBH, OBL))[br]
                ends += products([by_columns(slab, jj, hf, bs[2 * br + hf], hi, lo,
                                             lambda k, hf, br=br: ot_ready[br, k, hf]) for hf in range(2)], range(4),
                                 "kout", release=[slab] if jj == 3 else ())
            y_end = ends[3]
            for hf in range(2):
                i = 2 * j + hf
                q = i % 2
                ba, bb = bs[hf], bs[2 + hf]
                freed[ba] = m1 = dve.do(lambda e, q=q, ba=ba: e.tensor_tensor(Y[q][:, 0, :], bank(ba), G[q][:, 0, :], ALU.mult),
                                        ends[hf], g_in[i], y_read[q])
                freed[bb] = m2 = dve.do(lambda e, q=q, bb=bb: e.tensor_tensor(Y[q][:, 1, :], bank(bb), G[q][:, 1, :], ALU.mult),
                                        ends[2 + hf], g_in[i])
                g_read[q] = m2
                g_in[i + 2] = fetch_gates(i + 2)
                m3 = pool.do(lambda e, q=q: e.tensor_tensor(Y[q][:, 0, :], Y[q][:, 0, :], Y[q][:, 1, :], ALU.add), m1, m2)
                d = slice(512 * hf, 512 * hf + 512)
                m4 = act.do(lambda e, q=q, j=j, d=d: e.activation(UH[:, j, d], Y[q][:, 0, :], ACT.Copy), m3, ot_end)
                mix_ready[j, hf] = y_read[q] = dve.do(lambda e, q=q, j=j, d=d: e.tensor_tensor(
                    UL[:, j, d], Y[q][:, 0, :], UH[:, j, d].bitcast(F32), ALU.subtract), m4, ot_end)

        h_done = {}
        for t in range(NT):
            h_done[t] = dma(H[:, t, :], x_v[:, t, :], x_ds[t], y_end)
        gb_ready = dma(GB[:, :], row("g_mlp"), g_ds, x_read)

        def add_to_h(t, c, b, mark, *marks):
            d = slice(512 * c, 512 * c + 512)
            freed[b] = dve.do(lambda e: e.tensor_tensor(H[:, t, d], bank(b), H[:, t, d], ALU.add), mark, *marks)
            return freed[b]

        def into_h(slabs, operands_of, order0, then):
            for c in range(2):
                for t0 in (0, 4):
                    bs = banks(4)
                    order = order0 if (c, t0) == (0, 0) else "seq"
                    if order == "kout":
                        ends = products([operands_of(slabs[c], t0 + n, bs[n]) for n in range(4)], range(8), "kout")
                        for n in range(4):
                            h_done[t0 + n] = add_to_h(t0 + n, c, bs[n], ends[n], h_done[t0 + n])
                        continue
                    for n in range(4):
                        t = t0 + n
                        end, = products([operands_of(slabs[c], t, bs[n])], range(8), "seq",
                                        release=[slabs[c]] if t == NT - 1 else ())
                        h_done[t] = add_to_h(t, c, bs[n], end, h_done[t])
                        if c:
                            then(t, end)

        xs_m, u_free = {}, {}

        def norm_mlp(t, end):
            u_free[t] = end
            if t >= 2:
                to_u(t - 2, xs_m[t - 2], u_free[t - 2])
            xs_m[t] = norm(t, H[:, t, :], GB[:, :], gb_ready, h_done[t])

        into_h(S_mx, lambda s, t, b: by_tokens(s, t, b, ready=lambda k, t: mix_ready[k, t // 4]), "kout", norm_mlp)

        def start_columns(slab, j0, late, release, evac):
            bs = banks(2)
            for n in range(2):
                e0, = products([by_columns(slab, j0 + n, 0, bs[n])], range(8), "seq")
                evac(j0 + n, 0, bs[n], e0)
                late(n)
            bs = banks(2)
            ends = products([by_columns(slab, j0 + n, 1, bs[n]) for n in range(2)], range(8), "kout", release=release)
            for n in range(2):
                evac(j0 + n, 1, bs[n], ends[n])

        HH, HL = (at(f"HID{n}", OX + 16 * K * i, [P, 4, D], F32R) for i, n in enumerate("HL"))
        R = [at(f"R{i}", OX + 32 * K + 2048 * i, [P, 512]) for i in range(2)]
        R2 = [at(f"RR{i}", OX + 36 * K + 2048 * i, [P, 512]) for i in range(2)]
        r_read, n_r = [y_end, y_end], [0]
        hid_ready, hid_free = {}, [y_end]
        PST = at("PST", OX + 40 * K, [P, NT, 256])
        p_in = dma(PST[:, :, :], p_v, dsem("p_in"), mix_ready[7, 0], mix_ready[7, 1])

        def squared_relu(j, hf, b, end):
            i = n_r[0] % 2
            n_r[0] += 1
            d = slice(512 * hf, 512 * hf + 512)
            freed[b] = m = dve.do(lambda e: e.tensor_scalar(R[i][:, :], bank(b), 0.0, None, ALU.max), end, r_read[i],
                                  g_read, y_read)
            a = act.do(lambda e: e.activation(HH[:, j, d], R[i][:, :], ACT.Square), m, hid_free)
            s = pool.do(lambda e: e.tensor_tensor(R2[i][:, :], R[i][:, :], R[i][:, :], ALU.mult), m, r_read[i])
            hid_ready[j, hf] = r_read[i] = dve.do(lambda e: e.tensor_tensor(
                HL[:, j, d], R2[i][:, :], HH[:, j, d].bitcast(F32), ALU.subtract), a, s, hid_free)

        last_f1 = None
        gbp_ready = None
        ff2_end = {}

        def norm_ple(t, end):
            u_free[t] = last_f1
            xs_m[t] = norm(t, H[:, t, :], GB[:, :], gbp_ready, h_done[t])

        for c in range(8):
            s1, s2a, s2b = S_ff[c]
            for j0 in (0, 2):
                rel = [s1] if j0 else ()
                if c == 0 and j0 == 0:
                    start_columns(s1, 0, lambda n: to_u(6 + n, xs_m[6 + n], u_free[6 + n]), rel, squared_relu)
                    continue
                bs = banks(4)
                gr = [(j, hf) for j in (j0, j0 + 1) for hf in range(2)]
                ends = products([by_columns(s1, j, hf, bs[n]) for n, (j, hf) in enumerate(gr)], range(8), "kout", release=rel)
                last_f1 = ends[-1]
                for n, (j, hf) in enumerate(gr):
                    squared_relu(j, hf, bs[n], ends[n])
            if c == 0:
                gbp_ready = dma(GB[:, :], row("g_ple"), g_ds, xs_m[7])
            for cc, s2 in ((0, s2a), (1, s2b)):
                for t0 in (0, 4):
                    bs = banks(4)
                    op = lambda t, b: by_tokens(s2, t, b, hi=HH, lo=HL, ready=lambda k, t: hid_ready[k, t // 4])
                    rel = [s2] if t0 else ()
                    if c == 7 and cc == 1:
                        for n in range(4):
                            t = t0 + n
                            end, = products([op(t, bs[n])], range(4), "seq", release=rel if t == NT - 1 else ())
                            h_done[t] = add_to_h(t, cc, bs[n], end, h_done[t])
                            if t >= 2:
                                to_u(t - 2, xs_m[t - 2], u_free[t - 2])
                            norm_ple(t, end)
                    else:
                        ends = products([op(t0 + n, bs[n]) for n in range(4)], range(4), "kout", release=rel)
                        for n in range(4):
                            h_done[t0 + n] = add_to_h(t0 + n, cc, bs[n], ends[n], h_done[t0 + n])
                    end = (pe.sem, pe.count)
            hid_free[0] = end
        ff_end = (pe.sem, pe.count)

        PTH, PTL = (at(f"PLE{n}", OX + 8 * K * i, [P, 2, D], F32R) for i, n in enumerate("HL"))
        PP = at("PP", OX + 16 * K, [P, NT, D])
        pt_done = {}
        for j in range(2):
            for hf in range(2):
                b, = banks(1)
                pe.wait(freed[b], p_in)
                for n in range(4):
                    pt_end = pe.do(lambda e, n=n, b=b, j=j, hf=hf: e.transpose(
                        PS[:, b, P * n:P * n + P], PST[:, 4 * hf + n, P * j:P * j + P], ident), signal=(n == 3))
                d = slice(512 * hf, 512 * hf + 512)
                a = act.do(lambda e, b=b, j=j, d=d: e.activation(PTH[:, j, d], bank(b), ACT.Copy), pt_end, ff_end)
                freed[b] = pt_done[j, hf] = dve.do(lambda e, b=b, j=j, d=d: e.tensor_tensor(
                    PTL[:, j, d], bank(b), PTH[:, j, d].bitcast(F32), ALU.subtract), a, ff_end)
        pp_done = {}
        for c in range(2):
            for t0 in (0, 4):
                bs = banks(4)
                ends = products([by_tokens(S_pp[c], t0 + n, bs[n], hi=PTH, lo=PTL,
                                           ready=lambda k, t: pt_done[k, t // 4]) for n in range(4)], range(2), "kout",
                                release=[S_pp[c]] if t0 else ())
                for n in range(4):
                    freed[bs[n]] = pp_done[t0 + n, c] = act.do(lambda e, t=t0 + n, c=c, b=bs[n]: e.activation(
                        PP[:, t, 512 * c:512 * c + 512], bank(b), ACT.Copy), ends[n], ff_end, pt_end, r_read)
            if c == 0:
                to_u(6, xs_m[6], u_free[6])
                to_u(7, xs_m[7], u_free[7])
        proj_end = (pe.sem, pe.count)
        SG = [at(f"SG{i}", OX + 2048 * i, [P, 512]) for i in range(4)]
        GB2 = at("GB2", OX + 8 * K, [P, D])
        gbf_ready = dma(GB[:, :], row("g_final"), g_ds, xs_m[7])
        gb2_ready = dma(GB2[:, :], row("norm_w_2"), dsem("gain2"), proj_end)
        sg_read, n_sg = [proj_end] * 4, [0]
        h2_ds = [dsem(f"h2_{t}") for t in range(NT)]
        h2_stored, h_read = {}, {}

        def ple(t, c, b, end):
            i = n_sg[0] % 4
            n_sg[0] += 1
            s, d = SG[i][:, :], slice(512 * c, 512 * c + 512)
            freed[b] = m = act.do(lambda e: e.activation(s, bank(b), ACT.Exp, scale=-1.0), end, sg_read[i])
            m = dve.do(lambda e: e.tensor_scalar(s, s, 1.0, None, ALU.add), m)
            m = dve.do(lambda e: e.reciprocal(s, s), m)
            m = pool.do(lambda e: e.tensor_tensor(s, s, PP[:, t, d], ALU.mult), m, pp_done[t, c])
            h_done[t] = sg_read[i] = pool.do(lambda e: e.tensor_tensor(H[:, t, d], H[:, t, d], s, ALU.add), m, h_done[t])

        def finish_first(t):
            i = t % 2
            a, r = rstd(t, H[:, t, :], XS[i][:, :], xs_read[i], h_done[t])
            m = dve.do(lambda e: e.scalar_tensor_tensor(out=H[:, t, :], in0=H[:, t, :], scalar=rst[:, t:t + 1],
                                                        in1=GB[:, :], op0=ALU.mult, op1=ALU.mult), r, a, gbf_ready)
            h2_stored[t] = dma(h2_d[:, t, :], H[:, t, :], h2_ds[t], m)
            xs_m[t] = norm(t, H[:, t, :], GB2[:, :], gb2_ready, m)
            h_read[t] = xs_m[t]

        for c in range(2):
            for t0 in (0, 4):
                bs = banks(4)
                for n in range(4):
                    t = t0 + n
                    end, = products([by_tokens(S_pg[c], t, bs[n])], range(8), "seq",
                                    release=[S_pg[c]] if t == NT - 1 else ())
                    u_free[t] = end
                    ple(t, c, bs[n], end)
                    if c:
                        if t >= 2:
                            to_u(t - 2, xs_m[t - 2], u_free[t - 2])
                        finish_first(t)
        ple_end = (pool.sem, pool.count)

        YH = [at(f"YH{i}", (OH, OX)[i], [P, 4, D], F32R) for i in range(2)]
        YL = [at(f"YL{i}", (OH, OX)[i] + 16 * K, [P, 4, D], F32R) for i in range(2)]
        YF = [at(f"YF{i}", (OH, OX)[i] + 16 * K, [P, 4, D]) for i in range(2)]
        PLH, PLL = (at(f"PL{n}", OX + 32 * K + 8 * K * i, [P, 2, D], F32R) for i, n in enumerate("HL"))
        W0, W1 = (at(f"WN{i}", OX + 48 * K + 4160 * i, [P, 1040]) for i in range(2))
        h_free = [h2_stored[t] for t in range(NT)] + [h_read[7]]
        pl_ready, pl_free = {}, [None]
        w_free = [None]
        y_done = {}
        silu_done = {}

        class Pads:
            done = None

        def pooled(g, j, bs, ends):
            w = 2 << g
            if Pads.done is None:
                z = [dve.do(lambda e, v=v: e.memset(v[:, 0:16], 0.0), xs_read) for v in (W0, W1)]
                Pads.done = z
            u = PS[:, bs[0]:bs[0] + 2, :].rearrange("p b c -> p (b c)")
            m = act.do(lambda e: e.activation(W0[:, 16:1040], u, ACT.Copy), ends, w_free, Pads.done, xs_read)
            src, dst = W0, W1
            s = 1
            while s < w:
                q = pool if s in (2, 8) else dve
                m = q.do(lambda e, src=src, dst=dst, s=s: e.tensor_tensor(dst[:, 16:1040], src[:, 16:1040],
                                                                          src[:, 16 - s:1040 - s], ALU.add), m, Pads.done, w_free, xs_read)
                src, dst = dst, src
                s *= 2
            m1 = dve.do(lambda e: e.scalar_tensor_tensor(out=dst[:, 32:1040], in0=src[:, 32:1040], scalar=1.0 / w,
                                                         in1=u[:, 16:1024], op0=ALU.mult, op1=ALU.subtract), m)
            m2 = dve.do(lambda e: e.tensor_tensor(dst[:, 16:32], src[:, 16:32], INV[:, g, :], ALU.mult), m, sc_ready)
            m2 = dve.do(lambda e: e.tensor_tensor(dst[:, 16:32], dst[:, 16:32], u[:, 0:16], ALU.subtract), m2)
            freed[bs[0]] = freed[bs[1]] = m2
            a = act.do(lambda e: e.activation(PLH[:, j, :], dst[:, 16:1040], ACT.Copy), m1, m2, pl_free, ple_end, sg_read)
            pl_ready[j] = w_free[0] = dve.do(lambda e: e.tensor_tensor(PLL[:, j, :], dst[:, 16:1040],
                                                                       PLH[:, j, :].bitcast(F32), ALU.subtract), a, pl_free)

        def silu(g, j, hf, b, end):
            tile = 2 * g + j
            z = YF[tile // 4][:, tile % 4, 512 * hf:512 * hf + 512]
            m = act.do(lambda e: e.activation(z, bank(b), ACT.Exp, scale=-1.0), end, h_free, ple_end, proj_end)
            m = dve.do(lambda e: e.tensor_scalar(z, z, 1.0, None, ALU.add), m)
            m = dve.do(lambda e: e.reciprocal(z, z), m)
            freed[b] = silu_done[tile, hf] = dve.do(lambda e: e.scalar_tensor_tensor(
                out=z, in0=bank(b), scalar=psc[:, tile:tile + 1], in1=z, op0=ALU.mult, op1=ALU.mult), m, sc_ready)

        def mixed(g, j, hf, b, end):
            tile = 2 * g + j
            d = slice(512 * hf, 512 * hf + 512)
            q, i = tile // 4, tile % 4
            y, yh, yl = YF[q][:, i, d], YH[q][:, i, d], YL[q][:, i, d]
            freed[b] = m = dve.do(lambda e: e.scalar_tensor_tensor(out=y, in0=bank(b), scalar=pgb[:, tile:tile + 1], in1=y,
                                                                   op0=ALU.add, op1=ALU.mult), end, silu_done[tile, hf])
            a = act.do(lambda e: e.activation(yh, y, ACT.Copy), m, h_free, ple_end)
            y_done[tile, hf] = dve.do(lambda e: e.tensor_tensor(yl, y, yh.bitcast(F32), ALU.subtract), a)

        def pair():
            turn[0] += turn[0] % 2
            turn[0] %= 8
            return banks(2)

        for g in range(4):
            su, sg, sw = S_pi[g]
            if g == 0:
                ba, bb = pair(), pair()
                e00, = products([by_columns(su, 0, 0, ba[0])], range(8), "seq")
                to_u(6, xs_m[6], u_free[6])
                e10, = products([by_columns(su, 1, 0, bb[0])], range(8), "seq")
                to_u(7, xs_m[7], u_free[7])
                e01, e11 = products([by_columns(su, 0, 1, ba[1]), by_columns(su, 1, 1, bb[1])], range(8), "kout", release=[su])
                pooled(g, 0, ba, [e00, e01])
                pooled(g, 1, bb, [e10, e11])
            else:
                ba, bb = pair(), pair()
                ends = products([by_columns(su, j, hf, (ba, bb)[j][hf]) for j in range(2) for hf in range(2)], range(8),
                                "kout", release=[su])
                pooled(g, 0, ba, ends[0:2])
                pooled(g, 1, bb, ends[2:4])
            bs = banks(4)
            gr = [(j, hf) for j in range(2) for hf in range(2)]
            ends = products([by_columns(sg, j, hf, bs[n]) for n, (j, hf) in enumerate(gr)], range(8), "kout", release=[sg])
            u_end = ends[-1]
            for n, (j, hf) in enumerate(gr):
                silu(g, j, hf, bs[n], ends[n])
            bs = banks(4)
            ends = products([by_columns(sw, j, hf, bs[n], PLH, PLL, lambda k, hf: pl_ready[k]) for n, (j, hf) in enumerate(gr)],
                            range(2), "kout", release=[sw])
            pl_free[0] = ends[-1]
            for n, (j, hf) in enumerate(gr):
                mixed(g, j, hf, bs[n], ends[n])

        H2 = at("H2", OU, [P, NT, D])
        RES = [at(f"RES{i}", OU + 32 * K + 4096 * i, [P, D]) for i in range(4)]
        gbo_ready = dma(GB[:, :], row("final_norm_w_2"), g_ds, h_read[7])
        for t in range(NT):
            h_done[t] = dma(H2[:, t, :], h2_d[:, t, :], h2_ds[t], u_end)
        out_ds = [dsem(f"out{i}") for i in range(4)]
        out_done = [u_end] * 4

        def last_norm(t):
            i = t % 4
            a, r = rstd(t, H2[:, t, :], RES[i][:, :], h_done[t], out_done[i], u_end)
            m = dve.do(lambda e: e.scalar_tensor_tensor(out=RES[i][:, :], in0=H2[:, t, :], scalar=rst[:, t:t + 1],
                                                        in1=GB[:, :], op0=ALU.mult, op1=ALU.mult), r, a, gbo_ready)
            out_done[i] = dma(out_v[:, t, :], RES[i][:, :], out_ds[i], m)

        for c in range(2):
            for t0 in (0, 4):
                bs = banks(4)
                d = slice(512 * c, 512 * c + 512)

                class Both:
                    def __init__(self, slab, t, b):
                        self.slab, self.t, self.b = slab, t, b

                    def __call__(self, k):
                        s = slice(P * self.t, P * self.t + P)
                        return (YH[k // 4][:, k % 4, s], YL[k // 4][:, k % 4, s]), self.slab.at(k, 0, 512), \
                            [split_done[self.slab.load_of(k)], y_done[k, self.t // 4]]

                order = "kout" if (c, t0) == (0, 0) else "seq"
                gs = [(bank(bs[n]), bs[n], Both(S_po[c], t0 + n, bs[n])) for n in range(4)]
                if order == "kout":
                    ends = products(gs, range(8), "kout")
                for n in range(4):
                    t = t0 + n
                    if order == "seq":
                        end, = products([gs[n]], range(8), "seq", release=[S_po[c]] if t == NT - 1 else ())
                    else:
                        end = ends[n]
                    freed[bs[n]] = h_done[t] = dve.do(lambda e, t=t, b=bs[n], d=d: e.tensor_tensor(
                        H2[:, t, d], bank(b), H2[:, t, d], ALU.add), end, h_done[t])
                    if c:
                        last_norm(t)
        sp.wait(*out_done)

        block = ctx.enter_context(nc.Block())

        @block.sync
        def _(eng):
            sp.run(eng)

        @block.tensor
        def _(eng):
            pe.run(eng)

        @block.scalar
        def _(eng):
            act.run(eng)

        @block.vector
        def _(eng):
            dve.run(eng)

        @block.gpsimd
        def _(eng):
            pool.run(eng)


_INS = ["x", "p", "g_mix", "w_in", "b_forget", "swa_sinks", "w_br_swa", "w_br_fox", "w_mix_out", "g_mlp", "w_ff1",
        "w_ff2", "g_ple", "w_ple_gate", "w_ple_proj", "g_final", "norm_w_2", "pool_in_w_2", "pool_group_w_2",
        "pool_group_b_2", "pool_scale_2", "pool_out_w_2", "final_norm_w_2"]


def constants():
    i = np.arange(P)
    mats = np.zeros((4, P, P), np.float32)
    mats[0] = np.eye(P)
    mats[1] = np.where(i[None, :] <= i[:, None], 0.0, -FAR)
    mats[2] = i[:, None] <= i[None, :]
    mats[3] = 1.0
    q, s = i[:, None] + P, np.arange(2 * P)[None, :]
    ahead = q // 64 - s // 64
    seen = (ahead >= 0) & (ahead <= 2)
    slopes = 2.0 ** -(np.arange(8) + 1.0)
    bias = np.where(seen[:, None, :], -slopes[None, :, None] * np.abs(q - s)[:, None, :], -FAR)
    inv = np.zeros((P, 4, 16), np.float32)
    for g in range(4):
        inv[:, g, :] = 1.0 / np.minimum(np.arange(16) + 1, 2 << g)
    return {"c_mats": mats, "c_bias": bias.astype(np.float32), "c_inv": inv}


def kernel(**inputs):
    import concourse.bacc as _bacc
    from concourse.bass_utils import run_bass_kernel_spmd as _run

    nc = _bacc.Bacc("TRN2", target_bir_lowering=False, num_devices=1)
    arrays, args = {}, {}
    for name in _INS:
        a = np.asarray(inputs[name])
        if name in ("pool_group_b_2", "pool_scale_2"):
            a = a.reshape(NT, P).T
        arrays[f"in_{name}"] = np.ascontiguousarray(a)
    for name, a in constants().items():
        arrays[f"in_{name}"] = a
    for key, a in arrays.items():
        args[key[3:]] = nc.dram_tensor(key, a.shape, mybir.dt.from_np(a.dtype), kind="ExternalInput").ap()
    out = nc.dram_tensor("out_0", (1, 1024, D), F32, kind="ExternalOutput").ap()
    build(nc, args, out)
    r = _run(nc, [arrays], core_ids=[0])
    return r.results[0]["out_0"]
```

```python
from contextlib import ExitStack

import numpy as np

import concourse.bass as bass
from concourse import mybir

F32 = mybir.dt.float32
F32R = mybir.dt.float32r
ALU = mybir.AluOpType
ACT = mybir.ActivationFunctionType
AX_X = mybir.AxisListType.X

P = 128
D = 1024
NT = 8
EPS = 1e-6
FAR = 3e38


class Queue:

    def __init__(self, sem):
        self.sem, self.count, self.ops, self.met = sem, 0, [], {}

    def wait(self, *marks):
        for m in marks:
            if m is None:
                continue
            if isinstance(m, list):
                self.wait(*m)
            elif self.met.get(id(m[0]), 0) < m[1]:
                self.met[id(m[0])] = m[1]
                self.ops.append((None, m[0], m[1]))

    def do(self, fn, *marks, signal=True):
        self.wait(*marks)
        if not signal:
            self.ops.append((fn, None, 0))
            return None
        self.count += 1
        self.ops.append((fn, self.sem, 1))
        return (self.sem, self.count)

    def run(self, eng):
        for fn, sem, n in self.ops:
            if fn is None:
                eng.wait_ge(sem, n)
            elif sem is None:
                fn(eng)
            else:
                fn(eng).then_inc(sem, n)


class DmaSem:
    def __init__(self, sem):
        self.sem, self.count = sem, 0


def build(nc, A, out):
    ctx = ExitStack()
    with ctx:
        def new_sem(name):
            return ctx.enter_context(nc.semaphore(name))

        SIZE = 212832
        arena = ctx.enter_context(nc.sbuf_tensor("arena", [P, SIZE // 4], F32))
        ARENA0 = (16481 + 31) // 32 * 32

        def at(name, off, shape, dt=F32):
            n = int(np.prod(shape[1:])) * 4
            assert off + n <= SIZE, (name, off, n)
            return nc.alloc_sbuf_tensor_at(name, list(shape), dt, offset=ARENA0 + off)

        K = 1024
        NRAW, NRING = 2, 5
        RAW = at("RAW", 0, [P, NRAW, 1024])
        RH = at("RH", 8 * K, [P, NRING, 1024], F32R)
        RL = at("RL", 28 * K, [P, NRING, 1024], F32R)
        o = 48 * K
        CST = at("CST", o, [P, 4, 128])
        o += 2048
        INV = at("INV", o, [P, 4, 16])
        o += 256
        SM = at("SM", o, [P, 256])
        o += 1024
        GB = at("GB", o, [P, D])
        o += 4096
        OH = o
        H = at("H", OH, [P, NT, D])
        OU = OH + 32 * K
        UH = at("UH", OU, [P, NT, D], F32R)
        UL = at("UL", OU + 32 * K, [P, NT, D], F32R)
        OX = OU + 64 * K
        ident, causal, tri, ones = (CST[:, i, :] for i in range(4))

        PS = ctx.enter_context(nc.psum_tensor("PS", [P, 8, 512], F32))

        pe, act, dve, pool, sp = (Queue(new_sem(f"done_{n}")) for n in ("pe", "act", "dve", "pool", "sp"))

        def dma(dst, src, ds, *marks):
            sp.wait(*marks)
            ds.count += 16
            sp.ops.append((lambda e: e.dma_start(dst, src), ds.sem, 16))
            return (ds.sem, ds.count)

        def dsem(name):
            return DmaSem(new_sem(name))

        small_at = [0]

        def small(n):
            a = small_at[0]
            small_at[0] += n
            assert small_at[0] <= 256
            return SM[:, a:a + n]

        x_v = A["x"].rearrange("b (t p) d -> p (b t) d", p=P)
        p_v = A["p"].rearrange("l b (t p) d -> p (l b t) d", p=P)
        out_v = out.rearrange("b (t p) d -> p (b t) d", p=P)

        def mat(name):
            v = A[name]
            while len(v.shape) > 2:
                v = v.rearrange("a b c -> (a b) c") if len(v.shape) == 3 else v.rearrange("a b c d -> (a b) c d")
            return v

        w_in, w_sa, w_fx, w_mix = mat("w_in"), mat("w_br_swa"), mat("w_br_fox"), mat("w_mix_out")
        w_f1, w_f2, w_pg, w_pp = mat("w_ff1"), mat("w_ff2"), mat("w_ple_gate"), mat("w_ple_proj")
        w_pi, w_gr, w_po = mat("pool_in_w_2"), mat("pool_group_w_2"), mat("pool_out_w_2")

        def row(name):
            v = A[name]
            if len(v.shape) == 2:
                v = v.rearrange("a b -> (a b)")
            return v.partition_broadcast(P)

        gates_d = nc.dram_tensor("gates_scratch", [16, P, D], F32, kind="Internal").ap()
        h2_d = nc.dram_tensor("h2_scratch", [P, NT, D], F32, kind="Internal").ap()

        loads = []

        def load(parts, n):
            loads.append((parts, n))
            return len(loads) - 1

        def load_k2(w, r0, c0):
            src = w[r0:r0 + 256, c0:c0 + 512].rearrange("(k p) c -> p k c", p=P)
            return load([(lambda s: s.rearrange("p (k c) -> p k c", k=2), src)], 1024)

        def load_k4(w, r0, nk, c0):
            src = w[r0:r0 + nk * P, c0:c0 + 256].rearrange("(k p) c -> p k c", p=P)
            return load([(lambda s: s[:, 0:nk * 256].rearrange("p (k c) -> p k c", k=nk), src)], nk * 256)

        class Slab:

            def __init__(self, idx, per, width):
                self.idx, self.per, self.width = idx, per, width

            def load_of(self, k):
                return self.idx[k // self.per]

            def at(self, k, c0, c1):
                s = self.load_of(k) % NRING
                a = (k % self.per) * self.width
                return RH[:, s, a + c0:a + c1], RL[:, s, a + c0:a + c1]

        def slab512(w, r0, c0, nk=8):
            return Slab([load_k2(w, r0 + 256 * j, c0) for j in range(nk // 2)], 2, 512)

        def slab256(w, r0, c0, nk=8):
            step = min(nk, 4)
            return Slab([load_k4(w, r0 + P * step * j, step, c0) for j in range(nk // step)], step, 256)

        def slab_misc():
            idx = []
            for k0 in (0, 3, 6):
                nk = min(3, 8 - k0)
                rows = slice(k0 * P, (k0 + nk) * P)
                idx.append(load([
                    (lambda s, nk=nk: s[:, 0:nk * 264].rearrange("p (k c) -> p k c", k=nk)[:, :, 0:256],
                     w_in[rows, 512:768].rearrange("(k p) c -> p k c", p=P)),
                    (lambda s, nk=nk: s[:, 0:nk * 264].rearrange("p (k c) -> p k c", k=nk)[:, :, 256:264],
                     w_in[rows, 2304:2312].rearrange("(k p) c -> p k c", p=P))], nk * 264))
            return Slab(idx, 3, 264)

        S_qa = slab512(w_in, 0, 0)
        S_ms = slab_misc()
        S_qb = slab512(w_in, 0, 768)
        S_kb = slab512(w_in, 0, 1280)
        S_vb = slab512(w_in, 0, 1792)
        S_gt = [slab512(w_in, 0, 2312 + 512 * j) for j in range(4)]
        S_y = [(slab512(w_sa, 0, 512 * j, 4), slab512(w_fx, 0, 512 * j, 4)) for j in range(2)]
        S_mx = [slab512(w_mix, 0, 512 * j) for j in range(2)]
        S_ff = []
        for c in range(8):
            S_ff.append((slab512(w_f1, 0, 512 * c), slab512(w_f2, 512 * c, 0, 4), slab512(w_f2, 512 * c, 512, 4)))
        S_pp = [slab512(w_pp, 0, 512 * j, 2) for j in range(2)]
        S_pg = [slab512(w_pg, 0, 512 * j) for j in range(2)]
        S_pi = []
        for g in range(4):
            S_pi.append((slab256(w_pi, 0, 256 * g), slab256(w_pi, 0, D + 256 * g), slab256(w_gr, 256 * g, 0, 2)))
        S_po = [slab512(w_po, 0, 512 * j) for j in range(2)]

        raw_ds = [dsem(f"raw{i}") for i in range(NRAW)]
        landed, split_done = {}, {}

        def fetch(i):
            if i >= len(loads):
                return
            for view, src in loads[i][0]:
                landed[i] = dma(view(RAW[:, i % NRAW, :]), src, raw_ds[i % NRAW], split_done.get(i - NRAW))

        def split(i, released=None):
            if i >= len(loads):
                return
            n, s, r = loads[i][1], i % NRING, i % NRAW
            m = act.do(lambda e: e.activation(RH[:, s, 0:n], RAW[:, r, 0:n], ACT.Copy), landed[i], released)
            split_done[i] = dve.do(lambda e: e.tensor_tensor(RL[:, s, 0:n], RAW[:, r, 0:n], RH[:, s, 0:n].bitcast(F32),
                                                             ALU.subtract), m, released)
            fetch(i + NRAW)

        late_splits = []

        def flush_splits():
            for i, mark in late_splits:
                split(i, mark)
            late_splits.clear()

        freed = [None] * 8
        turn, held = [0], []

        def banks(n):
            got = []
            while len(got) < n:
                if turn[0] not in held:
                    got.append(turn[0])
                turn[0] = (turn[0] + 1) % 8
            return got

        def products(groups, ks, order="kout", release=(), between=None):
            flush_splits()
            last_use = {}
            steps = [(k, g) for k in ks for g in range(len(groups))] if order == "kout" else \
                [(k, g) for g in range(len(groups)) for k in ks]
            for n, (k, g) in enumerate(steps):
                last_use[k] = n
            ends = [None] * len(groups)
            of_load = {}
            for slab in release:
                for k in ks:
                    ld = slab.load_of(k)
                    of_load[ld] = max(of_load.get(ld, 0), last_use[k])
            for n, (k, g) in enumerate(steps):
                o_ap, b, operands = groups[g]
                (sh, sl), (mh, ml), marks = operands(k)
                first, last = k == ks[0], k == ks[-1]
                if first:
                    pe.wait(freed[b])
                pe.wait(marks)
                pe.do(lambda e, o_ap=o_ap, sh=sh, mh=mh, first=first: e.matmul(o_ap, sh, mh, start=first, stop=False),
                      signal=False)
                pe.do(lambda e, o_ap=o_ap, sh=sh, ml=ml: e.matmul(o_ap, sh, ml, start=False, stop=False), signal=False)
                out_of = [ld for ld, m in of_load.items() if m == n]
                mark = pe.do(lambda e, o_ap=o_ap, sl=sl, mh=mh, last=last:
                             e.matmul(o_ap, sl, mh, start=False, stop=last), signal=last or bool(out_of))
                if last:
                    ends[g] = mark
                for ld in sorted(out_of):
                    if n == len(steps) - 1:
                        late_splits.append((ld + NRING, mark))
                    else:
                        split(ld + NRING, mark)
                if between and k in between and g == len(groups) - 1:
                    between[k]()
            return ends

        def bank(b, n=512):
            return PS[:, b, 0:n]

        u_ready = [None] * NT

        def by_columns(slab, j, half, b, hi=None, lo=None, ready=None, kin=None):
            hi, lo, ready = hi or UH, lo or UL, ready or u_ready
            t0, t1 = 512 * half, 512 * half + 512

            def operands(k):
                r = ready(k, half) if callable(ready) else ready[4 * half:4 * half + 4]
                return slab.at(k, 128 * j, 128 * j + 128), (hi[:, k, t0:t1], lo[:, k, t0:t1]), \
                    [split_done[slab.load_of(k)], r]
            return (bank(b), b, operands)

        def by_tokens(slab, t, b, c0=0, c1=512, hi=None, lo=None, ready=None, o_ap=None):
            hi, lo = hi or UH, lo or UL

            def operands(k):
                r = ready(k, t) if callable(ready) else (ready or u_ready)[t]
                return (hi[:, k, P * t:P * t + P], lo[:, k, P * t:P * t + P]), slab.at(k, c0, c1), \
                    [split_done[slab.load_of(k)], r]
            return (bank(b, c1 - c0) if o_ap is None else o_ap, b, operands)

        ssq, rms, rst, mhalf = small(NT), small(NT), small(NT), small(1)
        mhalf_done = pool.do(lambda e: e.memset(mhalf, -0.5))
        XS = [at(f"XS{i}", OX + 48 * K + 4096 * i, [P, D]) for i in range(2)]
        xs_read = [None, None]

        def rstd(t, src, scratch, *marks):
            a = act.do(lambda e: e.activation(scratch, src, ACT.Square, accum_out=ssq[:, t:t + 1]), *marks)
            b = pool.do(lambda e: e.tensor_scalar(rms[:, t:t + 1], ssq[:, t:t + 1], 1.0 / D, EPS, ALU.mult, ALU.add), a)
            return a, pool.do(lambda e: e.tensor_tensor(rst[:, t:t + 1], rms[:, t:t + 1], mhalf, ALU.pow), b, mhalf_done)

        def norm(t, src, gain, gain_ready, *marks):
            i = t % 2
            a, r = rstd(t, src, XS[i][:, :], xs_read[i], *marks)
            return dve.do(lambda e: e.scalar_tensor_tensor(out=XS[i][:, :], in0=src, scalar=rst[:, t:t + 1], in1=gain,
                                                           op0=ALU.mult, op1=ALU.mult), r, a, gain_ready)

        def to_u(t, xs_mark, *marks):
            i = t % 2
            for q in range(2):
                b, = banks(1)
                pe.wait(freed[b], xs_mark, c_ready)
                for k in range(4):
                    m = pe.do(lambda e, k=k, q=q, b=b: e.transpose(
                        PS[:, b, P * k:P * k + P], XS[i][:, P * (4 * q + k):P * (4 * q + k) + P], ident),
                              signal=(k == 3))
                xs_read[i] = m
                src = PS[:, b, :].rearrange("p (k c) -> p k c", k=4)
                hi, lo = (v[:, 4 * q:4 * q + 4, P * t:P * t + P] for v in (UH, UL))
                a = act.do(lambda e, src=src, hi=hi: e.activation(hi, src, ACT.Copy), m, *marks)
                freed[b] = u_ready[t] = dve.do(lambda e, src=src, hi=hi, lo=lo: e.tensor_tensor(
                    lo, src, hi.bitcast(F32), ALU.subtract), a, *marks)

        x_ds = [dsem(f"x{t}") for t in range(NT)]
        c_ds = dsem("consts")
        g_ds, sc_ds = dsem("gain"), dsem("small_consts")
        x_in = [dma(H[:, 0, :], x_v[:, 0, :], x_ds[0])]
        gb_ready = dma(GB[:, :], row("g_mix"), g_ds)
        x_in.append(dma(H[:, 1, :], x_v[:, 1, :], x_ds[1]))
        c_ready = dma(CST[:, :, :], A["c_mats"].rearrange("i p c -> p i c"), c_ds)
        for t in (2, 3):
            x_in.append(dma(H[:, t, :], x_v[:, t, :], x_ds[t]))
        fetch(0)
        fetch(1)
        for t in range(4, NT):
            x_in.append(dma(H[:, t, :], x_v[:, t, :], x_ds[t]))
        bf, snk = small(8), small(8)
        pgb, psc = small(8), small(8)
        dma(INV[:, :, :], A["c_inv"], sc_ds)
        dma(bf, row("b_forget"), sc_ds)
        dma(snk, row("swa_sinks"), sc_ds)
        dma(pgb, A["pool_group_b_2"], sc_ds)
        sc_ready = dma(psc, A["pool_scale_2"], sc_ds)

        xs_m = {}

        def first_norm(t):
            xs_m[t] = norm(t, H[:, t, :], GB[:, :], gb_ready, x_in[t])
            to_u(t, xs_m[t])

        for t in range(4):
            first_norm(t)
            if t:
                split(t - 1)

        QB = at("QB", OH, [P, 4, D])
        KB = at("KB", OH + 16 * K, [P, 4, D])
        QA = at("QA", OX, [P, 4, D])
        KD = at("KD", OX + 16 * K, [P, 2, D])
        VB = at("VB", OX + 24 * K, [P, NT, 512])
        VA = at("VA", OX + 40 * K, [P, NT, P])
        GST = [at(f"GST{i}", OX + 44 * K + 2048 * i, [P, 512]) for i in range(2)]

        def first_half_first(slab, between, evac):
            for hf in range(2):
                bs = banks(4)
                held[:] = bs
                ends = products([by_columns(slab, j, hf, bs[j]) for j in range(4)], range(8), "kout",
                                release=[slab] if hf else (), between=None if hf else between)
                held.clear()
                for j in range(4):
                    evac(j, hf, bs[j], ends[j])
                if not hf:
                    turn[0] = (bs[0] + 4) % 8

        def heads(slab, dst, scale, *marks):
            done = {}
            for j0 in (0, 2):
                bs = banks(4)
                gr = [(j, h) for h in range(2) for j in (j0, j0 + 1)]
                ends = products([by_columns(slab, j, h, bs[n]) for n, (j, h) in enumerate(gr)], range(8), "seq",
                                release=[slab] if j0 else ())
                for n, (j, h) in enumerate(gr):
                    freed[bs[n]] = done[j, h] = act.do(
                        lambda e, b=bs[n], j=j, h=h: e.activation(dst[:, j, 512 * h:512 * h + 512], bank(b), ACT.Copy,
                                                                  scale=scale), ends[n], *marks)
            return done

        qa_done = {}

        def qa_evac(j, h, b, end):
            freed[b] = qa_done[j, h] = act.do(lambda e: e.activation(QA[:, j, 512 * h:512 * h + 512], bank(b), ACT.Copy,
                                                                     scale=0.125), end)

        def late_first(t):
            def f():
                first_norm(t)
                if t - 1 < NRING:
                    split(t - 1)
            return f

        first_half_first(S_qa, {2 * t - 8: late_first(t) for t in range(4, NT)}, qa_evac)
        x_read = xs_m[NT - 1]

        F = small(64)
        F3 = F.rearrange("p (t h) -> p t h", t=NT)
        bs = banks(2)
        ends = products([by_columns(S_ms, 0, h, bs[h]) for h in range(2)], range(8))
        kd_done = []
        for h in range(2):
            sl = slice(512 * h, 512 * h + 512)
            b = bs[h]
            for g in range(2):
                for r in range(2):
                    m = act.do(lambda e, g=g, r=r, b=b, sl=sl: e.activation(
                        KD[64 * r:64 * r + 64, g, sl], PS[64 * g:64 * g + 64, b, :], ACT.Copy), ends[h])
            freed[b] = m
            kd_done.append(m)
        bs = banks(4)
        va_done, f_done = {}, {}
        vf_end = {}
        for t in range(NT):
            b, c = bs[t // 2], 136 * (t % 2)
            vf_end[t], = products([by_tokens(S_ms, t, b, 128, 264, o_ap=PS[:, b, c:c + 136])], range(8),
                                  release=[S_ms] if t == NT - 1 else ())
            if t % 2:
                for tt in (t - 1, t):
                    c = 136 * (tt % 2)
                    va_done[tt] = dve.do(lambda e, tt=tt, b=b, c=c: e.tensor_copy(VA[:, tt, :], PS[:, b, c:c + P]),
                                         vf_end[t])
                    freed[b] = f_done[tt] = dve.do(lambda e, tt=tt, b=b, c=c: e.tensor_tensor(
                        F3[:, tt, :], PS[:, b, c + P:c + P + 8], bf, ALU.add), vf_end[t], sc_ready)

        qb_done = heads(S_qb, QB, 0.125, x_read)
        kb_done = heads(S_kb, KB, 1.0, x_read)
        vb_done = {}
        for t0 in (0, 4):
            bs = banks(4)
            ends = products([by_tokens(S_vb, t0 + n, bs[n]) for n in range(4)], range(8), "kout",
                            release=[S_vb] if t0 else ())
            for n in range(4):
                freed[bs[n]] = vb_done[t0 + n] = act.do(lambda e, t=t0 + n, b=bs[n]: e.activation(
                    VB[:, t, :], bank(b), ACT.Copy), ends[n])

        gst_ds = [dsem("gst0"), dsem("gst1")]
        gate_stored = {}
        stored = [None, None]
        n_st = 0
        last_gate = None
        for s in range(4):
            for j0 in (0, 2):
                bs = banks(4)
                gr = [(j, h) for j in (j0, j0 + 1) for h in range(2)]
                ends = products([by_columns(S_gt[s], j, h, bs[n]) for n, (j, h) in enumerate(gr)], range(8), "kout",
                                release=[S_gt[s]] if j0 else ())
                last_gate = ends[-1]
                for n, (j, h) in enumerate(gr):
                    i = n_st % 2
                    n_st += 1
                    g = GST[i][:, :]
                    freed[bs[n]] = m = act.do(lambda e, g=g, b=bs[n]: e.activation(g, bank(b), ACT.Sigmoid),
                                              ends[n], stored[i])
                    gate_stored[4 * s + j, h] = stored[i] = dma(gates_d[4 * s + j, :, 512 * h:512 * h + 512], g,
                                                                gst_ds[i], m)

        OA = at("OA", OU, [P, NT, 512])
        OB = at("OB", OU + 16 * K, [P, NT, 512])
        T = [at(f"T{i}", OU + 32 * K + 4096 * i, [P, D]) for i in range(2)]
        E = [at(f"E{i}", OU + 40 * K + 4096 * i, [P, D]) for i in range(4)]
        BIAS = at("BIAS", OU + 56 * K, [P, 8, 256])
        NC = [at(f"NC{i}", OU + 56 * K + 4096 * i, [P, D]) for i in range(2)]
        PT = [at(f"PT{i}", OX + 48 * K + 2048 * i, [P, 4, P]) for i in range(4)]
        pt_read = [None] * 4
        n_pt = [0]
        free_u = last_gate
        bias_ready = dma(BIAS[:, :, :], A["c_bias"], dsem("bias"), free_u)

        def turn_probs(src_blocks, src_mark, b_of):
            got = []
            for q0 in range(0, len(src_blocks), 4):
                blk = src_blocks[q0:q0 + 4]
                b = b_of(q0 // 4)
                pe.wait(freed[b], src_mark)
                for n, s in enumerate(blk):
                    m = pe.do(lambda e, n=n, s=s, b=b: e.transpose(PS[:, b, P * n:P * n + P], s, ident),
                              signal=(n == len(blk) - 1))
                i = n_pt[0] % 4
                n_pt[0] += 1
                w = P * len(blk)
                q = act if (q0 // 4 + n_pt[0]) % 2 else dve
                dst = PT[i][:, 0:len(blk), :].rearrange("p k c -> p (k c)")
                if q is act:
                    freed[b] = q.do(lambda e, dst=dst, b=b, w=w: e.activation(dst, PS[:, b, 0:w], ACT.Copy), m, pt_read[i], xs_read)
                else:
                    freed[b] = q.do(lambda e, dst=dst, b=b, w=w: e.tensor_copy(dst, PS[:, b, 0:w]), m, pt_read[i], xs_read)
                got.append((i, freed[b]))
            return got

        C = small(64)
        C3 = C.rearrange("p (t h) -> p t h", t=NT)

        def forget_gates():
            FT = at("FT", OX + 44 * K, [P, 6, 64])
            fa, fe, fw, fl, fm, LF = (FT[:, i, :] for i in range(6))
            fd = [f_done[t] for t in range(NT)]
            m1 = dve.do(lambda e: e.tensor_scalar(fm, F, 0.0, None, ALU.min), fd, stored)
            m2 = dve.do(lambda e: e.tensor_scalar(fa, F, -1.0, None, ALU.mult), fd)
            m2 = dve.do(lambda e: e.tensor_tensor(fa, F, fa, ALU.min), m2)
            m3 = act.do(lambda e: e.activation(fe, fa, ACT.Exp), m2)
            m4 = dve.do(lambda e: e.tensor_scalar(fw, fe, 1.0, None, ALU.add), m3)
            m5 = act.do(lambda e: e.activation(fl, fw, ACT.Ln), m4)
            m6 = dve.do(lambda e: e.tensor_scalar(fa, fw, -1.0, None, ALU.add), m4, m3)
            m6 = dve.do(lambda e: e.tensor_tensor(fa, fe, fa, ALU.subtract), m6)
            m7 = dve.do(lambda e: e.reciprocal(fw, fw), m5, m6)
            m7 = dve.do(lambda e: e.tensor_tensor(fa, fa, fw, ALU.mult), m7)
            m7 = dve.do(lambda e: e.tensor_tensor(fl, fl, fa, ALU.add), m7)
            lf_done = dve.do(lambda e: e.tensor_tensor(LF, fm, fl, ALU.subtract), m7, m1)
            LF3 = LF.rearrange("p (t h) -> p t h", t=NT)
            b = 6
            pe.wait(freed[b], lf_done, c_ready)
            for t in range(NT):
                for j in range(t + 1):
                    m = pe.do(lambda e, t=t, j=j, b=b: e.matmul(PS[:, b, 8 * t:8 * t + 8], tri if j == t else ones,
                                                                LF3[:, j, :], start=(j == 0), stop=(j == t)),
                              signal=(t == NT - 1 and j == t))
            freed[b] = dve.do(lambda e, b=b: e.tensor_copy(C, PS[:, b, 0:64]), m)
            return freed[b]

        mx, nm, es, den, rd = small(8), small(8), small(8), small(8), small(16)
        units = [(g, n) for n in range(NT) for g in range(2)]
        stage = {}
        t_read, e_read, rd_read, den_read = [None] * 2, [None] * 4, [None] * 4, [None] * 2

        def swa_scores(i):
            g, n = units[i]
            w = 256 if n else P
            s0 = P * (n - 1) if n else 0
            sb = 2 * (i % 2)
            pe.wait(freed[sb], freed[sb + 1], kd_done, [qa_done[j, n // 4] for j in range(4)])
            for a in range(4):
                h = 4 * g + a
                r = slice(64 * (h % 2), 64 * (h % 2) + 64)
                m = pe.do(lambda e, a=a, h=h, r=r: e.matmul(PS[:, sb + a % 2, 256 * (a // 2):256 * (a // 2) + w],
                                                            QA[r, h // 2, P * n:P * n + P], KD[r, g, s0:s0 + w],
                                                            start=True, stop=True), signal=(a == 3))
            tv = T[i % 2][:, :].rearrange("p (a c) -> p a c", a=4)[:, :, 0:w]
            q = slice(4 * (i % 2), 4 * (i % 2) + 4)
            for a in range(4):
                c = 4 * (i % 2) + a
                t1 = dve.do(lambda e, a=a, c=c: e.tensor_tensor_reduce(
                    tv[:, a, :], PS[:, sb + a % 2, 256 * (a // 2):256 * (a // 2) + w], BIAS[:, 4 * g + a, 256 - w:256],
                    1.0, -FAR, ALU.add, ALU.max, mx[:, c:c + 1]), m, bias_ready, t_read[i % 2], free_u)
            freed[sb] = freed[sb + 1] = t1
            t2 = dve.do(lambda e: e.tensor_tensor(mx[:, q], mx[:, q], snk[:, 4 * g:4 * g + 4], ALU.max), t1, sc_ready)
            t3 = dve.do(lambda e: e.tensor_scalar(nm[:, q], mx[:, q], -1.0, None, ALU.mult), t2, t_read[i % 2])
            ev = E[i % 4][:, :].rearrange("p (a c) -> p a c", a=4)[:, :, 0:w]
            ms = []
            for a in range(4):
                c = 4 * (i % 2) + a
                ms.append(act.do(lambda e, a=a, c=c: e.activation(ev[:, a, :], tv[:, a, :], ACT.Exp, bias=nm[:, c:c + 1],
                                                                  accum_out=den[:, c:c + 1]), t3, e_read[i % 4], den_read[i % 2]))
            t_read[i % 2] = ms[-1]
            t4 = dve.do(lambda e: e.tensor_tensor(es[:, q], snk[:, 4 * g:4 * g + 4], mx[:, q], ALU.subtract), t2)
            t5 = act.do(lambda e: e.activation(es[:, q], es[:, q], ACT.Exp), t4)
            t6 = dve.do(lambda e: e.tensor_tensor(den[:, q], den[:, q], es[:, q], ALU.add), t5, ms[-1])
            t7 = dve.do(lambda e: e.reciprocal(rd[:, 4 * (i % 4):4 * (i % 4) + 4], den[:, q]), t6, rd_read[i % 4])
            den_read[i % 2] = t7
            stage[i] = (ms[-1], t7)

        def swa_turn(i):
            g, n = units[i]
            nk = 2 if n else 1
            ev = E[i % 4][:, :].rearrange("p (a k c) -> p a k c", a=4, k=2)
            blocks = [ev[:, a, k, :] for a in range(4) for k in range(nk)]
            got = turn_probs(blocks, stage[i][0], lambda q: 4 + q)
            e_read[i % 4] = (pe.sem, pe.count)
            stage[i] += (got,)

        def swa_values(i):
            g, n = units[i]
            nk = 2 if n else 1
            _, rden, got = stage[i]
            b = 6 + i % 2
            pe.wait(freed[b], [m for _, m in got], [va_done[t] for t in range(max(n - 1, 0), n + 1)])
            for a in range(4):
                for k in range(nk):
                    blk = a * nk + k
                    pi = got[blk // 4][0]
                    tile = n - nk + 1 + k
                    m = pe.do(lambda e, a=a, k=k, pi=pi, blk=blk, tile=tile: e.matmul(
                        PS[:, b, 64 * a:64 * a + 64], PT[pi][:, blk % 4, :], VA[:, tile, 64 * g:64 * g + 64],
                        start=(k == 0), stop=(k == nk - 1)), signal=(k == nk - 1))
            for pi, _ in got:
                pt_read[pi] = m
            q = slice(4 * (i % 4), 4 * (i % 4) + 4)
            freed[b] = dve.do(lambda e: e.tensor_tensor(
                OA[:, n, 256 * g:256 * g + 256].rearrange("p (a c) -> p a c", a=4),
                PS[:, b, 0:256].rearrange("p (a c) -> p a c", a=4),
                rd[:, q].unsqueeze(2).to_broadcast([P, 4, 64]), ALU.mult), m, rden, free_u)
            rd_read[i % 4] = freed[b]
            oa_done[i] = freed[b]

        oa_done = {}
        LAGT, LAGV = 2, 3
        for i in range(len(units) + LAGV):
            if i >= LAGV:
                swa_values(i - LAGV)
            if LAGT <= i < len(units) + LAGT:
                swa_turn(i - LAGT)
            if i < len(units):
                swa_scores(i)
            if i == 6:
                c_done = forget_gates()

        nc_done, nc_read = {}, [None, None]

        def fox_keys(h):
            i = h % 2
            bb = (6, 7)
            for q in range(2):
                b = bb[q]
                pe.wait(freed[b], c_done, c_ready)
                for k in range(4):
                    col = C3[:, 4 * q + k, h:h + 1]
                    m = pe.do(lambda e, k=k, b=b, col=col: e.matmul(PS[:, b, P * k:P * k + P],
                                                                    col.to_broadcast([P, P]), ident, start=True,
                                                                    stop=True), signal=(k == 3))
                freed[b] = a = act.do(lambda e, q=q, b=b: e.activation(NC[i][:, 512 * q:512 * q + 512], bank(b), ACT.Copy,
                                                                       scale=-1.0), m, nc_read[i], oa_done[15], free_u)
            nc_done[h] = a

        fmx, fnm, fden, frd = small(2), small(2), small(4), small(4)
        funits = [(h, t) for h in range(8) for t in reversed(range(NT))]
        fst = {}
        fnm_read, frd_read, fden_read = [None] * 2, [None] * 4, [None] * 4
        ob_done = {}

        def fox_scores(i):
            h, t = funits[i]
            n = P * (t + 1)
            r = slice(64 * (h % 2), 64 * (h % 2) + 64)
            sb = 2 * (i % 2)
            pe.wait(freed[sb], freed[sb + 1], [qb_done[h // 2, x] for x in range(2)], [kb_done[h // 2, x] for x in range(2)])
            for c0 in range(0, n, 512):
                c1 = min(n, c0 + 512)
                m = pe.do(lambda e, c0=c0, c1=c1: e.matmul(PS[:, sb + c0 // 512, 0:c1 - c0], QB[r, h // 2, P * t:P * t + P],
                                                           KB[r, h // 2, c0:c1], start=True, stop=True),
                          signal=(c1 == n))
            s = PS[:, sb:sb + 2, :].rearrange("p b c -> p (b c)")
            tv, ev, ncv = T[i % 2], E[i % 4], NC[h % 2]
            cq = C3[:, t, h:h + 1]
            j, j4 = i % 2, i % 4
            km = pool.do(lambda e: e.tensor_tensor(ncv[:, n - P:n], ncv[:, n - P:n], causal, ALU.add), nc_done[h],
                         nc_read[h % 2] if t < NT - 1 else None, c_ready)
            t1 = dve.do(lambda e: e.tensor_tensor_reduce(tv[:, 0:n], s[:, 0:n], ncv[:, 0:n], 1.0, -FAR, ALU.add, ALU.max,
                                                         fmx[:, j:j + 1]), m, km, nc_done[h], t_read[j])
            freed[sb] = freed[sb + 1] = t1
            nc_read[h % 2] = t1
            t2 = dve.do(lambda e: e.tensor_tensor(fmx[:, j:j + 1], fmx[:, j:j + 1], cq, ALU.add), t1, c_done)
            t3 = dve.do(lambda e: e.tensor_tensor(fnm[:, j:j + 1], cq, fmx[:, j:j + 1], ALU.subtract), t2, fnm_read[j])
            t4 = act.do(lambda e: e.activation(ev[:, 0:n], tv[:, 0:n], ACT.Exp, bias=fnm[:, j:j + 1],
                                               accum_out=fden[:, j4:j4 + 1]), t3, e_read[j4], fden_read[j4])
            t_read[j] = fnm_read[j] = t4
            fst[i] = (t4,)

        def fox_turn(i):
            h, t = funits[i]
            blocks = [E[i % 4][:, P * k:P * k + P] for k in range(t + 1)]
            got = turn_probs(blocks, fst[i][0], lambda q: 4 + q)
            e_read[i % 4] = (pe.sem, pe.count)
            j = i % 4
            rden = fden_read[j] = dve.do(lambda e: e.reciprocal(frd[:, j:j + 1], fden[:, j:j + 1]), fst[i][0], frd_read[j])
            fst[i] = (got, rden)

        def fox_values(i):
            h, t = funits[i]
            got, rden = fst[i]
            b = 6 + i % 2
            pe.wait(freed[b], [m for _, m in got], [vb_done[k] for k in range(t + 1)])
            for k in range(t + 1):
                pi = got[k // 4][0]
                m = pe.do(lambda e, k=k, pi=pi: e.matmul(PS[:, b, 0:64], PT[pi][:, k % 4, :], VB[:, k, 64 * h:64 * h + 64],
                                                         start=(k == 0), stop=(k == t)), signal=(k == t))
            for pi, _ in got:
                pt_read[pi] = m
            j = i % 4
            freed[b] = frd_read[j] = ob_done[i] = act.do(lambda e: e.activation(
                OB[:, t, 64 * h:64 * h + 64], PS[:, b, 0:64], ACT.Copy, scale=frd[:, j:j + 1]), m, rden, free_u)

        LAGT, LAGV = 3, 4
        fox_keys(0)
        for i in range(len(funits) + LAGV):
            if i >= LAGV:
                fox_values(i - LAGV)
            if LAGT <= i < len(funits) + LAGT:
                fox_turn(i - LAGT)
            if i < len(funits):
                fox_scores(i)
                if i % 8 == 4 and i < 56:
                    fox_keys(i // 8 + 1)
        attn_end = ob_done[63]

        OAH, OAL = (at(f"OA{n}", OH + 16 * K * i, [P, 4, D], F32R) for i, n in enumerate("HL"))
        OBH, OBL = (at(f"OB{n}", OX + 16 * K * i, [P, 4, D], F32R) for i, n in enumerate("HL"))
        turn[0] = 0
        pe_mark = (pe.sem, pe.count)
        ot_ready = {}
        ot_end = None
        for src, hi, lo, done, br in ((OA, OAH, OAL, [oa_done[14], oa_done[15]], 0), (OB, OBH, OBL, [attn_end], 1)):
            for j in range(4):
                for hf in range(2):
                    b, = banks(1)
                    pe.wait(freed[b], done)
                    for n in range(4):
                        ot_end = m = pe.do(lambda e, n=n, b=b, src=src, j=j, hf=hf: e.transpose(
                            PS[:, b, P * n:P * n + P], src[:, 4 * hf + n, P * j:P * j + P], ident), signal=(n == 3))
                    d = slice(512 * hf, 512 * hf + 512)
                    a = act.do(lambda e, b=b, hi=hi, j=j, d=d: e.activation(hi[:, j, d], bank(b), ACT.Copy), m, pe_mark)
                    freed[b] = ot_ready[br, j, hf] = dve.do(lambda e, b=b, hi=hi, lo=lo, j=j, d=d: e.tensor_tensor(
                        lo[:, j, d], bank(b), hi[:, j, d].bitcast(F32), ALU.subtract), a, pe_mark)

        G = [at(f"G{i}", OX + 32 * K + 4096 * i, [P, 2, 512]) for i in range(2)]
        Y = [at(f"Y{i}", OX + 40 * K + 4096 * i, [P, 2, 512]) for i in range(2)]
        g_in_ds = [dsem("g_in0"), dsem("g_in1")]
        g_read, y_read = [pe_mark] * 2, [pe_mark] * 2
        mix_ready = {}

        def fetch_gates(i):
            if i >= 16:
                return None
            j, hf = i // 2, i % 2
            dma(G[i % 2][:, 0, :], gates_d[j, :, 512 * hf:512 * hf + 512], g_in_ds[i % 2], gate_stored[j, hf], g_read[i % 2])
            return dma(G[i % 2][:, 1, :], gates_d[8 + j, :, 512 * hf:512 * hf + 512], g_in_ds[i % 2],
                       gate_stored[8 + j, hf], g_read[i % 2])

        g_in = {0: fetch_gates(0), 1: fetch_gates(1)}
        y_end = None
        for j in range(8):
            bs = banks(4)
            sa, sf = S_y[j // 4]
            jj = j % 4
            gr = [(br, hf) for br in range(2) for hf in range(2)]
            ends = []
            for br, slab in ((0, sa), (1, sf)):
                hi, lo = ((OAH, OAL), (OBH, OBL))[br]
                ends += products([by_columns(slab, jj, hf, bs[2 * br + hf], hi, lo,
                                             lambda k, hf, br=br: ot_ready[br, k, hf]) for hf in range(2)], range(4),
                                 "kout", release=[slab] if jj == 3 else ())
            y_end = ends[3]
            for hf in range(2):
                i = 2 * j + hf
                q = i % 2
                ba, bb = bs[hf], bs[2 + hf]
                freed[ba] = m1 = dve.do(lambda e, q=q, ba=ba: e.tensor_tensor(Y[q][:, 0, :], bank(ba), G[q][:, 0, :], ALU.mult),
                                        ends[hf], g_in[i], y_read[q])
                freed[bb] = m2 = dve.do(lambda e, q=q, bb=bb: e.tensor_tensor(Y[q][:, 1, :], bank(bb), G[q][:, 1, :], ALU.mult),
                                        ends[2 + hf], g_in[i])
                g_read[q] = m2
                g_in[i + 2] = fetch_gates(i + 2)
                m3 = pool.do(lambda e, q=q: e.tensor_tensor(Y[q][:, 0, :], Y[q][:, 0, :], Y[q][:, 1, :], ALU.add), m1, m2)
                d = slice(512 * hf, 512 * hf + 512)
                m4 = act.do(lambda e, q=q, j=j, d=d: e.activation(UH[:, j, d], Y[q][:, 0, :], ACT.Copy), m3, ot_end)
                mix_ready[j, hf] = y_read[q] = dve.do(lambda e, q=q, j=j, d=d: e.tensor_tensor(
                    UL[:, j, d], Y[q][:, 0, :], UH[:, j, d].bitcast(F32), ALU.subtract), m4, ot_end)

        h_done = {}
        for t in range(NT):
            h_done[t] = dma(H[:, t, :], x_v[:, t, :], x_ds[t], y_end)
        gb_ready = dma(GB[:, :], row("g_mlp"), g_ds, x_read)

        def add_to_h(t, c, b, mark, *marks):
            d = slice(512 * c, 512 * c + 512)
            freed[b] = dve.do(lambda e: e.tensor_tensor(H[:, t, d], bank(b), H[:, t, d], ALU.add), mark, *marks)
            return freed[b]

        def into_h(slabs, operands_of, order0, then):
            for c in range(2):
                for t0 in (0, 4):
                    bs = banks(4)
                    order = order0 if (c, t0) == (0, 0) else "seq"
                    if order == "kout":
                        ends = products([operands_of(slabs[c], t0 + n, bs[n]) for n in range(4)], range(8), "kout")
                        for n in range(4):
                            h_done[t0 + n] = add_to_h(t0 + n, c, bs[n], ends[n], h_done[t0 + n])
                        continue
                    for n in range(4):
                        t = t0 + n
                        end, = products([operands_of(slabs[c], t, bs[n])], range(8), "seq",
                                        release=[slabs[c]] if t == NT - 1 else ())
                        h_done[t] = add_to_h(t, c, bs[n], end, h_done[t])
                        if c:
                            then(t, end)

        xs_m, u_free = {}, {}

        def norm_mlp(t, end):
            u_free[t] = end
            if t >= 2:
                to_u(t - 2, xs_m[t - 2], u_free[t - 2])
            xs_m[t] = norm(t, H[:, t, :], GB[:, :], gb_ready, h_done[t])

        into_h(S_mx, lambda s, t, b: by_tokens(s, t, b, ready=lambda k, t: mix_ready[k, t // 4]), "kout", norm_mlp)

        HH, HL = (at(f"HID{n}", OX + 16 * K * i, [P, 4, D], F32R) for i, n in enumerate("HL"))
        R = [at(f"R{i}", OX + 32 * K + 2048 * i, [P, 512]) for i in range(2)]
        R2 = [at(f"RR{i}", OX + 36 * K + 2048 * i, [P, 512]) for i in range(2)]
        r_read, n_r = [y_end, y_end], [0]
        hid_ready, hid_free = {}, [y_end]
        PST = at("PST", OX + 40 * K, [P, NT, 256])
        p_in = dma(PST[:, :, :], p_v, dsem("p_in"), mix_ready[7, 0], mix_ready[7, 1])

        def squared_relu(j, hf, b, end):
            i = n_r[0] % 2
            n_r[0] += 1
            d = slice(512 * hf, 512 * hf + 512)
            freed[b] = m = dve.do(lambda e: e.tensor_scalar(R[i][:, :], bank(b), 0.0, None, ALU.max), end, r_read[i],
                                  g_read, y_read)
            a = act.do(lambda e: e.activation(HH[:, j, d], R[i][:, :], ACT.Square), m, hid_free)
            s = pool.do(lambda e: e.tensor_tensor(R2[i][:, :], R[i][:, :], R[i][:, :], ALU.mult), m, r_read[i])
            hid_ready[j, hf] = r_read[i] = dve.do(lambda e: e.tensor_tensor(
                HL[:, j, d], R2[i][:, :], HH[:, j, d].bitcast(F32), ALU.subtract), a, s, hid_free)

        last_f1 = None
        gbp_ready = None
        ff2_end = {}

        def norm_ple(t, end):
            u_free[t] = last_f1
            xs_m[t] = norm(t, H[:, t, :], GB[:, :], gbp_ready, h_done[t])

        for c in range(8):
            s1, s2a, s2b = S_ff[c]
            if c == 0:
                first_half_first(s1, {2: lambda: to_u(6, xs_m[6], u_free[6]), 5: lambda: to_u(7, xs_m[7], u_free[7])},
                                 squared_relu)
            else:
                for j0 in (0, 2):
                    bs = banks(4)
                    gr = [(j, hf) for j in (j0, j0 + 1) for hf in range(2)]
                    ends = products([by_columns(s1, j, hf, bs[n]) for n, (j, hf) in enumerate(gr)], range(8), "kout",
                                    release=[s1] if j0 else ())
                    last_f1 = ends[-1]
                    for n, (j, hf) in enumerate(gr):
                        squared_relu(j, hf, bs[n], ends[n])
            if c == 0:
                gbp_ready = dma(GB[:, :], row("g_ple"), g_ds, xs_m[7])
            for cc, s2 in ((0, s2a), (1, s2b)):
                for t0 in (0, 4):
                    bs = banks(4)
                    op = lambda t, b: by_tokens(s2, t, b, hi=HH, lo=HL, ready=lambda k, t: hid_ready[k, t // 4])
                    rel = [s2] if t0 else ()
                    if c == 7 and cc == 1:
                        for n in range(4):
                            t = t0 + n
                            end, = products([op(t, bs[n])], range(4), "seq", release=rel if t == NT - 1 else ())
                            h_done[t] = add_to_h(t, cc, bs[n], end, h_done[t])
                            if t >= 2:
                                to_u(t - 2, xs_m[t - 2], u_free[t - 2])
                            norm_ple(t, end)
                    else:
                        ends = products([op(t0 + n, bs[n]) for n in range(4)], range(4), "kout", release=rel)
                        for n in range(4):
                            h_done[t0 + n] = add_to_h(t0 + n, cc, bs[n], ends[n], h_done[t0 + n])
                    end = (pe.sem, pe.count)
            hid_free[0] = end
        ff_end = (pe.sem, pe.count)

        PTH, PTL = (at(f"PLE{n}", OX + 8 * K * i, [P, 2, D], F32R) for i, n in enumerate("HL"))
        PP = at("PP", OX + 16 * K, [P, NT, D])
        pt_done = {}
        for j in range(2):
            for hf in range(2):
                b, = banks(1)
                pe.wait(freed[b], p_in)
                for n in range(4):
                    pt_end = pe.do(lambda e, n=n, b=b, j=j, hf=hf: e.transpose(
                        PS[:, b, P * n:P * n + P], PST[:, 4 * hf + n, P * j:P * j + P], ident), signal=(n == 3))
                d = slice(512 * hf, 512 * hf + 512)
                a = act.do(lambda e, b=b, j=j, d=d: e.activation(PTH[:, j, d], bank(b), ACT.Copy), pt_end, ff_end)
                freed[b] = pt_done[j, hf] = dve.do(lambda e, b=b, j=j, d=d: e.tensor_tensor(
                    PTL[:, j, d], bank(b), PTH[:, j, d].bitcast(F32), ALU.subtract), a, ff_end)
        pp_done = {}
        for c in range(2):
            for t0 in (0, 4):
                bs = banks(4)
                ends = products([by_tokens(S_pp[c], t0 + n, bs[n], hi=PTH, lo=PTL,
                                           ready=lambda k, t: pt_done[k, t // 4]) for n in range(4)], range(2), "kout",
                                release=[S_pp[c]] if t0 else ())
                for n in range(4):
                    freed[bs[n]] = pp_done[t0 + n, c] = act.do(lambda e, t=t0 + n, c=c, b=bs[n]: e.activation(
                        PP[:, t, 512 * c:512 * c + 512], bank(b), ACT.Copy), ends[n], ff_end, pt_end, r_read)
            if c == 0:
                to_u(6, xs_m[6], u_free[6])
                to_u(7, xs_m[7], u_free[7])
        proj_end = (pe.sem, pe.count)
        SG = [at(f"SG{i}", OX + 2048 * i, [P, 512]) for i in range(4)]
        GB2 = at("GB2", OX + 8 * K, [P, D])
        gbf_ready = dma(GB[:, :], row("g_final"), g_ds, xs_m[7])
        gb2_ready = dma(GB2[:, :], row("norm_w_2"), dsem("gain2"), proj_end)
        sg_read, n_sg = [proj_end] * 4, [0]
        h2_ds = [dsem(f"h2_{t}") for t in range(NT)]
        h2_stored, h_read = {}, {}

        def ple(t, c, b, end):
            i = n_sg[0] % 4
            n_sg[0] += 1
            s, d = SG[i][:, :], slice(512 * c, 512 * c + 512)
            freed[b] = m = act.do(lambda e: e.activation(s, bank(b), ACT.Sigmoid), end, sg_read[i])
            m = pool.do(lambda e: e.tensor_tensor(s, s, PP[:, t, d], ALU.mult), m, pp_done[t, c])
            h_done[t] = sg_read[i] = dve.do(lambda e: e.tensor_tensor(H[:, t, d], H[:, t, d], s, ALU.add), m, h_done[t])

        def finish_first(t):
            i = t % 2
            a, r = rstd(t, H[:, t, :], XS[i][:, :], xs_read[i], h_done[t])
            m = dve.do(lambda e: e.scalar_tensor_tensor(out=H[:, t, :], in0=H[:, t, :], scalar=rst[:, t:t + 1],
                                                        in1=GB[:, :], op0=ALU.mult, op1=ALU.mult), r, a, gbf_ready)
            h2_stored[t] = dma(h2_d[:, t, :], H[:, t, :], h2_ds[t], m)
            xs_m[t] = norm(t, H[:, t, :], GB2[:, :], gb2_ready, m)
            h_read[t] = xs_m[t]

        for c in range(2):
            for t0 in (0, 4):
                bs = banks(4)
                for n in range(4):
                    t = t0 + n
                    end, = products([by_tokens(S_pg[c], t, bs[n])], range(8), "seq",
                                    release=[S_pg[c]] if t == NT - 1 else ())
                    u_free[t] = end
                    ple(t, c, bs[n], end)
                    if c:
                        if t >= 2:
                            to_u(t - 2, xs_m[t - 2], u_free[t - 2])
                        finish_first(t)
        ple_end = [(pool.sem, pool.count), h_done[NT - 1]]

        YH = [at(f"YH{i}", (OH, OX)[i], [P, 4, D], F32R) for i in range(2)]
        YL = [at(f"YL{i}", (OH, OX)[i] + 16 * K, [P, 4, D], F32R) for i in range(2)]
        YF = [at(f"YF{i}", (OH, OX)[i] + 16 * K, [P, 4, D]) for i in range(2)]
        PLH, PLL = (at(f"PL{n}", OX + 32 * K + 8 * K * i, [P, 2, D], F32R) for i, n in enumerate("HL"))
        W0, W1 = (at(f"WN{i}", OX + 48 * K + 4160 * i, [P, 1040]) for i in range(2))
        h_free = [h2_stored[t] for t in range(NT)] + [h_read[7]]
        pl_ready, pl_free = {}, [None]
        w_free = [None]
        y_done = {}
        silu_done = {}

        class Pads:
            done = None

        def pooled(g, j, bs, ends):
            w = 2 << g
            if Pads.done is None:
                z = [dve.do(lambda e, v=v: e.memset(v[:, 0:16], 0.0), xs_read) for v in (W0, W1)]
                Pads.done = z
            u = PS[:, bs[0]:bs[0] + 2, :].rearrange("p b c -> p (b c)")
            m = act.do(lambda e: e.activation(W0[:, 16:1040], u, ACT.Copy), ends, w_free, Pads.done, xs_read)
            src, dst = W0, W1
            s = 1
            while s < w:
                q = pool if s in (2, 8) else dve
                m = q.do(lambda e, src=src, dst=dst, s=s: e.tensor_tensor(dst[:, 16:1040], src[:, 16:1040],
                                                                          src[:, 16 - s:1040 - s], ALU.add), m, Pads.done, w_free, xs_read)
                src, dst = dst, src
                s *= 2
            m1 = dve.do(lambda e: e.scalar_tensor_tensor(out=dst[:, 32:1040], in0=src[:, 32:1040], scalar=1.0 / w,
                                                         in1=u[:, 16:1024], op0=ALU.mult, op1=ALU.subtract), m)
            m2 = dve.do(lambda e: e.tensor_tensor(dst[:, 16:32], src[:, 16:32], INV[:, g, :], ALU.mult), m, sc_ready)
            m2 = dve.do(lambda e: e.tensor_tensor(dst[:, 16:32], dst[:, 16:32], u[:, 0:16], ALU.subtract), m2)
            freed[bs[0]] = freed[bs[1]] = m2
            a = act.do(lambda e: e.activation(PLH[:, j, :], dst[:, 16:1040], ACT.Copy), m1, m2, pl_free, ple_end, sg_read)
            pl_ready[j] = w_free[0] = dve.do(lambda e: e.tensor_tensor(PLL[:, j, :], dst[:, 16:1040],
                                                                       PLH[:, j, :].bitcast(F32), ALU.subtract), a, pl_free)

        def silu(g, j, hf, b, end):
            tile = 2 * g + j
            z = YF[tile // 4][:, tile % 4, 512 * hf:512 * hf + 512]
            m = act.do(lambda e: e.activation(z, bank(b), ACT.Sigmoid), end, h_free, ple_end, proj_end)
            freed[b] = silu_done[tile, hf] = dve.do(lambda e: e.scalar_tensor_tensor(
                out=z, in0=bank(b), scalar=psc[:, tile:tile + 1], in1=z, op0=ALU.mult, op1=ALU.mult), m, sc_ready)

        def mixed(g, j, hf, b, end):
            tile = 2 * g + j
            d = slice(512 * hf, 512 * hf + 512)
            q, i = tile // 4, tile % 4
            y, yh, yl = YF[q][:, i, d], YH[q][:, i, d], YL[q][:, i, d]
            freed[b] = m = dve.do(lambda e: e.scalar_tensor_tensor(out=y, in0=bank(b), scalar=pgb[:, tile:tile + 1], in1=y,
                                                                   op0=ALU.add, op1=ALU.mult), end, silu_done[tile, hf])
            a = act.do(lambda e: e.activation(yh, y, ACT.Copy), m, h_free, ple_end)
            y_done[tile, hf] = dve.do(lambda e: e.tensor_tensor(yl, y, yh.bitcast(F32), ALU.subtract), a)

        for g in range(4):
            su, sg, sw = S_pi[g]
            gr = [(j, hf) for j in range(2) for hf in range(2)]
            if g == 0:
                bu, bs = (0, 1, 2, 3), (4, 5, 6, 7)
                turn[0] = 4
                eu, eg = {}, {}
                for hf in range(2):
                    between = None if hf else {3: lambda: to_u(6, xs_m[6], u_free[6]), 6: lambda: to_u(7, xs_m[7], u_free[7])}
                    held[:] = bu
                    eu[0, hf], eu[1, hf] = products([by_columns(su, j, hf, bu[2 * j + hf]) for j in range(2)], range(8),
                                                    "kout", release=[su] if hf else (), between=between)
                    held.clear()
                    eg[0, hf], eg[1, hf] = products([by_columns(sg, j, hf, bs[2 * j + hf]) for j in range(2)], range(8),
                                                    "kout", release=[sg] if hf else ())
                turn[0] = 0
                for j in range(2):
                    pooled(g, j, bu[2 * j:2 * j + 2], [eu[j, 0], eu[j, 1]])
                ends = [eg[x] for x in gr]
            else:
                bu = banks(4)
                ends = products([by_columns(su, j, hf, bu[2 * j + hf]) for j, hf in gr], range(8), "kout", release=[su])
                for j in range(2):
                    pooled(g, j, bu[2 * j:2 * j + 2], ends[2 * j:2 * j + 2])
                bs = banks(4)
                ends = products([by_columns(sg, j, hf, bs[n]) for n, (j, hf) in enumerate(gr)], range(8), "kout", release=[sg])
            u_end = ends[-1]
            for n, (j, hf) in enumerate(gr):
                silu(g, j, hf, bs[n], ends[n])
            bs = banks(4)
            ends = products([by_columns(sw, j, hf, bs[n], PLH, PLL, lambda k, hf: pl_ready[k]) for n, (j, hf) in enumerate(gr)],
                            range(2), "kout", release=[sw])
            pl_free[0] = ends[-1]
            for n, (j, hf) in enumerate(gr):
                mixed(g, j, hf, bs[n], ends[n])

        H2 = at("H2", OU, [P, NT, D])
        RES = [at(f"RES{i}", OU + 32 * K + 4096 * i, [P, D]) for i in range(4)]
        gbo_ready = dma(GB[:, :], row("final_norm_w_2"), g_ds, h_read[7])
        for t in range(NT):
            h_done[t] = dma(H2[:, t, :], h2_d[:, t, :], h2_ds[t], u_end)
        out_ds = [dsem(f"out{i}") for i in range(4)]
        out_done = [u_end] * 4

        def last_norm(t):
            i = t % 4
            a, r = rstd(t, H2[:, t, :], RES[i][:, :], h_done[t], out_done[i], u_end)
            m = dve.do(lambda e: e.scalar_tensor_tensor(out=RES[i][:, :], in0=H2[:, t, :], scalar=rst[:, t:t + 1],
                                                        in1=GB[:, :], op0=ALU.mult, op1=ALU.mult), r, a, gbo_ready)
            out_done[i] = dma(out_v[:, t, :], RES[i][:, :], out_ds[i], m)

        for c in range(2):
            for t0 in (0, 4):
                bs = banks(4)
                d = slice(512 * c, 512 * c + 512)

                class Both:
                    def __init__(self, slab, t, b):
                        self.slab, self.t, self.b = slab, t, b

                    def __call__(self, k):
                        s = slice(P * self.t, P * self.t + P)
                        return (YH[k // 4][:, k % 4, s], YL[k // 4][:, k % 4, s]), self.slab.at(k, 0, 512), \
                            [split_done[self.slab.load_of(k)], y_done[k, self.t // 4]]

                order = "kout" if (c, t0) == (0, 0) else "seq"
                gs = [(bank(bs[n]), bs[n], Both(S_po[c], t0 + n, bs[n])) for n in range(4)]
                if order == "kout":
                    ends = products(gs, range(8), "kout")
                for n in range(4):
                    t = t0 + n
                    if order == "seq":
                        end, = products([gs[n]], range(8), "seq", release=[S_po[c]] if t == NT - 1 else ())
                    else:
                        end = ends[n]
                    freed[bs[n]] = h_done[t] = dve.do(lambda e, t=t, b=bs[n], d=d: e.tensor_tensor(
                        H2[:, t, d], bank(b), H2[:, t, d], ALU.add), end, h_done[t])
                    if c:
                        last_norm(t)
        sp.wait(*out_done)

        block = ctx.enter_context(nc.Block())

        @block.sync
        def _(eng):
            sp.run(eng)

        @block.tensor
        def _(eng):
            pe.run(eng)

        @block.scalar
        def _(eng):
            act.run(eng)

        @block.vector
        def _(eng):
            dve.run(eng)

        @block.gpsimd
        def _(eng):
            pool.run(eng)


_INS = ["x", "p", "g_mix", "w_in", "b_forget", "swa_sinks", "w_br_swa", "w_br_fox", "w_mix_out", "g_mlp", "w_ff1",
        "w_ff2", "g_ple", "w_ple_gate", "w_ple_proj", "g_final", "norm_w_2", "pool_in_w_2", "pool_group_w_2",
        "pool_group_b_2", "pool_scale_2", "pool_out_w_2", "final_norm_w_2"]


def constants():
    i = np.arange(P)
    mats = np.zeros((4, P, P), np.float32)
    mats[0] = np.eye(P)
    mats[1] = np.where(i[None, :] <= i[:, None], 0.0, -FAR)
    mats[2] = i[:, None] <= i[None, :]
    mats[3] = 1.0
    q, s = i[:, None] + P, np.arange(2 * P)[None, :]
    ahead = q // 64 - s // 64
    seen = (ahead >= 0) & (ahead <= 2)
    slopes = 2.0 ** -(np.arange(8) + 1.0)
    bias = np.where(seen[:, None, :], -slopes[None, :, None] * np.abs(q - s)[:, None, :], -FAR)
    inv = np.zeros((P, 4, 16), np.float32)
    for g in range(4):
        inv[:, g, :] = 1.0 / np.minimum(np.arange(16) + 1, 2 << g)
    return {"c_mats": mats, "c_bias": bias.astype(np.float32), "c_inv": inv}


def kernel(**inputs):
    import concourse.bacc as _bacc
    from concourse.bass_utils import run_bass_kernel_spmd as _run

    nc = _bacc.Bacc("TRN2", target_bir_lowering=False, num_devices=1)
    arrays, args = {}, {}
    for name in _INS:
        a = np.asarray(inputs[name])
        if name in ("pool_group_b_2", "pool_scale_2"):
            a = a.reshape(NT, P).T
        arrays[f"in_{name}"] = np.ascontiguousarray(a)
    for name, a in constants().items():
        arrays[f"in_{name}"] = a
    for key, a in arrays.items():
        args[key[3:]] = nc.dram_tensor(key, a.shape, mybir.dt.from_np(a.dtype), kind="ExternalInput").ap()
    out = nc.dram_tensor("out_0", (1, 1024, D), F32, kind="ExternalOutput").ap()
    build(nc, args, out)
    r = _run(nc, [arrays], core_ids=[0])
    return r.results[0]["out_0"]
```

```python
from contextlib import ExitStack

import numpy as np

import concourse.bass as bass
from concourse import mybir

F32 = mybir.dt.float32
F32R = mybir.dt.float32r
ALU = mybir.AluOpType
ACT = mybir.ActivationFunctionType
AX_X = mybir.AxisListType.X

P = 128
D = 1024
NT = 8
EPS = 1e-6
FAR = 1e38


class Queue:

    def __init__(self, sem):
        self.sem, self.count, self.ops, self.met = sem, 0, [], {}

    def wait(self, *marks):
        for m in marks:
            if m is None:
                continue
            if isinstance(m, list):
                self.wait(*m)
            elif self.met.get(id(m[0]), 0) < m[1]:
                self.met[id(m[0])] = m[1]
                self.ops.append((None, m[0], m[1]))

    def do(self, fn, *marks, signal=True):
        self.wait(*marks)
        if not signal:
            self.ops.append((fn, None, 0))
            return None
        self.count += 1
        self.ops.append((fn, self.sem, 1))
        return (self.sem, self.count)

    def run(self, eng):
        for fn, sem, n in self.ops:
            if fn is None:
                eng.wait_ge(sem, n)
            elif sem is None:
                fn(eng)
            else:
                fn(eng).then_inc(sem, n)


class DmaSem:
    def __init__(self, sem):
        self.sem, self.count = sem, 0


def build(nc, A, out):
    ctx = ExitStack()
    with ctx:
        def new_sem(name):
            return ctx.enter_context(nc.semaphore(name))

        SIZE = 212832
        arena = ctx.enter_context(nc.sbuf_tensor("arena", [P, SIZE // 4], F32))
        ARENA0 = (16481 + 31) // 32 * 32

        def at(name, off, shape, dt=F32):
            n = int(np.prod(shape[1:])) * 4
            assert off + n <= SIZE, (name, off, n)
            return nc.alloc_sbuf_tensor_at(name, list(shape), dt, offset=ARENA0 + off)

        K = 1024
        NRING = 6
        RHL = at("RHL", 0, [P, 2, NRING, 1024], F32R)[:, :, :, :]
        RH, RL = RHL[:, 0, :, :], RHL[:, 1, :, :]
        RAW = at("RAW", 24 * K, [P, NRING, 1024])
        o = 48 * K
        CST = at("CST", o, [P, 4, 128])
        o += 2048
        INV = at("INV", o, [P, 4, 16])
        o += 256
        SM = at("SM", o, [P, 256])
        o += 1024
        OGB = o
        GB = at("GB", o, [P, D])
        o += 4096
        OH = o
        H = at("H", OH, [P, NT, D])
        OU = OH + 32 * K
        UH = at("UH", OU, [P, NT, D], F32R)
        UL = at("UL", OU + 32 * K, [P, NT, D], F32R)
        OX = OU + 64 * K
        ident, causal, tri, ones = (CST[:, i, :] for i in range(4))

        PS = ctx.enter_context(nc.psum_tensor("PS", [P, 8, 512], F32))

        pe, act, dve, pool, sp = (Queue(new_sem(f"done_{n}")) for n in ("pe", "act", "dve", "pool", "sp"))

        def dma(dst, src, ds, *marks):
            sp.wait(*marks)
            ds.count += 16
            sp.ops.append((lambda e: e.dma_start(dst, src), ds.sem, 16))
            return (ds.sem, ds.count)

        def dsem(name):
            return DmaSem(new_sem(name))

        small_at = [0]

        def small(n):
            a = small_at[0]
            small_at[0] += n
            assert small_at[0] <= 256
            return SM[:, a:a + n]

        x_v = A["x"].rearrange("b (t p) d -> p (b t) d", p=P)
        p_v = A["p"].rearrange("l b (t p) d -> p (l b t) d", p=P)
        out_v = out.rearrange("b (t p) d -> p (b t) d", p=P)

        def mat(name):
            v = A[name]
            while len(v.shape) > 2:
                v = v.rearrange("a b c -> (a b) c") if len(v.shape) == 3 else v.rearrange("a b c d -> (a b) c d")
            return v

        w_in, w_sa, w_fx, w_mix = mat("w_in"), mat("w_br_swa"), mat("w_br_fox"), mat("w_mix_out")
        w_f1, w_f2, w_pg, w_pp = mat("w_ff1"), mat("w_ff2"), mat("w_ple_gate"), mat("w_ple_proj")
        w_pi, w_gr, w_po = mat("pool_in_w_2"), mat("pool_group_w_2"), mat("pool_out_w_2")

        def row(name):
            v = A[name]
            if len(v.shape) == 2:
                v = v.rearrange("a b -> (a b)")
            return v.partition_broadcast(P)

        gates_d = nc.dram_tensor("gates_scratch", [16, P, D], F32, kind="Internal").ap()
        h2_d = nc.dram_tensor("h2_scratch", [P, NT, D], F32, kind="Internal").ap()

        loads = []

        def load(parts, n):
            loads.append((parts, n))
            return len(loads) - 1

        def load_k2(w, r0, c0):
            src = w[r0:r0 + 256, c0:c0 + 512].rearrange("(k p) c -> p k c", p=P)
            return load([(lambda s: s.rearrange("p (k c) -> p k c", k=2), src)], 1024)

        def load_k4(w, r0, nk, c0):
            src = w[r0:r0 + nk * P, c0:c0 + 256].rearrange("(k p) c -> p k c", p=P)
            return load([(lambda s: s[:, 0:nk * 256].rearrange("p (k c) -> p k c", k=nk), src)], nk * 256)

        class Slab:

            def __init__(self, idx, per, width):
                self.idx, self.per, self.width = idx, per, width
                self.last = per * len(idx) - 1

            def load_of(self, k):
                return self.idx[k // self.per]

            def at(self, k, c0, c1):
                need(self.load_of(min(k + 2, self.last)))
                s = self.load_of(k) % NRING
                a = (k % self.per) * self.width
                return RH[:, s, a + c0:a + c1], RL[:, s, a + c0:a + c1]

        def slab512(w, r0, c0, nk=8):
            return Slab([load_k2(w, r0 + 256 * j, c0) for j in range(nk // 2)], 2, 512)

        def slab256(w, r0, c0, nk=8):
            step = min(nk, 4)
            return Slab([load_k4(w, r0 + P * step * j, step, c0) for j in range(nk // step)], step, 256)

        def slab_misc():
            idx = []
            for k0 in (0, 3, 6):
                nk = min(3, 8 - k0)
                rows = slice(k0 * P, (k0 + nk) * P)
                idx.append(load([
                    (lambda s, nk=nk: s[:, 0:nk * 264].rearrange("p (k c) -> p k c", k=nk)[:, :, 0:256],
                     w_in[rows, 512:768].rearrange("(k p) c -> p k c", p=P)),
                    (lambda s, nk=nk: s[:, 0:nk * 264].rearrange("p (k c) -> p k c", k=nk)[:, :, 256:264],
                     w_in[rows, 2304:2312].rearrange("(k p) c -> p k c", p=P))], nk * 264))
            return Slab(idx, 3, 264)

        S_qa = slab512(w_in, 0, 0)
        S_ms = slab_misc()
        S_qb = slab512(w_in, 0, 768)
        S_kb = slab512(w_in, 0, 1280)
        S_gt = [slab512(w_in, 0, 2312 + 512 * j) for j in range(4)]
        S_vb = slab512(w_in, 0, 1792)
        S_y = [(slab512(w_fx, 0, 512 * j, 4), slab512(w_sa, 0, 512 * j, 4)) for j in range(2)]
        S_mx = [slab512(w_mix, 0, 512 * j) for j in range(2)]
        S_ff = []
        for c in range(8):
            S_ff.append((slab512(w_f1, 0, 512 * c), slab512(w_f2, 512 * c, 0, 4), slab512(w_f2, 512 * c, 512, 4)))
        S_pg, S_pp = [], []
        for c in range(2):
            S_pg.append(slab512(w_pg, 0, 512 * c))
            S_pp.append(slab512(w_pp, 0, 512 * c, 2))
        S_pi = []
        for g in range(4):
            S_pi.append((slab256(w_pi, 0, 256 * g), slab256(w_pi, 0, D + 256 * g), slab256(w_gr, 256 * g, 0, 2)))
        S_po = [slab512(w_po, 0, 512 * j) for j in range(2)]

        raw_ds = [dsem(f"raw{i}") for i in range(NRING)]
        landed, split_done = {}, {}
        to_split = []

        def fetch(i, released=None):
            if i >= len(loads):
                return
            for view, src in loads[i][0]:
                landed[i] = dma(view(RAW[:, i % NRING, :]), src, raw_ds[i % NRING], released)
            to_split.append(i)

        def split(i):
            n, s = loads[i][1], i % NRING
            m = act.do(lambda e: e.activation(RH[:, s, 0:n], RAW[:, s, 0:n], ACT.Copy), landed[i])
            split_done[i] = dve.do(lambda e: e.tensor_tensor(RL[:, s, 0:n], RAW[:, s, 0:n], RH[:, s, 0:n].bitcast(F32),
                                                             ALU.subtract), m)

        def split_all_but(n):
            while len(to_split) > n:
                split(to_split.pop(0))

        def need(i):
            while to_split and to_split[0] <= i:
                split(to_split.pop(0))

        freed = [None] * 8
        turn, held = [0], []

        def banks(n):
            got = []
            while len(got) < n:
                if turn[0] not in held:
                    got.append(turn[0])
                turn[0] = (turn[0] + 1) % 8
            return got

        def products(groups, ks, order="kout", release=(), between=None):
            if order == "seq" and not release:
                split_all_but(0)
            last_use = {}
            steps = [(k, g) for k in ks for g in range(len(groups))] if order == "kout" else \
                [(k, g) for g in range(len(groups)) for k in ks]
            for n, (k, g) in enumerate(steps):
                last_use[k] = n
            ends = [None] * len(groups)
            of_load = {}
            for slab in release:
                for k in ks:
                    ld = slab.load_of(k)
                    of_load[ld] = max(of_load.get(ld, 0), last_use[k])
            for n, (k, g) in enumerate(steps):
                o_ap, b, operands = groups[g]
                (sh, sl), (mh, ml), marks = operands(k)
                first, last = k == ks[0], k == ks[-1]
                if first:
                    pe.wait(freed[b])
                pe.wait(marks)
                pe.do(lambda e, o_ap=o_ap, sh=sh, mh=mh, first=first: e.matmul(o_ap, sh, mh, start=first, stop=False),
                      signal=False)
                pe.do(lambda e, o_ap=o_ap, sh=sh, ml=ml: e.matmul(o_ap, sh, ml, start=False, stop=False), signal=False)
                out_of = [ld for ld, m in of_load.items() if m == n]
                mark = pe.do(lambda e, o_ap=o_ap, sl=sl, mh=mh, last=last:
                             e.matmul(o_ap, sl, mh, start=False, stop=last), signal=last or bool(out_of))
                if last:
                    ends[g] = mark
                for ld in sorted(out_of):
                    fetch(ld + NRING, mark)
                    if order == "kout":
                        split_all_but(2)
                if between and k in between and g == len(groups) - 1:
                    between[k]()
            return ends

        def bank(b, n=512):
            return PS[:, b, 0:n]

        u_ready = [None] * NT

        def by_columns(slab, j, half, b, hi=None, lo=None, ready=None, cols=(0, 512)):
            hi, lo, ready = hi or UH, lo or UL, ready or u_ready
            t0, t1 = 512 * half + cols[0], 512 * half + cols[1]

            def operands(k):
                r = ready(k, half) if callable(ready) else ready[t0 // P:t1 // P]
                return slab.at(k, 128 * j, 128 * j + 128), (hi[:, k, t0:t1], lo[:, k, t0:t1]), \
                    [split_done[slab.load_of(k)], r]
            return (PS[:, b, cols[0]:cols[1]], b, operands)

        def by_tokens(slab, t, b, c0=0, c1=512, hi=None, lo=None, ready=None, o_ap=None):
            hi, lo = hi or UH, lo or UL

            def operands(k):
                r = ready(k, t) if callable(ready) else (ready or u_ready)[t]
                return (hi[:, k, P * t:P * t + P], lo[:, k, P * t:P * t + P]), slab.at(k, c0, c1), \
                    [split_done[slab.load_of(k)], r]
            return (bank(b, c1 - c0) if o_ap is None else o_ap, b, operands)

        ssq, rms, rst, mhalf = small(NT), small(NT), small(NT), small(1)
        mhalf_done = pool.do(lambda e: e.memset(mhalf, -0.5))
        XS = [at(f"XT{i}", OX + 4096 * i, [P, D]) for i in range(NT)]
        xs_read, xs_m = [None] * NT, {}
        summed = {}

        def sum_squares(t, src, junk, *marks):
            if junk is None:
                junk = XS[t % len(XS)][:, :]
                marks += (xs_read[t % len(XS)],)
            a = act.do(lambda e: e.activation(junk, src, ACT.Square, accum_out=ssq[:, t:t + 1]), *marks)
            b = pool.do(lambda e: e.tensor_scalar(rms[:, t:t + 1], ssq[:, t:t + 1], 1.0 / D, EPS, ALU.mult, ALU.add), a)
            r = pool.do(lambda e: e.tensor_tensor(rst[:, t:t + 1], rms[:, t:t + 1], mhalf, ALU.pow), b, mhalf_done)
            summed[t] = [r, a]

        def scaled(t, dst, src, gain, *marks):
            return dve.do(lambda e: e.scalar_tensor_tensor(out=dst, in0=src, scalar=rst[:, t:t + 1], in1=gain,
                                                           op0=ALU.mult, op1=ALU.mult), summed[t], *marks)

        def norm(t, src, gain, *marks):
            xs_m[t] = scaled(t, XS[t % len(XS)][:, :], src, gain, xs_read[t % len(XS)], *marks)

        def to_u(t, *marks):
            i, xs_mark = t % len(XS), xs_m[t]
            xs = XS[i]
            for q in range(2):
                b, = banks(1)
                pe.wait(freed[b], xs_mark, c_ready)
                for k in range(4):
                    m = pe.do(lambda e, k=k, q=q, b=b: e.transpose(
                        PS[:, b, P * k:P * k + P], xs[:, P * (4 * q + k):P * (4 * q + k) + P], ident),
                              signal=(k == 3))
                xs_read[i] = m
                src = PS[:, b, :].rearrange("p (k c) -> p k c", k=4)
                hi, lo = (v[:, 4 * q:4 * q + 4, P * t:P * t + P] for v in (UH, UL))
                a = act.do(lambda e, src=src, hi=hi: e.activation(hi, src, ACT.Copy), m, *marks)
                freed[b] = u_ready[t] = dve.do(lambda e, src=src, hi=hi, lo=lo: e.tensor_tensor(
                    lo, src, hi.bitcast(F32), ALU.subtract), a, *marks)

        x_ds = [dsem(f"x{t}") for t in range(NT)]
        c_ds = dsem("consts")
        g_ds, sc_ds = dsem("gain"), dsem("small_consts")
        x_in = [dma(H[:, 0, :], x_v[:, 0, :], x_ds[0])]
        gb_ready = dma(GB[:, :], row("g_mix"), g_ds)
        x_in.append(dma(H[:, 1, :], x_v[:, 1, :], x_ds[1]))
        c_ready = dma(CST[:, :, :], A["c_mats"].rearrange("i p c -> p i c"), c_ds)
        fetch(0)
        x_in.append(dma(H[:, 2, :], x_v[:, 2, :], x_ds[2]))
        for i in range(1, 4):
            fetch(i)
            x_in.append(dma(H[:, 2 + i, :], x_v[:, 2 + i, :], x_ds[2 + i]))
        for t in (6, 7):
            x_in.append(dma(H[:, t, :], x_v[:, t, :], x_ds[t]))
        for i in range(4, NRING):
            fetch(i)
        bf, snk = small(8), small(8)
        pgb, psc = small(8), small(8)
        dma(INV[:, :, :], A["c_inv"], sc_ds)
        dma(bf, row("b_forget"), sc_ds)
        dma(snk, row("swa_sinks"), sc_ds)
        dma(pgb, A["pool_group_b_2"], sc_ds)
        sc_ready = dma(psc, A["pool_scale_2"], sc_ds)

        def first_sum(t):
            sum_squares(t, H[:, t, :], None, x_in[t])

        def first_norm(t):
            norm(t, H[:, t, :], GB[:, :], gb_ready)

        def first(what, t):
            return lambda: (first_sum, first_norm, to_u)["snu".index(what)](t)

        def in_turn(text):
            for v in text.split():
                first(v[0], int(v[1]))()

        in_turn("s0 n0 s1 n1 u0")
        need(0)
        in_turn("u1 s2 n2")

        VB = at("VB", OH, [P, 8, NT, P], F32R)
        KD = at("KD", OX, [P, 2, 2, D], F32R)
        VA = at("VA", OX + 16 * K, [P, NT, 2, P], F32R)
        QS = at("QS", OH, [P, 4, D], F32R)
        STG = [at(f"STG{i}", OX + 40 * K + 4096 * i, [P, 2, 512], F32R) for i in range(4)]
        GST = [at(f"GST{i}", OX + 32 * K + 2048 * i, [P, 512]) for i in range(2)]
        BIAS = at("BIAS", OX + 48 * K, [P, 8, 256])
        FT = at("FT", OX + 24 * K, [P, 6, 64])
        CT = at("CT", OX + 26 * K, [P, P])
        cn_d = nc.dram_tensor("cn_scratch", [64, P], F32, kind="Internal").ap()

        qa_d, qb_d, kb_d = (nc.dram_tensor(f"{n}_scratch", [4, 2, P, D], F32, kind="Internal").ap()
                            for n in ("qa", "qb", "kb"))
        stg_ds = [dsem(f"stg{i}") for i in range(4)]
        stg_out, n_stg = [None] * 4, [0]

        def spill(dst, scale, done):
            def evac(j, h, b, end):
                i = n_stg[0] % 4
                n_stg[0] += 1
                hi, lo = STG[i][:, 0, :], STG[i][:, 1, :]
                m = act.do(lambda e: e.activation(hi, bank(b), ACT.Copy, scale=scale), end, stg_out[i])
                freed[b] = m = dve.do(lambda e: e.scalar_tensor_tensor(
                    out=lo, in0=bank(b), scalar=scale, in1=hi.bitcast(F32), op0=ALU.mult, op1=ALU.subtract), m)
                done[j, h] = stg_out[i] = dma(
                    dst[j, :, :, 512 * h:512 * h + 512].rearrange("a p c -> p a c"), STG[i][:, :, :].bitcast(F32),
                    stg_ds[i], m)
            return evac

        def first_half_first(slab, between, evac):
            for hf in range(2):
                bs = banks(4)
                held[:] = bs
                ends = products([by_columns(slab, j, hf, bs[j]) for j in range(4)], range(8), "kout",
                                release=[slab] if hf else (), between=None if hf else between)
                held.clear()
                for j in range(4):
                    evac(j, hf, bs[j], ends[j])
                if not hf:
                    turn[0] = (bs[0] + 4) % 8

        def heads(slab, evac):
            for j0 in (0, 2):
                bs = banks(4)
                gr = [(j, h) for h in range(2) for j in (j0, j0 + 1)]
                ends = products([by_columns(slab, j, h, bs[n]) for n, (j, h) in enumerate(gr)], range(8), "kout",
                                release=[slab] if j0 else ())
                for n, (j, h) in enumerate(gr):
                    evac(j, h, bs[n], ends[n])

        qa_out, qb_out, kb_out = {}, {}, {}

        late = [{0: "s3 n3", 2: "s4 n4 u2", 4: "s5 n5", 5: "u3", 6: "s6 n6"}, {0: "s7 n7 u4", 2: "u5", 4: "u6", 6: "u7"}]
        qa_evac = spill(qa_d, 0.125, qa_out)
        bs = banks(4)
        held[:] = bs
        for q in range(2):
            ends = products([by_columns(S_qa, j, 0, bs[j], cols=(256 * q, 256 * q + 256)) for j in range(4)], range(8),
                            between={k: (lambda text=text: in_turn(text)) for k, text in late[q].items()})
        held.clear()
        for j in range(4):
            qa_evac(j, 0, bs[j], ends[j])
        turn[0] = (bs[0] + 4) % 8
        bs = banks(4)
        ends = products([by_columns(S_qa, j, 1, bs[j]) for j in range(4)], range(8), release=[S_qa])
        for j in range(4):
            qa_evac(j, 1, bs[j], ends[j])
        x_read = xs_m[NT - 1]

        F = small(64)
        F3 = F.rearrange("p (t h) -> p t h", t=NT)
        bs = banks(2)
        ends = products([by_columns(S_ms, 0, h, bs[h]) for h in range(2)], range(8))
        kd_done = []
        for h in range(2):
            sl = slice(512 * h, 512 * h + 512)
            b = bs[h]
            m = None
            for g in range(2):
                own = slice(64 * g, 64 * g + 64)
                for r in range(2):
                    to = slice(64 * r, 64 * r + 64)
                    m = act.do(lambda e, g=g, b=b, sl=sl, own=own, to=to: e.activation(
                        KD[to, g, 0, sl], PS[own, b, :], ACT.Copy), ends[h])
            for g in range(2):
                own = slice(64 * g, 64 * g + 64)
                for r in range(2):
                    to = slice(64 * r, 64 * r + 64)
                    d = dve.do(lambda e, g=g, b=b, sl=sl, own=own, to=to: e.tensor_tensor(
                        KD[to, g, 1, sl], PS[own, b, :], KD[own, g, 0, sl].bitcast(F32), ALU.subtract), m)
            freed[b] = d
            kd_done += [m, d]
        VL = [at(f"VL{i}", OX + 27 * K + 1024 * i, [P, 136]) for i in range(2)]
        VS = [at(f"VS{i}", OX + 29 * K + 1024 * i, [P, 136]) for i in range(2)]
        vl_added, vs_read = [None, None], [None, None]
        split_all_but(0)
        bs = banks(6)
        va_done, f_done = {}, {}
        for t in range(NT):
            b, i = bs[t % 6], t % 2
            pe.wait(freed[b], u_ready[t])
            for k in range(8):
                w_high, _ = S_ms.at(k, 128, 264)
                ld = S_ms.load_of(k)
                a = (k - 3 * (k // 3)) * 264 + 128
                w_both = RHL[:, :, ld % NRING, a:a + 136]
                tok = slice(P * t, P * t + P)
                pe.wait(split_done[ld])

                def high(k=k, b=b, w_both=w_both, tok=tok, **signal):
                    return pe.do(lambda e: e.matmul(PS[:, b, 0:272].rearrange("p (a c) -> p a c", a=2), UH[:, k, tok],
                                                    w_both, start=(k == 0), stop=(k == 7)), **signal)

                def low(k=k, b=b, w_high=w_high, tok=tok, **signal):
                    return pe.do(lambda e: e.matmul(PS[:, b, 0:136], UL[:, k, tok], w_high, start=False, stop=False),
                                 **signal)

                if k < 7:
                    high(signal=False)
                    end = low()
                else:
                    low(signal=False)
                    end = high()
                if t == NT - 1 and (k == 7 or S_ms.load_of(k + 1) != ld):
                    fetch(ld + NRING, end)
            vl, vs = VL[i], VS[i]
            m = act.do(lambda e, vl=vl, b=b: e.activation(vl[:, :], PS[:, b, 136:272], ACT.Copy), end, vl_added[i])
            freed[b] = vl_added[i] = m = dve.do(lambda e, vl=vl, vs=vs, b=b: e.tensor_tensor(
                vs[:, :], PS[:, b, 0:136], vl[:, :], ALU.add), m, vs_read[i])
            hi, lo = VA[:, t, :, 0:64], VA[:, t, :, 64:P]
            va = vs[:, 0:P].rearrange("p (g c) -> p g c", g=2)
            f_done[t] = dve.do(lambda e, t=t, vs=vs: e.tensor_tensor(F3[:, t, :], vs[:, P:P + 8], bf, ALU.add), m, sc_ready)
            m = act.do(lambda e, va=va, hi=hi: e.activation(hi, va, ACT.Copy), m)
            vs_read[i] = va_done[t] = dve.do(lambda e, va=va, hi=hi, lo=lo: e.tensor_tensor(
                lo, va, hi.bitcast(F32), ALU.subtract), m)

        C = small(64)
        C3 = C.rearrange("p (t h) -> p t h", t=NT)

        def forget_logs():
            fa, fe, fw, fl, fm, LF = (FT[:, i, :] for i in range(6))
            fd = [f_done[t] for t in range(NT)]
            m1 = dve.do(lambda e: e.tensor_scalar(fm, F, 0.0, None, ALU.min), fd)
            m2 = dve.do(lambda e: e.tensor_scalar(fa, F, -1.0, None, ALU.mult), fd)
            m2 = dve.do(lambda e: e.tensor_tensor(fa, F, fa, ALU.min), m2)
            m3 = act.do(lambda e: e.activation(fe, fa, ACT.Exp), m2)
            m4 = dve.do(lambda e: e.tensor_scalar(fw, fe, 1.0, None, ALU.add), m3)
            m5 = act.do(lambda e: e.activation(fl, fw, ACT.Ln), m4)
            m6 = dve.do(lambda e: e.tensor_scalar(fa, fw, -1.0, None, ALU.add), m4, m3)
            m6 = dve.do(lambda e: e.tensor_tensor(fa, fe, fa, ALU.subtract), m6)
            m7 = dve.do(lambda e: e.reciprocal(fw, fw), m5, m6)
            m7 = dve.do(lambda e: e.tensor_tensor(fa, fa, fw, ALU.mult), m7)
            m7 = dve.do(lambda e: e.tensor_tensor(fl, fl, fa, ALU.add), m7)
            lf_done = dve.do(lambda e: e.tensor_tensor(LF, fm, fl, ALU.subtract), m7, m1)
            return LF.rearrange("p (t h) -> p t h", t=NT), lf_done

        def forget_sums(LF3, lf_done):
            b, = banks(1)
            pe.wait(freed[b], lf_done, c_ready)
            LF = LF3.rearrange("p t h -> p (t h)")
            pe.do(lambda e, b=b: e.matmul(PS[:, b, 0:64], tri, LF, start=True, stop=False), signal=False)
            for j in range(1, NT):
                m = pe.do(lambda e, j=j, b=b: e.matmul(PS[:, b, 8 * j:64], ones, LF[:, 0:64 - 8 * j], start=False,
                                                       stop=(j == NT - 1)), signal=(j == NT - 1))
            freed[b] = got = dve.do(lambda e, b=b: e.tensor_copy(C, PS[:, b, 0:64]), m)
            b, = banks(1)
            pe.wait(freed[b], got, c_ready)
            m = pe.do(lambda e, b=b: e.transpose(PS[0:64, b, 0:P], C, ident))
            freed[b] = m = act.do(lambda e, b=b: e.activation(CT[0:64, :], PS[0:64, b, 0:P], ACT.Copy, scale=-1.0), m)
            return got, dma(cn_d, CT[0:64, :], dsem("cn"), m)

        logs = forget_logs()
        heads(S_qb, spill(qb_d, 0.125, qb_out))
        c_done, cn_out = forget_sums(*logs)
        heads(S_kb, spill(kb_d, 1.0, kb_out))
        q_ds = [dsem("q_ab0"), dsem("q_ab1"), dsem("k_ab0"), dsem("k_ab1")]

        def stack(dst, src, j, r, ds, *marks):
            own = slice(64 * r, 64 * r + 64)
            dma(dst[0:64, :].bitcast(F32), src[j, 0, own, :], ds, *marks)
            return dma(dst[64:P, :].bitcast(F32), src[j, 1, own, :], ds, *marks)

        def out_of(done, j):
            return [done[j, 0], done[j, 1]]

        qs_ready = [None, None]

        def load_qs(g, *marks):
            for a in range(4):
                j = 2 * g + a // 2
                qs_ready[g] = stack(QS[:, a, :], qa_d, j, a % 2, q_ds[g], out_of(qa_out, j), *marks)

        load_qs(0, x_read)
        bias_ready = dma(BIAS[:, :, :], A["c_bias"], dsem("bias"), stg_out)

        T = [at(f"T{i}", OH + (16 + 4 * i) * K, [P, D]) for i in range(2)]
        PRH, PRL = (at(f"PR{n}", OH + (24 + 4 * i) * K, [P, 2, 512], F32R) for i, n in enumerate("HL"))
        OA = [at("OA0", OX + 24 * K, [P, 2, D]), at("OA1", OX + 40 * K, [P, 2, D])]
        TMP = [at(f"TMP{i}", OGB + 2048 * i, [P, 512]) for i in range(2)]
        oa_free = [[c_done, cn_out], stg_out]
        tmp_read = [x_read, x_read]
        n_ev = [0]

        def transposes(b, blocks, *ready):
            pe.wait(freed[b], *ready)
            for n, src in enumerate(blocks):
                m = pe.do(lambda e, n=n, src=src: e.transpose(PS[:, b, P * n:P * n + P], src, ident),
                          signal=(n == len(blocks) - 1))
            return m

        def high_part(b, dst, w, turned, *slot_free):
            return act.do(lambda e: e.activation(dst[:, 0:w], PS[:, b, 0:w], ACT.Copy), turned, *slot_free)

        def low_part(b, dst, hi, w, high):
            freed[b] = m = dve.do(lambda e: e.tensor_tensor(dst[:, 0:w], PS[:, b, 0:w], hi[:, 0:w].bitcast(F32),
                                                            ALU.subtract), high)
            return m

        class Sum:

            def __init__(self, b, even, odd, end):
                self.b, self.i, self.end = b, n_ev[0] % 2, end
                n_ev[0] += 1
                self.jobs = [j for j in ((slice(0, 64), slice(64, P), even), (slice(64, P), slice(0, 64), odd)) if j[2]]

            def act(self):
                b, i = self.b, self.i
                for own, other, (col, dst) in self.jobs:
                    self.copied = act.do(lambda e, own=own, other=other, col=col: e.activation(
                        col(TMP[i][own, :]), col(bank(b)[other, :]), ACT.Copy), self.end, tmp_read[i])

            def dve(self, *marks):
                b, i = self.b, self.i
                for own, other, (col, dst) in self.jobs:
                    d = dve.do(lambda e, own=own, col=col, dst=dst: e.tensor_tensor(
                        dst[own], col(bank(b)[own, :]), col(TMP[i][own, :]), ALU.add), self.copied, *marks)
                freed[b] = tmp_read[i] = d

        events = []

        def plan(when, fn, *args):
            events.append((when, len(events), fn, args))

        mx, nm, es, den = (F[:, 16 * i:16 * i + 16] for i in range(4))
        scored, windows = {}, []

        class Window:
            def __init__(self, i, g, n):
                self.i, self.g, self.n = i, g, n
                self.w = 256 if n else P
                self.q = slice(4 * (i % 4), 4 * (i % 4) + 4)
                self.tv = T[i % 2][:, :].rearrange("p (a c) -> p a c", a=4)[:, :, 0:self.w]
                self.tiles = (n - 1, n) if n else (n,)
                self.last = len(self.tiles) - 1
                self.summed, self.turned, self.high, self.low, self.valued = [], {}, {}, {}, {}
                self.t_before, self.pr_before = [windows[i - n] if i >= n else None for n in (2, 1)]
                windows.append(self)

            def scores(self, r):
                g, n, b = self.g, self.n, 4 + r
                s0 = P * self.tiles[0]
                pe.wait(freed[b], kd_done, qs_ready[g])
                for x in range(2):
                    for part in range(2):
                        self.end = pe.do(lambda e, a=2 * r + x, x=x, part=part: e.matmul(
                            PS[:, b, 256 * x:256 * x + 256], QS[:, a, P * n:P * n + P],
                            KD[:, g, part, s0:s0 + 256], start=(part == 0), stop=(part == 1)),
                                         signal=(x == 1 and part == 1))

            def bias(self, r):
                i, g, w, tv, b = self.i, self.g, self.w, self.tv, 4 + r
                t_free = self.t_before.turned[self.t_before.last] if self.t_before else None
                for x in range(2):
                    a = 2 * r + x
                    c = 4 * (i % 4) + a
                    self.top = freed[b] = scored[i] = dve.do(lambda e, a=a, x=x, c=c: e.tensor_tensor_reduce(
                        tv[:, a, :], PS[:, b, 256 * x:256 * x + w], BIAS[:, 4 * g + a, 256 - w:256],
                        1.0, -FAR, ALU.add, ALU.max, mx[:, c:c + 1]), self.end, bias_ready, t_free, x_read,
                                                             c_done)

            def maximum(self):
                sk, q = snk[:, 4 * self.g:4 * self.g + 4], self.q
                m = dve.do(lambda e: e.tensor_tensor(mx[:, q], mx[:, q], sk, ALU.max), self.top, sc_ready)
                self.shift = pool.do(lambda e: e.tensor_scalar(nm[:, q], mx[:, q], -1.0, None, ALU.mult), m)
                self.sink = pool.do(lambda e: e.tensor_tensor(es[:, q], sk, mx[:, q], ALU.subtract), m)

            def probs(self, r):
                tv, q = self.tv, self.q
                if r == 0:
                    self.summed.append(act.do(lambda e: e.activation(es[:, q], es[:, q], ACT.Exp), self.sink))
                for a in (2 * r, 2 * r + 1):
                    c = 4 * (self.i % 4) + a
                    m = act.do(lambda e, a=a, c=c: e.activation(tv[:, a, :], tv[:, a, :], ACT.Exp, bias=nm[:, c:c + 1],
                                                                accum_out=den[:, c:c + 1]), self.shift)
                self.summed.append(m)

            def inverse(self):
                q = self.q
                d = dve.do(lambda e: e.tensor_tensor(den[:, q], den[:, q], es[:, q], ALU.add), self.summed)
                self.rden = dve.do(lambda e: e.reciprocal(den[:, q], den[:, q]), d)

            def norm(self):
                tv, q, w = self.tv, self.q, self.w
                self.normed = pool.do(lambda e: e.tensor_tensor(tv, tv, den[:, q].unsqueeze(2).to_broadcast([P, 4, w]),
                                                                ALU.mult), self.rden, self.summed)

            def turn(self, k):
                self.turned[k] = transposes(6, [self.tv[:, a, P * k:P * k + P] for a in range(4)], self.normed)

            def split_high(self, k):
                before = self.pr_before
                slot_free = before.valued[min(k, before.last)] if before else x_read
                self.high[k] = high_part(6, PRH[:, k, :], 512, self.turned[k], slot_free)

            def split_low(self, k):
                self.low[k] = low_part(6, PRL[:, k, :], PRH[:, k, :], 512, self.high[k])

            def values(self, k):
                i, g, last, tile, b = self.i, self.g, self.last, self.tiles[k], 7
                if k == 0:
                    pe.wait(freed[b])
                pe.wait(self.low[k], va_done[tile])
                for part, pr in enumerate((PRH, PRL)):
                    m = pe.do(lambda e, pr=pr, part=part: e.matmul(
                        bank(b), VA[:, tile, g, :], pr[:, k, :], start=(k == 0 and part == 0),
                        stop=(k == last and part == 1)), signal=(part == 1))
                self.valued[k] = m
                if k == last:
                    dst = OA[g][:, :, P * self.n:P * self.n + P]
                    view = lambda r: (lambda v: v.rearrange("p (j r c) -> p j r c", j=2, r=2)[:, :, r, :])
                    self.sum = Sum(b, (view(0), dst), (view(1), dst), m)

            def schedule(self, at):
                for r in range(2):
                    plan(at, self.scores, r)
                    plan(at + 1, self.bias, r)
                    plan(at + 2 + r, self.probs, r)
                plan(at + 1, self.maximum)
                plan(at + 4, self.inverse)
                plan(at + 4, self.norm)
                for k in range(self.last + 1):
                    plan(at + 8.5 + 2.75 * k, self.turn, k)
                    plan(at + 8.5 + 2.75 * k, self.split_high, k)
                    plan(at + 8.5 + 2.75 * k, self.split_low, k)
                    plan(at + 10.5 + 2.5 * k, self.values, k)
                plan(at + 14.5, lambda: self.sum.act())
                plan(at + 14.5, lambda: self.sum.dve(oa_free[self.g]))
                if self.i == NT - 1:
                    plan(at + 2, lambda: load_qs(1, scored[self.i]))

        gst_ds = [dsem(f"gst{i}") for i in range(2)]
        gate_stored = {}
        stored = [None] * 2
        for g in range(2):
            for n in range(NT):
                Window(NT * g + n, g, n).schedule(10 + 6.75 * (NT * g + n) + 1.5 * g)
        events.sort(key=lambda v: v[:2])
        steps = [0]

        def due(until):
            while events and events[0][0] <= until:
                _, _, fn, args = events.pop(0)
                fn(*args)

        def step():
            due(steps[0])
            steps[0] += 1

        for s in range(4):
            for j in range(4):
                bs = [2 * (j % 2), 2 * (j % 2) + 1]
                ends = products([by_columns(S_gt[s], j, h, bs[h]) for h in range(2)], range(8), "kout",
                                release=[S_gt[s]] if j == 3 else (), between={k: step for k in range(8)})
                for h in range(2):
                    g = GST[h][:, :]
                    freed[bs[h]] = m = act.do(lambda e, g=g, b=bs[h]: e.activation(g, bank(b), ACT.Copy), ends[h], stored[h])
                    gate_stored[4 * s + j, h] = stored[h] = dma(gates_d[4 * s + j, :, 512 * h:512 * h + 512], g,
                                                                gst_ds[h], m)
        due(1000)
        window_end = [(pe.sem, pe.count), (dve.sem, dve.count)]

        QK = [(at(f"Q{n}", oq, [P, D], F32R), at(f"K{n}", ok, [P, 2, D], F32R)) for n, oq, ok in (
            ("E", OX + 32 * K, OU + 56 * K), ("O", OU, OU + 4 * K), ("F", OX + 4 * K, OX + 8 * K))]
        NC = [at(f"NC{n}", on, [P, D]) for n, on in (("E", OU + 36 * K), ("O", OX + 48 * K), ("F", OX + 52 * K))]
        BAND, EYE = at("BAND", OX + 36 * K, [P, 3 * P], F32R), at("EYE", OX + 38 * K, [P, P], F32R)
        for dst, src in ((EYE[:, :], ident), (BAND[:, P:2 * P], causal)):
            act.do(lambda e, dst=dst, src=src: e.activation(dst, src, ACT.Copy), c_ready)
        for k, v in ((0, 0.0), (2, -FAR)):
            band_done = act.do(lambda e, k=k, v=v: e.activation(BAND[:, P * k:P * k + P], causal, ACT.Copy,
                                                                 bias=v, scale=0.0), c_ready)
        nc_ds = [dsem(f"nc{i}") for i in range(3)]
        qk_ds = [dsem(f"qk{i}") for i in range(3)]
        nc_in, qk_ready = {}, {}
        nc_read, qk_read = [None, window_end, window_end], [[stored], None, window_end]
        cn_v = cn_d.rearrange("(t h) c -> h t c", h=8)

        def place(h):
            return h % 2 if h else 2

        def fox_load_qk(h):
            i, j, r = place(h), h // 2, h % 2
            own = slice(64 * r, 64 * r + 64)
            marks = out_of(qb_out, j) + out_of(kb_out, j) + [qk_read[i], rows_read,
                                                             forgets[0, 2].turned[2] if h == 2 else None]
            q, k = QK[i]
            stack(q, qb_d, j, r, qk_ds[i], marks)
            for part in range(2):
                for half in (slice(0, 64), slice(64, P)):
                    qk_ready[h] = dma(k[half, part, :].bitcast(F32), kb_d[j, part, own, :], qk_ds[i], marks)

        def fox_load_c(h):
            i = place(h)
            nc_in[h] = dma(NC[i].rearrange("p (t c) -> p t c", t=NT), cn_v[h].partition_broadcast(P),
                           nc_ds[i], cn_out, nc_read[i], rows_read)

        free_u = None
        rows_read = []
        fox_load_qk(0)
        fox_load_c(0)

        vb_done = {}
        OT = OU + 16 * K
        PFH, PFL = (at(f"PF{n}", OU + 40 * K + 8 * K * i, [P, 4, 512], F32R) for i, n in enumerate("HL"))
        n_turns, forgets, pf_valued = [0], {}, {}
        OB = at("OB", OX, [P, 4, D])
        ob_free = [window_end]
        FTILE = {(3, 0): 0, (3, 1): 4, (2, 0): 16, (2, 1): 8, (1, 0): 12, (1, 1): 14, (0, 0): 11, (0, 1): 19}
        TF = {k: at(f"TF{k[0]}{k[1]}", OT + v * K, [P, 256 * (k[0] + 1)]) for k, v in FTILE.items()}
        TF[5, 0], TF[5, 1] = (at(f"TF5{i}", OX + (16 + 4 * i) * K, [P, D]) for i in range(2))
        TF[6, 0], TF[6, 1] = (at(f"TF6{i}", OX + (0, 32 * K)[i], [P, 768]) for i in range(2))
        TF[4, 0], TF[4, 1] = (at(f"TF4{i}", (OX + 52 * K, OU + 12 * K)[i], [P, 768]) for i in range(2))
        fmx, fnm, fden = (small(8) for _ in range(3))

        class Forget:
            def __init__(self, i, h, u):
                self.i, self.h, self.u = i, h, u
                self.widths = (256 * u + P, 256 * u + 256)
                self.nb = 1 if u < 2 else 2
                self.slot = u + 2 if u == 3 and h % 2 == 0 or u == 2 and h % 2 else 6 if u == 2 and h == 0 else u
                self.tiles = [TF[self.slot, par][:, :] for par in range(2)]
                self.turns = list(range(n_turns[0], n_turns[0] + u + 1))
                n_turns[0] += u + 1
                self.turned, self.high, self.low = {}, {}, {}
                self.before = forgets.get((h - (2 if u >= 2 else 1), u))
                forgets[h, u] = self
                self.end, self.top, self.shift, self.summed, self.rden, self.normed = ([None, None] for _ in range(6))

            def cols(self, par):
                c = 2 * (self.i % 4)
                return slice(c + par, c + par + 1) if self.u == 3 else slice(c, c + 2)

            def scores(self, par):
                h, u, n, nb, x = self.h, self.u, max(self.widths[par], 256), self.nb, place(self.h)
                q, kk = QK[x]
                w = n // nb
                t, sb = 2 * u + par, 2 * par
                band = P if u == 0 and par == 0 else 0
                pe.wait(freed[sb], freed[sb + 1], qk_ready[h])
                for ch in range(nb):
                    for part in range(2):
                        pe.do(lambda e, ch=ch, part=part: e.matmul(
                            PS[:, sb + ch, 0:w], q[:, P * t:P * t + P], kk[:, part, w * ch:w * ch + w],
                            start=(part == 0), stop=(part == 1 and ch < nb - 1)), signal=False)
                self.end[par] = qk_read[x] = pe.do(lambda e: e.matmul(
                    PS[:, sb + nb - 1, w - 256:w], EYE[:, :], BAND[:, band:band + 256], start=False, stop=True),
                                                   band_done)

            def bias(self, par):
                u, n, nb, x, sb = self.u, self.widths[par], self.nb, place(self.h), 2 * par
                c = 2 * (self.i % 4) + par
                s = PS[:, sb:sb + nb, 0:n // nb]
                tv = self.tiles[par][:, 0:n].rearrange("p (b c) -> p b c", b=nb)
                kv = NC[x][:, 0:n].rearrange("p (b c) -> p b c", b=nb)
                if self.before:
                    t_free = self.before.turned[self.before.u]
                else:
                    t_free = [window_end, stored if self.slot == 6 else None, nc_read[2] if self.slot == 4 else None]
                self.top[par] = freed[sb] = freed[sb + 1] = nc_read[x] = dve.do(lambda e: e.tensor_tensor_reduce(
                    tv, s, kv, 1.0, -FAR, ALU.add, ALU.max, fmx[:, c:c + 1]), self.end[par], nc_in[self.h], t_free, free_u)

            def maximum(self, par):
                cc, t = self.cols(par), 2 * self.u
                cq = C3[:, t + par:t + par + 1, self.h] if self.u == 3 else C3[:, t:t + 2, self.h]
                m = pool.do(lambda e: e.tensor_tensor(fmx[:, cc], fmx[:, cc], cq, ALU.add), self.top, c_done)
                m = pool.do(lambda e: e.tensor_tensor(fnm[:, cc], cq, fmx[:, cc], ALU.subtract), m)
                self.shift = [m if x == par or self.u < 3 else self.shift[x] for x in range(2)]

            def probs(self, par):
                c, tv = 2 * (self.i % 4) + par, self.tiles[par][:, 0:self.widths[par]]
                self.summed[par] = act.do(lambda e: e.activation(tv, tv, ACT.Exp, bias=fnm[:, c:c + 1],
                                                                 accum_out=fden[:, c:c + 1]), self.shift[par])

            def inverse(self, par):
                cc = self.cols(par)
                m = dve.do(lambda e: e.reciprocal(fden[:, cc], fden[:, cc]), self.summed)
                self.rden = [m if x == par or self.u < 3 else self.rden[x] for x in range(2)]

            def norm(self, par):
                c, n = 2 * (self.i % 4) + par, self.widths[par]
                tv = self.tiles[par][:, 0:n]
                self.normed[par] = pool.do(lambda e: e.tensor_tensor(tv, tv, fden[:, c:c + 1].to_broadcast([P, n]),
                                                                     ALU.mult), self.rden[par], self.summed[par])

            def turn(self, k):
                self.turned[k] = transposes(
                    4 + self.turns[k] % 2,
                    [self.tiles[par][:, P * x:P * x + P] for x in (2 * k, 2 * k + 1) for par in range(2)], self.normed)

            def split_high(self, k):
                m = self.turns[k]
                self.high[k] = high_part(4 + m % 2, PFH[:, m % 4, :], 512, self.turned[k],
                                         pf_valued[m - 4] if m >= 4 else free_u)

            def split_low(self, k):
                m = self.turns[k]
                self.low[k] = low_part(4 + m % 2, PFL[:, m % 4, :], PFH[:, m % 4, :], 512, self.high[k])

            def values(self, k):
                h, u, b, slot = self.h, self.u, 6 + self.i % 2, self.turns[k] % 4
                if k == 0:
                    pe.wait(freed[b])
                last = 2 * u + 1
                for x in (2 * k, 2 * k + 1):
                    pe.wait(self.low[k], vb_done[x])
                    for part, pr in enumerate((PFH, PFL)):
                        m = pe.do(lambda e, x=x, pr=pr, part=part: e.matmul(
                            PS[:, b, 0:256], VB[:, h, x, :], pr[:, slot, 256 * (x % 2):256 * (x % 2) + 256],
                            start=(x == 0 and part == 0), stop=(x == last and part == 1)), signal=(part == 1))
                pf_valued[self.turns[k]] = m
                if k == u:
                    part = (lambda v: v[:, 0:256], OB[:, h // 2, 256 * u:256 * u + 256])
                    self.sum = Sum(b, None if h % 2 else part, part if h % 2 else None, m)
                    vb_read[h] = m

            def schedule(self, at):
                u = self.u
                score = ((1.75, 2.75), (1, 2.25), (1.25, 2), (2.25, 4))[u]
                for par in range(2):
                    top = at + (score[par] if u == 3 else score[1]) + 1.5
                    plan(at + score[par], self.scores, par)
                    plan(at + score[par] + 1.5, self.bias, par)
                    if u == 3 or par:
                        plan(top, self.maximum, par)
                    late = par if u < 3 else 0
                    plan(top + 1.75 + late, self.probs, par)
                    if u == 3 or par:
                        plan(top + 2.5 + late, self.inverse, par)
                top = at + score[1] + 1.5
                for par in range(2):
                    plan(at + score[par] + 4 if u == 3 else top + 3.5 + 1.25 * par, self.norm, par)
                for k in range(u + 1):
                    plan(at + k + 10.75, self.turn, k)
                    plan(at + k + 11.75, self.split_high, k)
                    plan(at + k + 12.5, self.split_low, k)
                    plan(at + k + 14.75, self.values, k)
                plan(at + u + 15.75, lambda: self.sum.act())
                plan(at + u + 16.25, lambda: self.sum.dve(ob_free, qk_read[2], nc_read[2]))
                if u == 0:
                    plan(at + 18, split_out, self.h // 4, self.h % 4, 0)
                    plan(at + 24, split_out, self.h // 4, self.h % 4, 1)
                if u == 0 and self.h < 6:
                    plan(at + (3 if self.h else 8), fox_load_qk, self.h + 2)
                    plan(at + 4.5, fox_load_c, self.h + 2)

        OAH, OBH = (at(n, OH + 16 * K * i, [P, 4, D], F32R) for i, n in enumerate(("OAH", "OBH")))
        def zeros(slots, *marks):
            for k in slots:
                w = TF[k].shape[1] - P
                pool.wait(*marks)
                pool.do(lambda e, v=TF[k][:, w:w + P]: e.memset(v, 0.0), signal=False)

        OBL = at("OBL", OX, [P, 4, D], F32R)
        OAL = [at("OAL0", OX + 24 * K, [P, 2, D], F32R), at("OAL1", OX + 40 * K, [P, 2, D], F32R)]
        low = {1: [OBL[:, j, :] for j in range(4)], 0: [OAL[j // 2][:, j % 2, :] for j in range(4)]}
        ot_ready, vb_read = {}, {}

        def split_out(br, j, half):
            d = slice(512 * half, 512 * half + 512)
            src = OB[:, j, d] if br else OA[j // 2][:, j % 2, d]
            hi, lo = (OBH if br else OAH)[:, j, d], low[br][j][:, d]
            summed_up = (dve.sem, dve.count)
            a = act.do(lambda e: e.activation(hi, src, ACT.Copy), summed_up, vb_read[4 + j if br else j])
            q = dve if br and j == 3 else pool
            ot_ready[br, j, half] = q.do(lambda e: e.tensor_tensor(lo, src, hi.bitcast(F32), ALU.subtract), a)

        for h in range(8):
            for u, past in ((3, 0), (2, 4), (1, 7), (0, 9)):
                Forget(4 * h + 3 - u, h, u).schedule(10 * h + past + (0 if h else 0))
        events.sort(key=lambda v: v[:2])

        def load_second():
            rows_read.append((pe.sem, pe.count))
            fox_load_c(1)
            fox_load_qk(1)

        def step_first():
            steps[0] += 9 / 8
            due(steps[0])

        zeros([(5, 0), (6, 0)], window_end)
        first_head = {k: step_first for k in range(8)}
        first_head[3] = lambda: (load_second(), step_first())
        steps[0] = 0
        turn[0] = 0
        for t0 in (0, 4):
            bs = banks(4)
            ends = products([by_tokens(S_vb, t0 + n, bs[n]) for n in range(4)], range(8), "kout",
                            release=[S_vb] if t0 else (), between=first_head if t0 else None)
            for n in range(4):
                t, b = t0 + n, bs[n]
                v = bank(b).rearrange("p (h c) -> p h c", h=8)
                m = act.do(lambda e, t=t, v=v: e.activation(VB[:, :, t, 0:64], v, ACT.Copy), ends[n], window_end)
                freed[b] = vb_done[t] = dve.do(lambda e, t=t, v=v: e.tensor_tensor(
                    VB[:, :, t, 64:P], v, VB[:, :, t, 0:64].bitcast(F32), ALU.subtract), m)

        free_u = (pe.sem, pe.count)
        ob_free.append(free_u)
        zeros([(u, 0) for u in range(4)], free_u)
        zeros([(4, 0)], nc_read[2])


        def of_branch(br, slab, j, hf, b):
            d = slice(512 * hf, 512 * hf + 512)

            def operands(k):
                return slab.at(k, P * j, P * j + P), ((OBH if br else OAH)[:, k, d], low[br][k][:, d]), \
                    [split_done[slab.load_of(k)], ot_ready[br, k, hf]]
            return (bank(b), b, operands)

        due(83.5)
        steps[0] = 83.5

        def step_last():
            steps[0] += 1.25
            due(steps[0])

        turn[0] = 0
        bs_first = banks(4)
        first_ends = [products([of_branch(0, S_y[0][1], 0, hf, bs_first[hf])], range(4), "kout",
                               between={k: step_last for k in range(4)})[0] for hf in range(2)]
        due(1000)

        pe_mark = (pe.sem, pe.count)
        attn_end = [(dve.sem, dve.count), (act.sem, act.count), (pool.sem, pool.count)]

        G = [at(f"G{i}", OX + 16 * K + 4096 * i, [P, 2, 512]) for i in range(2)]
        Y = [at(f"Y{i}", OX + 48 * K + 4096 * i, [P, 2, 512]) for i in range(2)]
        g_in_ds = [dsem("g_in0"), dsem("g_in1")]
        g_read, y_read = [attn_end + [pe_mark]] * 2, [attn_end + [pe_mark]] * 2
        mix_ready = {}

        def fetch_gates(i):
            if i >= 16:
                return None
            j, hf = i // 2, i % 2
            dma(G[i % 2][:, 0, :], gates_d[j, :, 512 * hf:512 * hf + 512], g_in_ds[i % 2], gate_stored[j, hf], g_read[i % 2])
            return dma(G[i % 2][:, 1, :], gates_d[8 + j, :, 512 * hf:512 * hf + 512], g_in_ds[i % 2],
                       gate_stored[8 + j, hf], g_read[i % 2])

        g_in = {0: fetch_gates(0), 1: fetch_gates(1)}
        y_end = None
        added = {}

        def into_u(j, hf):
            y, d = Y[hf][:, 0, :], slice(512 * hf, 512 * hf + 512)
            m = act.do(lambda e: e.activation(UH[:, j, d], y, ACT.Copy), added[j, hf], pe_mark, attn_end)
            mix_ready[j, hf] = y_read[hf] = dve.do(lambda e: e.tensor_tensor(
                UL[:, j, d], y, UH[:, j, d].bitcast(F32), ALU.subtract), m, pe_mark)

        def gate_values(i):
            g = G[i % 2][:, :, :]
            g_in[i] = act.do(lambda e: e.activation(g, g, ACT.Sigmoid), g_in[i])

        for j in range(8):
            bs = banks(4) if j else bs_first
            sf, sa = S_y[j // 4]
            jj = j % 4
            gr = [(br, hf) for br in range(2) for hf in range(2)]
            ends = [None] * 4
            ends[0:2] = first_ends
            for br, slab in ((1, sf), (0, sa)) if j else ((1, sf),):
                ends[2 * br:2 * br + 2] = products([of_branch(br, slab, jj, hf, bs[2 * br + hf]) for hf in range(2)], range(4),
                                 "kout", release=[slab] if jj == 3 else ())
            for hf in range(2):
                gate_values(2 * j + hf)
            y_end = ends[1]
            for hf in range(2):
                i = 2 * j + hf
                q = i % 2
                ba, bb = bs[hf], bs[2 + hf]
                freed[ba] = m1 = dve.do(lambda e, q=q, ba=ba: e.tensor_tensor(Y[q][:, 0, :], bank(ba), G[q][:, 0, :], ALU.mult),
                                        ends[hf], g_in[i], y_read[q])
                freed[bb] = m2 = dve.do(lambda e, q=q, bb=bb: e.tensor_tensor(Y[q][:, 1, :], bank(bb), G[q][:, 1, :], ALU.mult),
                                        ends[2 + hf], g_in[i])
                g_read[q] = m2
                g_in[i + 2] = fetch_gates(i + 2)
                added[j, hf] = pool.do(lambda e, q=q: e.tensor_tensor(Y[q][:, 0, :], Y[q][:, 0, :], Y[q][:, 1, :], ALU.add),
                                       m1, m2)
                into_u(j, hf)

        h_done = {}
        for t in range(NT):
            h_done[t] = dma(H[:, t, :], x_v[:, t, :], x_ds[t], y_end)
        gb_ready = dma(GB[:, :], row("g_mlp"), g_ds, attn_end)

        def add_to_h(t, c, b, mark, *marks):
            d = slice(512 * c, 512 * c + 512)
            freed[b] = dve.do(lambda e: e.tensor_tensor(H[:, t, d], bank(b), H[:, t, d], ALU.add), mark, *marks)
            return freed[b]

        def into_h(slabs, operands_of, then):
            for c in range(2):
                for t0 in (0, 4):
                    bs = banks(4)
                    if c == 0:
                        ends = products([operands_of(slabs[c], t0 + n, bs[n]) for n in range(4)], range(8), "kout",
                                        release=[slabs[c]] if t0 else ())
                        for n in range(4):
                            h_done[t0 + n] = add_to_h(t0 + n, c, bs[n], ends[n], h_done[t0 + n])
                        continue
                    for n in range(4):
                        t = t0 + n
                        end, = products([operands_of(slabs[c], t, bs[n])], range(8), "seq",
                                        release=[slabs[c]] if t == NT - 1 else ())
                        h_done[t] = add_to_h(t, c, bs[n], end, h_done[t])
                        then(t, end)

        u_free = {}
        XS = [at(f"XS{i}", OX + 48 * K + 4096 * i, [P, D]) for i in range(2)]
        xs_read = list(y_read)
        SQ = at("SQ", OX + 12 * K, [P, D])

        def norm_step(t, gain, ready):
            if 2 <= t < 7:
                to_u(t - 2, u_free[t - 2])
            sum_squares(t, H[:, t, :], SQ[:, :] if t == 7 else None, h_done[t], y_end)
            if t:
                norm(t - 1, H[:, t - 1, :], gain, ready)

        def norm_mlp(t, end):
            u_free[t] = end
            norm_step(t, GB[:, :], gb_ready)

        into_h(S_mx, lambda s, t, b: by_tokens(s, t, b, ready=lambda k, t: mix_ready[k, t // 4]), norm_mlp)

        def fifth_and(gain, ready):
            to_u(5, u_free[5])
            norm(7, H[:, 7, :], gain, ready)

        HH, HL = (at(f"HID{n}", OX + 16 * K * i, [P, 4, D], F32R) for i, n in enumerate("HL"))
        R = [at(f"R{i}", OX + 32 * K + 2048 * i, [P, 512]) for i in range(2)]
        R2 = [at(f"RR{i}", OX + 36 * K + 2048 * i, [P, 512]) for i in range(2)]
        r_read, n_r = [y_end, y_end], [0]
        hid_ready, hid_free = {}, [[y_end, y_read]]
        PST = at("PST", OX + 40 * K, [P, NT, 256])
        p_in = dma(PST[:, :, :], p_v, dsem("p_in"), y_end)

        def squared_relu(j, hf, b, end):
            i = n_r[0] % 2
            n_r[0] += 1
            d = slice(512 * hf, 512 * hf + 512)
            freed[b] = m = dve.do(lambda e: e.tensor_scalar(R[i][:, :], bank(b), 0.0, None, ALU.max), end, r_read[i],
                                  y_end)
            a = act.do(lambda e: e.activation(HH[:, j, d], R[i][:, :], ACT.Square), m, hid_free)
            s = pool.do(lambda e: e.tensor_tensor(R2[i][:, :], R[i][:, :], R[i][:, :], ALU.mult), m, r_read[i])
            hid_ready[j, hf] = r_read[i] = dve.do(lambda e: e.tensor_tensor(
                HL[:, j, d], R2[i][:, :], HH[:, j, d].bitcast(F32), ALU.subtract), a, s, hid_free)

        last_f1 = None
        gbp_ready = None
        ff2_end = {}

        def norm_ple(t, end):
            u_free[t] = last_f1
            norm_step(t, GB[:, :], gbp_ready)

        PTH, PTL = (at(f"PLE{n}", OX + (32 + 8 * i) * K, [P, 2, D], F32R) for i, n in enumerate("HL"))
        pt_done = {}

        def ple_operand():
            parts = list(zip([(j, hf) for j in range(2) for hf in range(2)], banks(4)))
            for (j, hf), b in parts:
                pe.wait(freed[b], p_in)
                for n in range(4):
                    end = pe.do(lambda e, n=n, b=b, j=j, hf=hf: e.transpose(
                        PS[:, b, P * n:P * n + P], PST[:, 4 * hf + n, P * j:P * j + P], ident), signal=(n == 3))
            for (j, hf), b in parts:
                d = slice(512 * hf, 512 * hf + 512)
                a = act.do(lambda e, b=b, j=j, d=d: e.activation(PTH[:, j, d], bank(b), ACT.Copy), end, r_read)
                freed[b] = pt_done[j, hf] = dve.do(lambda e, b=b, j=j, d=d: e.tensor_tensor(
                    PTL[:, j, d], bank(b), PTH[:, j, d].bitcast(F32), ALU.subtract), a)

        for c in range(8):
            s1, s2a, s2b = S_ff[c]
            if c == 0:
                first_half_first(s1, {1: lambda: fifth_and(GB[:, :], gb_ready), 3: lambda: to_u(6, u_free[6]),
                                      6: lambda: to_u(7, u_free[7])}, squared_relu)
            else:
                for j0 in (0, 2):
                    bs = banks(4)
                    gr = [(j, hf) for j in (j0, j0 + 1) for hf in range(2)]
                    ends = products([by_columns(s1, j, hf, bs[n]) for n, (j, hf) in enumerate(gr)], range(8), "kout",
                                    release=[s1] if j0 else ())
                    last_f1 = ends[-1]
                    for n, (j, hf) in enumerate(gr):
                        squared_relu(j, hf, bs[n], ends[n])
            if c == 0:
                gbp_ready = dma(GB[:, :], row("g_ple"), g_ds, xs_m[7])
            for cc, s2 in ((0, s2a), (1, s2b)):
                for t0 in (0, 4):
                    bs = banks(4)
                    op = lambda t, b: by_tokens(s2, t, b, hi=HH, lo=HL, ready=lambda k, t: hid_ready[k, t // 4])
                    rel = [s2] if t0 else ()
                    if c == 7 and cc == 1:
                        for n in range(4):
                            t = t0 + n
                            end, = products([op(t, bs[n])], range(4), "seq", release=rel if t == NT - 1 else ())
                            h_done[t] = add_to_h(t, cc, bs[n], end, h_done[t])
                            norm_ple(t, end)
                    else:
                        ends = products([op(t0 + n, bs[n]) for n in range(4)], range(4), "kout", release=rel)
                        for n in range(4):
                            h_done[t0 + n] = add_to_h(t0 + n, cc, bs[n], ends[n], h_done[t0 + n])
                    end = (pe.sem, pe.count)
                    if c == 7 and cc == 0 and t0:
                        ple_operand()
            hid_free[0] = end
        ff_end = (pe.sem, pe.count)

        SG = [at(f"SG{i}", OX + 2048 * i, [P, 512]) for i in range(4)]
        GB2 = at("GB2", OX + 8 * K, [P, D])
        gb2_ready = dma(GB2[:, :], row("norm_w_2"), dsem("gain2"), ff_end)
        sg_read, n_sg = [ff_end] * 4, [0]
        h2_ds = [dsem(f"h2_{t}") for t in range(NT)]
        h2_stored, h_read, sq_done = {}, {}, [ff_end]

        def ple(t, c, gate, gate_end, proj, proj_end):
            i = n_sg[0] % 4
            n_sg[0] += 1
            s, d = SG[i][:, :], slice(512 * c, 512 * c + 512)
            freed[gate] = m = act.do(lambda e: e.activation(s, bank(gate), ACT.Sigmoid), gate_end, sg_read[i])
            freed[proj] = m = dve.do(lambda e: e.tensor_tensor(s, s, bank(proj), ALU.mult), m, proj_end)
            q = dve if c else pool
            h_done[t] = sg_read[i] = q.do(lambda e: e.tensor_tensor(H[:, t, d], H[:, t, d], s, ALU.add), m, h_done[t])

        def sum_h(t, mark):
            sum_squares(t, H[:, t, :], SQ[:, :], mark, sq_done[0])
            sq_done[0] = summed[t][1]

        def final_first(t):
            m = scaled(t, H[:, t, :], H[:, t, :], GB[:, :], gbf_ready)
            h2_stored[t] = dma(h2_d[:, t, :], H[:, t, :], h2_ds[t], m)
            sum_h(t, m)

        def final_second(t):
            norm(t, H[:, t, :], GB2[:, :], gb2_ready)
            h_read[t] = xs_m[t]

        def proj_of(c, t, b):
            return by_tokens(S_pp[c], t, b, hi=PTH, lo=PTL, ready=lambda k, t: pt_done[k, t // 4])

        for t0 in (0, 4):
            bs, bp = banks(4), banks(4)
            rel = lambda slab: [slab] if t0 else ()
            if t0:
                ends = products([by_tokens(S_pg[0], t0 + n, bs[n]) for n in range(4)], range(8), "kout", release=[S_pg[0]])
            else:
                ends, held[:] = [], bs
                for n in range(4):
                    ends += products([by_tokens(S_pg[0], n, bs[n])], range(8), "seq")
                    if n == 0:
                        fifth_and(GB[:, :], gbp_ready)
                        gbf_ready = dma(GB[:, :], row("g_final"), g_ds, xs_m[7])
                    elif n < 3:
                        to_u(5 + n, u_free[5 + n])
                held.clear()
            pends = products([proj_of(0, t0 + n, bp[n]) for n in range(4)], range(2), "kout", release=[S_pp[0]] if t0 else ())
            for n in range(4):
                ple(t0 + n, 0, bs[n], ends[n], bp[n], pends[n])
        for t in range(NT):
            b, bp = banks(2)
            last = t == NT - 1
            end, = products([by_tokens(S_pg[1], t, b)], range(8), "seq", release=[S_pg[1]] if last else ())
            pend, = products([proj_of(1, t, bp)], range(2), "seq", release=[S_pp[1]] if last else ())
            u_free[t] = end
            ple(t, 1, b, end, bp, pend)
            if last:
                need(S_pi[0][0].idx[1])
            if t >= 3:
                to_u(t - 3, u_free[t - 3])
            sum_h(t, h_done[t])
            if t >= 1:
                final_first(t - 1)
            if t >= 2:
                final_second(t - 2)
        final_first(7)
        final_second(6)
        proj_end = (pe.sem, pe.count)
        ple_end = h_done[NT - 1]

        YH = [at(f"YH{i}", (OH, OX)[i], [P, 4, D], F32R) for i in range(2)]
        YL = [at(f"YL{i}", (OH, OX)[i] + 16 * K, [P, 4, D], F32R) for i in range(2)]
        YF = [at(f"YF{i}", (OH, OX)[i] + 16 * K, [P, 4, D]) for i in range(2)]
        PLH, PLL = (at(f"PL{n}", OX + 32 * K + 8 * K * i, [P, 2, D], F32R) for i, n in enumerate("HL"))
        W0, W1 = (at(f"WN{i}", OX + 48 * K + 4160 * i, [P, 1040]) for i in range(2))
        h_free = [h2_stored[t] for t in range(NT)]
        pl_ready, pl_free = {}, [None]
        w_free = [None]
        y_done = {}
        silu_done = {}

        class Pads:
            done = None

        def pooled(g, j, bs, ends):
            w = 2 << g
            if Pads.done is None:
                z = [dve.do(lambda e, v=v: e.memset(v[:, 0:16], 0.0), xs_read) for v in (W0, W1)]
                Pads.done = z
            u = PS[:, bs[0]:bs[0] + 2, :].rearrange("p b c -> p (b c)")
            m = act.do(lambda e: e.activation(W0[:, 16:1040], u, ACT.Copy), ends, w_free, Pads.done, xs_read)
            src, dst = W0, W1
            s = 1
            while s < w:
                q = pool if s in (2, 8) else dve
                m = q.do(lambda e, src=src, dst=dst, s=s: e.tensor_tensor(dst[:, 16:1040], src[:, 16:1040],
                                                                          src[:, 16 - s:1040 - s], ALU.add), m, Pads.done, w_free, xs_read)
                src, dst = dst, src
                s *= 2
            m1 = dve.do(lambda e: e.scalar_tensor_tensor(out=dst[:, 32:1040], in0=src[:, 32:1040], scalar=1.0 / w,
                                                         in1=u[:, 16:1024], op0=ALU.mult, op1=ALU.subtract), m)
            m2 = dve.do(lambda e: e.tensor_tensor(dst[:, 16:32], src[:, 16:32], INV[:, g, :], ALU.mult), m, sc_ready)
            m2 = dve.do(lambda e: e.tensor_tensor(dst[:, 16:32], dst[:, 16:32], u[:, 0:16], ALU.subtract), m2)
            freed[bs[0]] = freed[bs[1]] = m2
            a = act.do(lambda e: e.activation(PLH[:, j, :], dst[:, 16:1040], ACT.Copy), m1, m2, pl_free, ple_end, sg_read)
            pl_ready[j] = w_free[0] = dve.do(lambda e: e.tensor_tensor(PLL[:, j, :], dst[:, 16:1040],
                                                                       PLH[:, j, :].bitcast(F32), ALU.subtract), a, pl_free)

        def silu(g, j, hf, b, end):
            tile = 2 * g + j
            z = YF[tile // 4][:, tile % 4, 512 * hf:512 * hf + 512]
            m = act.do(lambda e: e.activation(z, bank(b), ACT.Sigmoid), end, h_free, ple_end, proj_end)
            freed[b] = silu_done[tile, hf] = dve.do(lambda e: e.scalar_tensor_tensor(
                out=z, in0=bank(b), scalar=psc[:, tile:tile + 1], in1=z, op0=ALU.mult, op1=ALU.mult), m, sc_ready)

        def mixed(g, j, hf, b, end):
            tile = 2 * g + j
            d = slice(512 * hf, 512 * hf + 512)
            q, i = tile // 4, tile % 4
            y, yh, yl = YF[q][:, i, d], YH[q][:, i, d], YL[q][:, i, d]
            freed[b] = m = dve.do(lambda e: e.scalar_tensor_tensor(out=y, in0=bank(b), scalar=pgb[:, tile:tile + 1], in1=y,
                                                                   op0=ALU.add, op1=ALU.mult), end, silu_done[tile, hf])
            a = act.do(lambda e: e.activation(yh, y, ACT.Copy), m, h_free, ple_end)
            y_done[tile, hf] = dve.do(lambda e: e.tensor_tensor(yl, y, yh.bitcast(F32), ALU.subtract), a)

        for g in range(4):
            su, sg, sw = S_pi[g]
            gr = [(j, hf) for j in range(2) for hf in range(2)]
            if g == 0:
                bu, bs = banks(4), banks(4)
                turn[0] = bs[2]
                eu, eg = {}, {}

                def fifth():
                    to_u(5, u_free[5])
                    final_second(7)
                    h_free.append(h_read[7])

                def part(slab, bank_of, marks, which, between=None, release=(), cols=(0, 512)):
                    got = products([by_columns(slab, j, hf, bank_of[2 * j + hf], cols=cols) for j, hf in which], range(8), "kout",
                                   release=release, between=between)
                    marks.update(zip(which, got))

                held[:] = bu
                part(su, bu, eu, [(0, 0), (1, 0)], {5: fifth})
                held[:] = bu + bs[:1]
                part(sg, bs, eg, [(0, 0)], {0: lambda: to_u(6, u_free[6]), 3: lambda: to_u(7, u_free[7])})
                part(su, bu, eu, [(0, 1), (1, 1)], cols=(0, 256))
                part(su, bu, eu, [(0, 1), (1, 1)], release=[su], cols=(256, 512))
                part(sg, bs, eg, [(1, 0), (0, 1), (1, 1)], release=[sg])
                held.clear()
                turn[0] = bu[0]
                for j in range(2):
                    pooled(g, j, bu[2 * j:2 * j + 2], [eu[j, 0], eu[j, 1]])
                ends = [eg[x] for x in gr]
            else:
                bu = banks(4)
                ends = products([by_columns(su, j, hf, bu[2 * j + hf]) for j, hf in gr], range(8), "kout", release=[su])
                for j in range(2):
                    pooled(g, j, bu[2 * j:2 * j + 2], ends[2 * j:2 * j + 2])
                bs = banks(4)
                ends = products([by_columns(sg, j, hf, bs[n]) for n, (j, hf) in enumerate(gr)], range(8), "kout", release=[sg])
            u_end = ends[-1]
            for n, (j, hf) in enumerate(gr):
                silu(g, j, hf, bs[n], ends[n])
            bs = banks(4)
            ends = products([by_columns(sw, j, hf, bs[n], PLH, PLL, lambda k, hf: pl_ready[k]) for n, (j, hf) in enumerate(gr)],
                            range(2), "kout", release=[sw])
            pl_free[0] = ends[-1]
            for n, (j, hf) in enumerate(gr):
                mixed(g, j, hf, bs[n], ends[n])

        H2 = at("H2", OU, [P, NT, D])
        RES = [at(f"RES{i}", OU + 32 * K + 4096 * i, [P, D]) for i in range(4)]
        gbo_ready = dma(GB[:, :], row("final_norm_w_2"), g_ds, h_read[7])
        for t in range(NT):
            h_done[t] = dma(H2[:, t, :], h2_d[:, t, :], h2_ds[t], u_end)
        out_ds = [dsem(f"out{i}") for i in range(4)]
        out_done = [u_end] * 4

        def last_sum(t):
            sum_squares(t, H2[:, t, :], RES[t % 4][:, :], h_done[t], out_done[t % 4])

        def last_norm(t):
            i = t % 4
            m = scaled(t, RES[i][:, :], H2[:, t, :], GB[:, :], gbo_ready)
            out_done[i] = dma(out_v[:, t, :], RES[i][:, :], out_ds[i], m)

        for c in range(2):
            for t0 in (0, 4):
                bs = banks(4)
                d = slice(512 * c, 512 * c + 512)

                class Both:
                    def __init__(self, slab, t, b):
                        self.slab, self.t, self.b = slab, t, b

                    def __call__(self, k):
                        s = slice(P * self.t, P * self.t + P)
                        return (YH[k // 4][:, k % 4, s], YL[k // 4][:, k % 4, s]), self.slab.at(k, 0, 512), \
                            [split_done[self.slab.load_of(k)], y_done[k, self.t // 4]]

                order = "seq" if c else "kout"
                gs = [(bank(bs[n]), bs[n], Both(S_po[c], t0 + n, bs[n])) for n in range(4)]
                if order == "kout":
                    ends = products(gs, range(8), "kout", release=[S_po[c]] if t0 else ())
                for n in range(4):
                    t = t0 + n
                    if order == "seq":
                        end, = products([gs[n]], range(8), "seq", release=[S_po[c]] if t == NT - 1 else ())
                    else:
                        end = ends[n]
                    freed[bs[n]] = h_done[t] = dve.do(lambda e, t=t, b=bs[n], d=d: e.tensor_tensor(
                        H2[:, t, d], bank(b), H2[:, t, d], ALU.add), end, h_done[t])
                    if c:
                        last_sum(t)
                        if t:
                            last_norm(t - 1)
        last_norm(NT - 1)
        sp.wait(*out_done)

        block = ctx.enter_context(nc.Block())

        @block.sync
        def _(eng):
            sp.run(eng)

        @block.tensor
        def _(eng):
            pe.run(eng)

        @block.scalar
        def _(eng):
            act.run(eng)

        @block.vector
        def _(eng):
            dve.run(eng)

        @block.gpsimd
        def _(eng):
            pool.run(eng)


_INS = ["x", "p", "g_mix", "w_in", "b_forget", "swa_sinks", "w_br_swa", "w_br_fox", "w_mix_out", "g_mlp", "w_ff1",
        "w_ff2", "g_ple", "w_ple_gate", "w_ple_proj", "g_final", "norm_w_2", "pool_in_w_2", "pool_group_w_2",
        "pool_group_b_2", "pool_scale_2", "pool_out_w_2", "final_norm_w_2"]


def constants():
    i = np.arange(P)
    mats = np.zeros((4, P, P), np.float32)
    mats[0] = np.eye(P)
    mats[1] = np.where(i[None, :] <= i[:, None], 0.0, -FAR)
    mats[2] = i[:, None] <= i[None, :]
    mats[3] = 1.0
    q, s = i[:, None] + P, np.arange(2 * P)[None, :]
    ahead = q // 64 - s // 64
    seen = (ahead >= 0) & (ahead <= 2)
    slopes = 2.0 ** -(np.arange(8) + 1.0)
    bias = np.where(seen[:, None, :], -slopes[None, :, None] * np.abs(q - s)[:, None, :], -FAR)
    inv = np.zeros((P, 4, 16), np.float32)
    for g in range(4):
        inv[:, g, :] = 1.0 / np.minimum(np.arange(16) + 1, 2 << g)
    return {"c_mats": mats, "c_bias": bias.astype(np.float32), "c_inv": inv}


def kernel(**inputs):
    import concourse.bacc as _bacc
    from concourse.bass_utils import run_bass_kernel_spmd as _run

    nc = _bacc.Bacc("TRN2", target_bir_lowering=False, num_devices=1)
    arrays, args = {}, {}
    for name in _INS:
        a = np.asarray(inputs[name])
        if name in ("pool_group_b_2", "pool_scale_2"):
            a = a.reshape(NT, P).T
        arrays[f"in_{name}"] = np.ascontiguousarray(a)
    for name, a in constants().items():
        arrays[f"in_{name}"] = a
    for key, a in arrays.items():
        args[key[3:]] = nc.dram_tensor(key, a.shape, mybir.dt.from_np(a.dtype), kind="ExternalInput").ap()
    out = nc.dram_tensor("out_0", (1, 1024, D), F32, kind="ExternalOutput").ap()
    build(nc, args, out)
    r = _run(nc, [arrays], core_ids=[0])
    return r.results[0]["out_0"]
```
